# Optimizing a Trainium2 kernel written in Bass

```python
import math
import jax
import jax.numpy as jnp
from jax import lax
import numpy as np

D_MODEL = 1024
BATCH = 1
SEQ = 256
DEPTH = 2
DEC_BATCH = 8
DEC_SEQ = 1
PAST_LEN = 1024
PAGE_SIZE = 128

N_MIXERS = 2
N_SSM_LAYERS = (DEPTH + 1) // 2
N_ATTN_LAYERS = DEPTH // 2
EPS = 1e-6

SSM_EXPAND = 2
SSM_D_INNER = SSM_EXPAND * D_MODEL
SSM_HEAD_DIM = 64
SSM_HEADS = SSM_D_INNER // SSM_HEAD_DIM
SSM_GROUPS = 4
SSM_HEADS_PER_GROUP = SSM_HEADS // SSM_GROUPS
SSM_D_STATE = 128
CONV_WIDTH = 4
SSD_CHUNK = 128
SSM_CONV_DIM = SSM_D_INNER + 2 * SSM_GROUPS * SSM_D_STATE
SSM_IN_DIM = SSM_D_INNER + SSM_CONV_DIM + SSM_HEADS
DT_MIN = 0.001
DT_MAX = 0.1

ATTN_PATTERNS = ((128, 1), (512, 4), (2048, 16))
N_ATTN_GROUPS = len(ATTN_PATTERNS)
ATTN_HEAD_DIM = 64
ATTN_HEADS = D_MODEL // ATTN_HEAD_DIM
ATTN_WIDTH = ATTN_HEADS * ATTN_HEAD_DIM
ATTN_BLOCK = 128
ATTN_SCALE = ATTN_HEAD_DIM ** -0.5

N_EXPERT_GROUPS = 4
EXPERTS_PER_GROUP = 8
TOP_K_INNER = 2
D_EXPERT = 512

kernel_name = 'hybrid_ssd_dilated_swa_hmoe_step'

def rmsnorm(x, g):
    xf = x.astype(jnp.float32)
    y = xf * lax.rsqrt(jnp.mean(xf * xf, axis=-1, keepdims=True) + EPS)
    return (y * g.astype(jnp.float32)).astype(x.dtype)

def _pad_axis(a, axis, front, back):
    cfg = [(0, 0)] * a.ndim
    cfg[axis] = (front, back)
    return jnp.pad(a, cfg)

def ssd_scan(x, dt, a, b_in, c_in, h0):
    f32 = jnp.float32
    nb, L = x.shape[:2]
    q = min(SSD_CHUNK, L)
    nc = -(-L // q)
    pad = nc * q - L
    G, E, P, N = SSM_GROUPS, SSM_HEADS_PER_GROUP, SSM_HEAD_DIM, SSM_D_STATE
    x = _pad_axis(x.astype(f32), 1, 0, pad).reshape(nb, nc, q, G, E, P)
    dt = _pad_axis(dt, 1, 0, pad).reshape(nb, nc, q, G, E)
    bm = _pad_axis(b_in.astype(f32), 1, 0, pad).reshape(nb, nc, q, G, N)
    cm = _pad_axis(c_in.astype(f32), 1, 0, pad).reshape(nb, nc, q, G, N)
    cs = jnp.cumsum(dt * a.reshape(G, E), axis=2)
    xdt = x * dt[..., None]
    causal = jnp.tril(jnp.ones((q, q), dtype=bool))[None, None, :, :, None, None]
    seg = cs[:, :, :, None] - cs[:, :, None, :]
    decay = jnp.exp(jnp.where(causal, seg, -jnp.inf))
    cb = jnp.einsum('bcign,bcjgn->bcijg', cm, bm)
    y_diag = jnp.einsum('bcijg,bcijge,bcjgep->bcigep', cb, decay, xdt)
    to_end = jnp.exp(cs[:, :, -1:] - cs)
    states = jnp.einsum('bcjgn,bcjge,bcjgep->bcgepn', bm, to_end, xdt)
    chunk_decay = jnp.exp(cs[:, :, -1])

    def step(h, inp):
        s, dcy = inp
        return h * dcy[..., None, None] + s, h

    h_last, h_in = lax.scan(step, h0.astype(f32).reshape(nb, G, E, P, N),
                            (jnp.moveaxis(states, 1, 0), jnp.moveaxis(chunk_decay, 1, 0)))
    h_in = jnp.moveaxis(h_in, 0, 1)
    y_off = jnp.einsum('bcign,bcige,bcgepn->bcigep', cm, jnp.exp(cs), h_in)
    y = (y_diag + y_off).reshape(nb, nc * q, SSM_HEADS, P)[:, :L]
    return y, h_last.reshape(nb, SSM_HEADS, P, N)

def mamba2_mixer(h, conv_state, ssm_state, w_in, conv_w, conv_b, dt_bias, a_log, d_skip, norm_g, w_out):
    f32 = jnp.float32
    nb, L, _ = h.shape
    proj = h @ w_in
    z = proj[..., :SSM_D_INNER]
    xbc = proj[..., SSM_D_INNER:SSM_D_INNER + SSM_CONV_DIM]
    dt_raw = proj[..., SSM_D_INNER + SSM_CONV_DIM:]
    xpad = jnp.concatenate([conv_state.astype(xbc.dtype), xbc], axis=1)
    conv = lax.conv_general_dilated(xpad, conv_w[:, None, :].astype(xbc.dtype), window_strides=(1,),
                                    padding='VALID', dimension_numbers=('NWC', 'WIO', 'NWC'),
                                    feature_group_count=SSM_CONV_DIM)
    new_conv_state = xpad[:, xpad.shape[1] - (CONV_WIDTH - 1):]
    xbc = jax.nn.silu((conv + conv_b).astype(f32))
    nbc = SSM_GROUPS * SSM_D_STATE
    xs = xbc[..., :SSM_D_INNER].reshape(nb, L, SSM_HEADS, SSM_HEAD_DIM)
    bm = xbc[..., SSM_D_INNER:SSM_D_INNER + nbc].reshape(nb, L, SSM_GROUPS, SSM_D_STATE)
    cm = xbc[..., SSM_D_INNER + nbc:].reshape(nb, L, SSM_GROUPS, SSM_D_STATE)
    dt = jax.nn.softplus(dt_raw.astype(f32) + dt_bias.astype(f32))
    a = -jnp.exp(a_log.astype(f32))
    y, h_last = ssd_scan(xs, dt, a, bm, cm, ssm_state)
    y = y + xs * d_skip.astype(f32)[:, None]
    y = y.reshape(nb, L, SSM_D_INNER) * jax.nn.silu(z.astype(f32))
    y = y * lax.rsqrt(jnp.mean(y * y, axis=-1, keepdims=True) + EPS) * norm_g.astype(f32)
    return y.astype(h.dtype) @ w_out, new_conv_state, h_last.astype(ssm_state.dtype)

def to_strided(a, dil):
    b, L = a.shape[:2]
    return jnp.swapaxes(a.reshape((b, L // dil, dil) + a.shape[2:]), 1, 2)

def from_strided(a, dil):
    b, _, lq = a.shape[:3]
    return jnp.swapaxes(a, 1, 2).reshape((b, lq * dil) + a.shape[3:])

def band_attention(q, k, v, n_back):
    nb, r, L = q.shape[:3]
    qb_len = min(ATTN_BLOCK, L)
    n_blk = -(-L // qb_len)
    lp = n_blk * qb_len
    qp = _pad_axis(q, 2, 0, lp - L).reshape(nb, r, n_blk, qb_len, ATTN_HEADS, ATTN_HEAD_DIM)
    kp = _pad_axis(k, 2, n_back, lp - L)
    vp = _pad_axis(v, 2, n_back, lp - L)
    kidx = (jnp.arange(n_blk) * qb_len)[:, None] + jnp.arange(qb_len + n_back)[None, :]
    kb = kp[:, :, kidx]
    vb = vp[:, :, kidx]
    s = jnp.einsum('brnqhd,brnkhd->brnhqk', qp, kb, preferred_element_type=jnp.float32) * ATTN_SCALE
    dist = jnp.arange(qb_len)[:, None] + n_back - jnp.arange(qb_len + n_back)[None, :]
    key_pos = kidx - n_back
    mask = (dist >= 0)[None] & (dist <= n_back)[None] & (key_pos >= 0)[:, None, :]
    s = jnp.where(mask[None, None, :, None], s, -jnp.inf)
    m = jnp.max(s, axis=-1)
    p = jnp.exp(s - m[..., None])
    l = jnp.sum(p, axis=-1)
    o = jnp.einsum('brnhqk,brnkhd->brnqhd', p, vb.astype(jnp.float32))
    m = jnp.swapaxes(m, 3, 4)
    l = jnp.swapaxes(l, 3, 4)
    o = (o / l[..., None]).reshape(nb, r, lp, ATTN_HEADS, ATTN_HEAD_DIM)[:, :, :L]
    lam = (m + jnp.log(l)).reshape(nb, r, lp, ATTN_HEADS)[:, :, :L]
    return o, lam

def combine_groups(outs, lams):
    alpha = jax.nn.softmax(jnp.stack(lams), axis=0)
    return jnp.sum(alpha[..., None] * jnp.stack(outs), axis=0)

def dilated_attention_prompt(h, w_qkv, w_out):
    nb, L, _ = h.shape
    qkv = (h @ w_qkv).reshape(nb, L, N_ATTN_GROUPS, 3, ATTN_HEADS, ATTN_HEAD_DIM)
    outs, lams, rows = [], [], []
    for g, (window, dil) in enumerate(ATTN_PATTERNS):
        q, k, v = qkv[:, :, g, 0], qkv[:, :, g, 1], qkv[:, :, g, 2]
        o, lam = band_attention(to_strided(q, dil), to_strided(k, dil), to_strided(v, dil), window // dil)
        outs.append(from_strided(o, dil))
        lams.append(from_strided(lam, dil))
        keep = min(window, L)
        rows.append(jnp.stack([k, v], axis=2)[:, L - keep:])
    y = combine_groups(outs, lams).reshape(nb, L, ATTN_WIDTH)
    return y.astype(h.dtype) @ w_out, rows

def dilated_attention_sample(h, kv_bufs, w_qkv, w_out):
    nb, S, _ = h.shape
    qkv = (h @ w_qkv).reshape(nb, S, N_ATTN_GROUPS, 3, ATTN_HEADS, ATTN_HEAD_DIM)
    outs, lams, rows = [], [], []
    for g, (window, dil) in enumerate(ATTN_PATTERNS):
        q, k, v = qkv[:, :, g, 0], qkv[:, :, g, 1], qkv[:, :, g, 2]
        buf = kv_bufs[g]
        wl = buf.shape[1]
        k_all = jnp.concatenate([buf[:, :, 0].astype(k.dtype), k], axis=1)
        v_all = jnp.concatenate([buf[:, :, 1].astype(v.dtype), v], axis=1)
        n_back = window // dil
        idx = wl + jnp.arange(S)[:, None] - dil * jnp.arange(n_back + 1)[None, :]
        valid = idx >= 0
        idx = jnp.maximum(idx, 0)
        kg = k_all[:, idx]
        vg = v_all[:, idx]
        s = jnp.einsum('bshd,bskhd->bshk', q, kg, preferred_element_type=jnp.float32) * ATTN_SCALE
        s = jnp.where(valid[None, :, None, :], s, -jnp.inf)
        m = jnp.max(s, axis=-1)
        p = jnp.exp(s - m[..., None])
        l = jnp.sum(p, axis=-1)
        o = jnp.einsum('bshk,bskhd->bshd', p, vg.astype(jnp.float32)) / l[..., None]
        outs.append(o)
        lams.append(m + jnp.log(l))
        rows.append(jnp.stack([k, v], axis=2))
    y = combine_groups(outs, lams).reshape(nb, S, ATTN_WIDTH)
    return y.astype(h.dtype) @ w_out, rows

def hier_moe(t, w_route_group, w_route_expert, w_gate_up, w_down):
    f32 = jnp.float32
    g_logits = jnp.einsum('td,dg->tg', t, w_route_group, preferred_element_type=f32)
    g_prob = jax.nn.softmax(g_logits, axis=-1)
    grp = jnp.argmax(g_logits, axis=-1)
    g_gate = jnp.take_along_axis(g_prob, grp[:, None], axis=-1)
    e_logits_all = jnp.einsum('td,gde->tge', t, w_route_expert, preferred_element_type=f32)
    e_logits = jnp.take_along_axis(e_logits_all, grp[:, None, None], axis=1)[:, 0]
    e_prob = jax.nn.softmax(e_logits, axis=-1)
    top_v, top_i = lax.top_k(e_prob, TOP_K_INNER)
    top_v = top_v / jnp.sum(top_v, axis=-1, keepdims=True)
    inner = jnp.sum(jax.nn.one_hot(top_i, EXPERTS_PER_GROUP, dtype=f32) * top_v[..., None], axis=1)
    combine = jax.nn.one_hot(grp, N_EXPERT_GROUPS, dtype=f32)[:, :, None] * (g_gate * inner)[:, None, :]
    out = jnp.zeros(t.shape, f32)
    for g in range(N_EXPERT_GROUPS):
        gu = jnp.einsum('td,edf->tef', t, w_gate_up[g])
        act = jax.nn.silu(gu[..., :D_EXPERT].astype(f32)) * gu[..., D_EXPERT:].astype(f32) * combine[:, g, :, None]
        out = out + jnp.einsum('tef,efd->td', act.astype(t.dtype), w_down[g], preferred_element_type=f32)
    return out.astype(t.dtype)

def setup_inputs(seed: int = 0) -> dict:
    key = jax.random.key(seed)
    ks = jax.random.split(key, 24)
    f32 = jnp.float32

    def nrm(i, shape, scale):
        return scale * jax.random.normal(ks[i], shape, f32)

    kv_shape = lambda n_rows: (N_ATTN_LAYERS, DEC_BATCH, n_rows, 2, ATTN_HEADS, ATTN_HEAD_DIM)
    wl = [min(w, PAST_LEN) for w, _ in ATTN_PATTERNS]
    u = jax.random.uniform(ks[13], (N_SSM_LAYERS, SSM_HEADS), f32)
    dt0 = jnp.exp(u * (math.log(DT_MAX) - math.log(DT_MIN)) + math.log(DT_MIN))
    dt_bias = dt0 + jnp.log(-jnp.expm1(-dt0))
    a_log = jnp.log(jax.random.uniform(ks[14], (N_SSM_LAYERS, SSM_HEADS), f32, minval=1.0, maxval=16.0))
    return {
        'x_prompt': nrm(0, (BATCH, SEQ, D_MODEL), 1.0),
        'x_sample': nrm(1, (DEC_BATCH, DEC_SEQ, D_MODEL), 1.0),
        'state_conv': nrm(2, (N_SSM_LAYERS, DEC_BATCH, CONV_WIDTH - 1, SSM_CONV_DIM), 1.0),
        'state_ssm': nrm(3, (N_SSM_LAYERS, DEC_BATCH, SSM_HEADS, SSM_HEAD_DIM, SSM_D_STATE), 0.1),
        'cache_kv_w128': nrm(4, kv_shape(wl[0]), 1.0),
        'cache_kv_w512': nrm(5, kv_shape(wl[1]), 1.0),
        'cache_kv_w2048': nrm(6, kv_shape(wl[2]), 1.0),
        'norm_mix': 1.0 + nrm(7, (DEPTH, D_MODEL), 0.1),
        'norm_ffn': 1.0 + nrm(8, (DEPTH, D_MODEL), 0.1),
        'norm_final': 1.0 + nrm(9, (D_MODEL,), 0.1),
        'ssm_in_proj': nrm(10, (N_SSM_LAYERS, D_MODEL, SSM_IN_DIM), D_MODEL ** -0.5),
        'ssm_conv_w': nrm(11, (N_SSM_LAYERS, CONV_WIDTH, SSM_CONV_DIM), CONV_WIDTH ** -0.5),
        'ssm_conv_b': nrm(12, (N_SSM_LAYERS, SSM_CONV_DIM), 0.1),
        'ssm_dt_bias': dt_bias,
        'ssm_a_log': a_log,
        'ssm_d': 1.0 + nrm(15, (N_SSM_LAYERS, SSM_HEADS), 0.1),
        'ssm_norm': 1.0 + nrm(16, (N_SSM_LAYERS, SSM_D_INNER), 0.1),
        'ssm_out_proj': nrm(17, (N_SSM_LAYERS, SSM_D_INNER, D_MODEL), SSM_D_INNER ** -0.5),
        'attn_qkv': nrm(18, (N_ATTN_LAYERS, D_MODEL, N_ATTN_GROUPS * 3 * ATTN_WIDTH), D_MODEL ** -0.5),
        'attn_out': nrm(19, (N_ATTN_LAYERS, ATTN_WIDTH, D_MODEL), ATTN_WIDTH ** -0.5),
        'moe_route_group': nrm(20, (DEPTH, D_MODEL, N_EXPERT_GROUPS), D_MODEL ** -0.5),
        'moe_route_expert': nrm(21, (DEPTH, N_EXPERT_GROUPS, D_MODEL, EXPERTS_PER_GROUP), D_MODEL ** -0.5),
        'moe_w_gate_up': nrm(22, (DEPTH, N_EXPERT_GROUPS, EXPERTS_PER_GROUP, D_MODEL, 2 * D_EXPERT), D_MODEL ** -0.5),
        'moe_w_down': nrm(23, (DEPTH, N_EXPERT_GROUPS, EXPERTS_PER_GROUP, D_EXPERT, D_MODEL), D_EXPERT ** -0.5),
    }

def reference(x_prompt, x_sample, state_conv, state_ssm, cache_kv_w128, cache_kv_w512, cache_kv_w2048,
              norm_mix, norm_ffn, norm_final, ssm_in_proj, ssm_conv_w, ssm_conv_b, ssm_dt_bias, ssm_a_log,
              ssm_d, ssm_norm, ssm_out_proj, attn_qkv, attn_out, moe_route_group, moe_route_expert,
              moe_w_gate_up, moe_w_down):
    kv_caches = (cache_kv_w128, cache_kv_w512, cache_kv_w2048)
    xp, xs = x_prompt, x_sample
    conv_p, conv_s, ssm_p, ssm_s = [], [], [], []
    kv_p = [[] for _ in ATTN_PATTERNS]
    kv_s = [[] for _ in ATTN_PATTERNS]
    for i in range(DEPTH):
        j = i // N_MIXERS
        hp = rmsnorm(xp, norm_mix[i])
        hs = rmsnorm(xs, norm_mix[i])
        if i % N_MIXERS == 0:
            params = (ssm_in_proj[j], ssm_conv_w[j], ssm_conv_b[j], ssm_dt_bias[j], ssm_a_log[j],
                      ssm_d[j], ssm_norm[j], ssm_out_proj[j])
            zero_conv = jnp.zeros((xp.shape[0], CONV_WIDTH - 1, SSM_CONV_DIM), xp.dtype)
            zero_ssm = jnp.zeros((xp.shape[0], SSM_HEADS, SSM_HEAD_DIM, SSM_D_STATE), xp.dtype)
            yp, c_new, s_new = mamba2_mixer(hp, zero_conv, zero_ssm, *params)
            conv_p.append(c_new)
            ssm_p.append(s_new)
            ys, c_new, s_new = mamba2_mixer(hs, state_conv[j], state_ssm[j], *params)
            conv_s.append(c_new)
            ssm_s.append(s_new)
        else:
            yp, rows_p = dilated_attention_prompt(hp, attn_qkv[j], attn_out[j])
            ys, rows_s = dilated_attention_sample(hs, [c[j] for c in kv_caches], attn_qkv[j], attn_out[j])
            for g in range(N_ATTN_GROUPS):
                kv_p[g].append(rows_p[g])
                kv_s[g].append(rows_s[g])
        xp = xp + yp
        xs = xs + ys
        moe_params = (moe_route_group[i], moe_route_expert[i], moe_w_gate_up[i], moe_w_down[i])
        xp = xp + hier_moe(rmsnorm(xp, norm_ffn[i]).reshape(-1, D_MODEL), *moe_params).reshape(xp.shape)
        xs = xs + hier_moe(rmsnorm(xs, norm_ffn[i]).reshape(-1, D_MODEL), *moe_params).reshape(xs.shape)
    y_prompt = rmsnorm(xp, norm_final)
    y_sample = rmsnorm(xs, norm_final)
    return (y_prompt, y_sample, jnp.stack(conv_p), jnp.stack(conv_s), jnp.stack(ssm_p), jnp.stack(ssm_s),
            jnp.stack(kv_p[0]), jnp.stack(kv_s[0]), jnp.stack(kv_p[1]), jnp.stack(kv_s[1]),
            jnp.stack(kv_p[2]), jnp.stack(kv_s[2]))


_drawn_inputs = setup_inputs


def setup_inputs(seed=0):
    import zlib

    import numpy as np

    out = dict(_drawn_inputs(seed))
    spreads = {}
    factors = {}
    for name, (base, spread) in spreads.items():
        noise = np.random.default_rng([zlib.crc32(name.encode()), seed]).standard_normal(out[name].shape)
        drawn = base * np.exp(spread * noise) if base else spread * noise
        out[name] = jnp.asarray(drawn.astype(out[name].dtype))
    for name, factor in factors.items():
        out[name] = (out[name] * factor).astype(out[name].dtype)
    return out
```

```python
from contextlib import ExitStack

import concourse.bass as bass
from concourse import mybir

ALU = mybir.AluOpType
ACT = mybir.ActivationFunctionType
F32 = mybir.dt.float32
I32 = mybir.dt.int32
AX = mybir.AxisListType.X

P = 128
D = 1024
DT = D // P
TP = 256
NS = 8
T = TP + NS
ROWS = (P, P, NS)
EPS = 1e-6

DI = 2 * D
HD = 64
SH = DI // HD
SG = 4
N = 128
CD = DI + 2 * SG * N
CW = 4
CT = CD // P
XT_TILES = DI // P
TPG = XT_TILES // SG
IN_DIM = DI + CD + SH
PADW = CW - 1
SAMP0 = PADW + TP
RAW = SAMP0 + CW * NS
CONV = RAW - PADW
RAWS = 8

AH = 16
PATTERNS = ((128, 1), (512, 4), (2048, 16))
PAST = 1024
NGRP = len(PATTERNS)
KEYS = [min(w, PAST) // dil for w, dil in PATTERNS]
SCALE = HD ** -0.5
NEG = -1.0e30

EG = 4
EPG = 8
NE = EG * EPG
DE = 512
SLOTS = 64
ROUNDS = -(-T // SLOTS)
BIG = 1.0e30
RC = ROUNDS * NE + 2
PAIRS = NE // 2

CH = 4096
RING = 6
SSM_CHUNKS = (IN_DIM - SH) // 512 + DI * D // (P * CH)
ATT_CHUNKS = NGRP * 3 * D // 512 + D * D // (P * CH)
STREAM_SLOT = (0, (SSM_CHUNKS + 3 * NE) % RING)
MOE_SLOT = (SSM_CHUNKS % RING, (STREAM_SLOT[1] + ATT_CHUNKS) % RING)


def bass_hybrid_step(nc, a, outs):
    (y_p, y_s, conv_p, conv_s, ssm_p, ssm_s, kv0_p, kv0_s, kv1_p, kv1_s, kv2_p, kv2_s) = outs
    kv_p = (kv0_p, kv1_p, kv2_p)
    kv_s = (kv0_s, kv1_s, kv2_s)
    caches = (a["cache_kv_w128"], a["cache_kv_w512"], a["cache_kv_w2048"])

    with ExitStack() as ctx:
        ctx.enter_context(nc.allow_non_contiguous_dma("short per-head vectors"))

        def sb(name, shape, dt=F32):
            return ctx.enter_context(nc.sbuf_tensor(name, shape, dt))

        def sem(name):
            return ctx.enter_context(nc.semaphore(name))

        ring = sb("ring", [P, RING, CH])
        X = sb("X", [P, 3, D])
        hT = sb("hT", [P, DT, T])
        ident = sb("ident", [P, P])
        upper = sb("upper", [P, P])
        strict = sb("strict", [P, P])
        ones = sb("ones", [P, P])
        half = sb("half", [2, P])
        vcol = sb("vcol", [P, 72])
        cwcol = sb("cwcol", [P, CW * CT])
        slot_no = sb("slot_no", [P, SLOTS])
        first4 = sb("first4", [P, EG])
        first8 = sb("first8", [P, EPG])
        thresh = sb("thresh", [1, 8])
        ss = sb("ss", [P, 4])
        rstd = sb("rstd", [P, 4])
        rounds_i = sb("rounds_i", [1, 2], I32)
        ARENA = 22330
        arena = sb("arena", [P, ARENA])
        bank = [ctx.enter_context(nc.psum_tensor(f"bank{i}", [P, 512], F32)) for i in range(8)]

        class Area:

            def __init__(self, at=0):
                self.at = at

            def __call__(self, *shape):
                n = 1
                for s in shape:
                    n *= s
                v = arena[:, self.at:self.at + n]
                self.at += n
                assert self.at <= ARENA, self.at
                if len(shape) == 2:
                    return v.rearrange("p (a b) -> p a b", b=shape[1])
                if len(shape) == 3:
                    return v.rearrange("p (a b c) -> p a b c", b=shape[1], c=shape[2])
                if len(shape) == 4:
                    return v.rearrange("p (a b c d) -> p a b c d", b=shape[1], c=shape[2], d=shape[3])
                return v

        def gmix(i):
            return vcol[:, DT * i:DT * i + DT]

        def gffn(i):
            return vcol[:, 16 + DT * i:16 + DT * i + DT]

        gssm = vcol[:, 32:48]
        cbcol = vcol[:, 48:72]

        m = Area()
        conv_out = m(CT, T)
        zT = m(XT_TILES, T)
        dtT = m(T)
        dAT = m(T)
        dt_tok = m(3, SH)
        dA_tok = m(3, SH)
        cs_tok = m(2, SH)
        w_tok = m(2, SH)
        b_tok = m(2, SG * N)
        d_col = m(16)
        head_v = m(8)
        d_row = m(16)
        dAe = m(XT_TILES, NS)
        ysum = m(T)
        after_vec = m.at
        raws = m(RAWS, RAW)
        cacc = m(2, CONV)
        stT = m(CT, CW * NS - NS)
        newc = m(CT, 3 + NS)
        newr = m(2, 512)
        spt = m(6, T)
        conv_end = m.at
        m = Area(after_vec)
        xdt = m(2, TPG * P)
        xw = m(2, TPG * P)
        seg = m(2, 512)
        cbm = m(3, P)
        Et = m(2, P)
        y1 = m(2, P)
        hout = m(2, P)
        sb_rows = m(2 * SG * N)
        diagm = m(NS, N)
        Cb = m(NS, N)
        st_in = m(2, 4, N)
        st_y = m(4, N)
        dtx = m(TPG * P)
        eyes = m(NS)
        m = Area(conv_end)
        dtw = m(DT, SH)
        vrow = m(P)
        cwrow = m(P)
        m = Area(0)
        xn_m = m(3, D)
        csr = m(CD)

        m = Area()
        xn_e = m(3, D)
        accT = m(DT, T)
        Xg = m(DT, P)
        Pm = m(3, 2, SLOTS)
        Cm = m(3, 2, SLOTS)
        CmT = m(T)
        sg = m(DE)
        act_r = m(DE)
        actT = m(4, P)
        ysl = m(DT, P)
        rk = m(3, RC)
        cc = m(3, RC)
        wr = m(DT, EG + NE)
        lg = m(3, EG + NE)
        g_a, g_b, g_oh = m(3, EG), m(3, EG), m(3, EG)
        g_s = m(8, 3)
        e_w = m(3, EG, EPG)
        es, e_a, oh1, oh2, e_sel, e_in = (m(3, EPG) for _ in range(6))
        msk, cmb, rnk = m(3, NE), m(3, NE), m(3, NE)
        cnt = m(NE)
        cnt_s = m(8)
        gfin = m(D)

        m = Area()
        qT = m(DT, T)
        kT = m(DT, T)
        yT = qT
        V_in = Area(m.at)(2, NGRP, D)
        KV = m(2, 2, D)
        vT = m(4, T)
        sm = m(2, 2, 3 * P)
        pT = m(2, 2, 3, P)
        assert m.at >= 2 * DT * T + 2 * NGRP * D
        O = m(2, D)
        mask = m(NGRP, 3 * P)
        K_in = m(2, D)
        q_s = m(D)
        kv_s_rows = m(2 * D)
        S_s = m(NGRP, P)
        prod = m(NGRP, DT * NS)
        vTs = m(NGRP, DT * NS)
        O_st = m(5, 2, AH)
        M_, Mn, L_, al, rs = (O_st[:, i, :, :] for i in range(5))
        xn_a = Area(2 * DT * T)(3, D)
        fold = sb("fold", [P, DT * NS])
        s_st = sb("s_st", [P, 8])
        p_s = K_in.rearrange("p a n -> p (a n)")[:, 0:384]
        pTs = K_in.rearrange("p a n -> p (a n)")[:, 384:768].rearrange("p (g c) -> p g c", g=NGRP)
        PHp = K_in.rearrange("p a n -> p (a n)")[:, 768:1152].rearrange("p (g c) -> p g c", g=NGRP)
        y_s1 = K_in.rearrange("p a n -> p (a n)")[:, 1152:1344].rearrange("p (g c) -> p g c", g=NGRP)
        y_s2 = K_in.rearrange("p a n -> p (a n)")[:, 1344:1408]
        same = K_in.rearrange("p a n -> p (a n)")[:, 1408:1536]

        loads = [[sem(f"weights{l}_landed{i}") for i in range(RING)] for l in range(2)]
        s_ld = loads[0]
        s_xld = sem("x_landed")
        s_vld = sem("vectors_landed")
        s_csld = sem("conv_state_landed")
        s_dtld = sem("dt_weights_landed")
        s_const = sem("constants_made")
        s_chain = sem("vector_step")
        s_achain = sem("scalar_step")
        s_pchain = sem("pool_step")
        s_pvec = sem("pe_vectors")
        s_vvec = sem("vectors_ready")
        s_out = sem("outputs_stored")
        s_pout = sem("old_conv_rows_moved")
        n_ss = sem("norm_squares")
        n_var = sem("norm_var")
        n_std = sem("norm_std")
        n_xn = sem("norm_rows")
        n_tp = sem("norm_transposed")
        n_ht = sem("norm_ready")
        s_stp = sem("conv_state_transposed")
        s_stc = sem("conv_state_columns")
        s_dtp = sem("dt_projected")
        s_dtz = sem("dt_biased")
        s_dte = sem("dt_exp")
        s_dt = sem("dt_ready")
        s_prj = sem("tile_projected")
        s_raw = sem("raw_ready")
        s_rst = sem("raw_state_ready")
        s_cv = sem("convolved")
        s_cx = sem("conv_activated")
        s_nc = sem("new_conv_columns")
        s_ntp = sem("new_conv_transposed")
        s_nrw = sem("new_conv_rows")
        s_nst = [sem(f"new_conv_stored{i}") for i in range(2)]
        s_tk = sem("scan_tokens_pe")
        s_tkv = sem("scan_tokens_ready")
        s_xtp = sem("x_transposed")
        s_xdt = sem("xdt_ready")
        s_cb = sem("cb_products")
        s_cbm = sem("cb_masked")
        s_csb = sem("cs_broadcast")
        s_seg = sem("segments")
        s_dec = sem("decays")
        s_M = sem("scores_ready")
        s_yp = sem("scan_products")
        s_E = sem("offset_decay")
        s_y = sem("scan_rows")
        s_Sp = sem("state_products")
        s_S1 = sem("state_copied")
        s_So = sem("state_ready")
        s_Sst = [sem(f"state_stored{i}") for i in range(2)]
        s_dtk = sem("decode_rows_pe")
        s_dcv = sem("decode_rows_ready")
        s_cbp = sem("decode_c_pe")
        s_cbv = sem("decode_c_ready")
        s_op = sem("decode_outer")
        s_stl = [sem(f"decode_state_landed{i}") for i in range(2)]
        s_h = sem("decode_state_new")
        s_hst = [sem(f"decode_state_stored{i}") for i in range(2)]
        s_ys = sem("decode_rows_summed")
        s_zp = sem("z_projected")
        s_zc = sem("z_copied")
        s_zs = sem("z_silu")
        s_g = sem("gated")
        s_gq = sem("gated_squares")
        s_gs = sem("gated_sum_pe")
        s_gn = sem("gated_scaled")
        s_op2 = sem("out_projected")
        s_oc = sem("out_copied")
        s_ot = sem("out_transposed")
        s_xa = sem("residual_added")
        m_wr = sem("router_weights_landed")
        m_lg = sem("logits_projected")
        m_ge = sem("router_exponents")
        m_ex = sem("router_exps")
        m_mk = sem("token_masks")
        m_rk = sem("token_ranks")
        m_R = sem("rounds_known")
        m_t = sem("experts_transposed")

        class Moe:

            def __init__(self, l):
                self.peq = sem(f"slots_built{l}")
                self.cm = sem(f"shares_built{l}")
                self.ga = sem(f"tokens_gathered{l}")
                self.xg = sem(f"tokens_ready{l}")
                self.gu = sem(f"gate_or_up_done{l}")
                self.sg = sem(f"silu_done{l}")
                self.act = sem(f"act_ready{l}")
                self.tp = sem(f"act_transposed{l}")
                self.at = sem(f"act_columns_ready{l}")
                self.cp = sem(f"shares_transposed{l}")
                self.cpt = sem(f"shares_copied{l}")
                self.dh = sem(f"down_half_done{l}")
                self.dn = sem(f"down_done{l}")
                self.y = sem(f"result_rows_ready{l}")
                self.sc = sem(f"results_scattered{l}")
                self.acc = sem(f"results_added{l}")

        moes = [Moe(0), Moe(1)]

        a_mv = sem("masks_ready")
        q_p = sem("qkv_projected")
        q_e = sem("qkv_copied")
        q_vs = sem("sample_v_copied")
        kv_t = sem("kv_rows_transposed")
        kv_e = sem("kv_rows_copied")
        kvst = sem("kv_stored")
        h_s = sem("head_scores")
        h_m = sem("head_masked")
        h_x = sem("head_maxima")
        h_e = sem("head_exps")
        h_t = sem("head_transposed")
        h_c = sem("head_probs_copied")
        h_v = sem("head_values")
        h_o = sem("head_output")
        k_l = [sem(f"cache_keys_landed{i}") for i in range(2)]
        k_q = sem("cache_query_broadcast")
        k_m = sem("cache_products")
        k_r = sem("cache_scores")
        c_p = sem("sample_softmax_pe")
        c_v = sem("sample_softmax_vector")
        c_a = sem("sample_softmax_scalar")
        v_l = [sem(f"cache_values_landed{i}") for i in range(2)]
        v_p = sem("cache_values_summed")
        o_n = sem("rows_divided")
        o_t = sem("rows_transposed")
        o_c = sem("rows_copied")
        s_fin = sem("final_rows")

        block = ctx.enter_context(nc.Block())

        w_in = a["ssm_in_proj"][0].rearrange("(k p) n -> p k n", p=P)
        w_out = a["ssm_out_proj"][0].rearrange("(k p) n -> p k n", p=P)

        in_cols = [2 * DI, 2 * DI + 512] + [DI + 512 * i for i in range(4)] + [512 * i for i in range(4)]
        tile_order = [16 + i for i in range(8)] + list(range(16))

        def wait_chunk(eng, n):
            eng.wait_ge(s_ld[n % RING], 16 * (n // RING + 1))

        @block.sync
        def _(sp):
            def chunk_used(n):
                if n < 6:
                    sp.wait_ge(s_prj, 4 * (n + 1))
                else:
                    sp.wait_ge(s_zp, 4 * (n - 5))

            def moe_stream(l):
                s = moes[l]
                gu = a["moe_w_gate_up"][l].rearrange("g e (k p) n -> (g e) p k n", p=P)
                dn = a["moe_w_down"][l].rearrange("g e (k p) n -> (g e) p k n", p=P)

                def chunk(j, pair, e):
                    slot = (MOE_SLOT[l] + j) % RING
                    half = slice((j // 2) * DE, (j // 2 + 1) * DE)
                    if j < 4:
                        sp.wait_ge(s.gu, pair * 2 + (j // 2 + 1))
                        src = gu[bass.ds(e + j % 2, 1), :, :, half]
                    else:
                        sp.wait_ge(s.dn, pair * 2 + (j - 3))
                        src = dn[bass.ds(e + (j - 4), 1)]
                    dst = ring[:, slot, :].rearrange("p (k n) -> p k n", n=src.shape[3])
                    sp.dma_start(dst, src.rearrange("o p k n -> (o p) k n")).then_inc(loads[l][slot], 16)

                for j in range(6):
                    chunk(j, 0, 0)
                sp.wait_ge(m_R, l + 1)
                rounds = sp.value_load(rounds_i[0:1, 0:1], min_val=1, max_val=ROUNDS)
                with sp.Fori(0, rounds) as r:
                    with sp.Fori(1, PAIRS) as q:
                        for j in range(6):
                            chunk(j, r * PAIRS + q, q * 2)
                    with sp.If(r + 1 < rounds):
                        for j in range(6):
                            chunk(j, r * PAIRS + PAIRS, 0)
                    sp.nop()
                return rounds

            sp.dma_start(dtw[:, :, :], w_in[:, :, IN_DIM - SH:IN_DIM]).then_inc(s_dtld, 16)
            for n in range(SSM_CHUNKS):
                if n >= RING:
                    chunk_used(n - RING)
                if n < 10:
                    c = in_cols[n]
                    src = w_in[:, :, c:c + 512]
                    dst = ring[:, n % RING, :].rearrange("p (k n) -> p k n", k=DT)
                else:
                    c = (n - 10) * 256
                    src = w_out[:, :, c:c + 256]
                    dst = ring[:, n % RING, :].rearrange("p (k n) -> p k n", k=16)
                sp.dma_start(dst, src).then_inc(s_ld[n % RING], 16)
            rounds = moe_stream(0)
            qkv = a["attn_qkv"][0].rearrange("(k p) n -> p k n", p=P)
            wo = a["attn_out"][0].rearrange("(k p) n -> p k n", p=P)
            for n in range(ATT_CHUNKS):
                slot = (STREAM_SLOT[1] + n) % RING
                if n < RING:
                    free = moes[0].gu if n < 4 else moes[0].dn
                    sp.wait_ge(free, rounds * NE + 1 + (n // 2 if n < 4 else n - 4))
                else:
                    sp.wait_ge(q_p, 4 * (n - RING + 1))
                if n < ATT_CHUNKS - 2:
                    g, j = n // 6, n % 6
                    c = (3 * g + 2 - j // 2) * D + (j % 2) * 512
                    src = qkv[:, :, c:c + 512]
                else:
                    c = (n - ATT_CHUNKS + 2) * 512
                    src = wo[:, :, c:c + 512]
                sp.dma_start(ring[:, slot, :].rearrange("p (k n) -> p k n", k=DT), src).then_inc(loads[1][slot], 16)
            moe_stream(1)
            sp.wait_ge(s_fin, 3)
            sp.dma_start(y_p[0].rearrange("(t p) d -> p t d", p=P), X[:, 0:2, :]).then_inc(s_out, 16)
            sp.dma_start(y_s.rearrange("b s d -> (b s) d"), X[0:NS, 2, :]).then_inc(s_out, 16)
            sp.wait_ge(s_out, 32)

        @block.gpsimd
        def _(pool):
            steps = [0]

            def link(ins):
                steps[0] += 1
                ins.then_inc(s_pchain, 1)
                pool.wait_ge(s_pchain, steps[0])

            def router_weights(l):
                pool.wait_ge(s_xa, 12 * l + 6)
                pool.dma_start(wr[:, :, 0:EG],
                               a["moe_route_group"][l].rearrange("(k p) g -> p k g", p=P)).then_inc(m_wr, 16)
                for g in range(EG):
                    pool.dma_start(wr[:, :, EG + EPG * g:EG + EPG * (g + 1)],
                                   a["moe_route_expert"][l, g].rearrange("(k p) e -> p k e", p=P)).then_inc(m_wr, 16)

            pool.dma_start(X[:, 0:2, :], a["x_prompt"][0].rearrange("(t p) d -> p t d", p=P)).then_inc(s_xld, 16)
            pool.dma_start(X[0:NS, 2, :], a["x_sample"].rearrange("b s d -> (b s) d")).then_inc(s_xld, 16)
            pool.dma_start(vrow[0:16, :], a["norm_mix"].rearrange("l (t p) -> (l t) p", p=P)).then_inc(s_vld, 16)
            pool.dma_start(vrow[16:32, :], a["norm_ffn"].rearrange("l (t p) -> (l t) p", p=P)).then_inc(s_vld, 16)
            pool.dma_start(vrow[32:48, :], a["ssm_norm"].rearrange("l (t p) -> (l t) p", p=P)).then_inc(s_vld, 16)
            pool.dma_start(vrow[48:72, :], a["ssm_conv_b"].rearrange("l (t p) -> (l t) p", p=P)).then_inc(s_vld, 16)
            pool.dma_start(cwrow[0:96, :], a["ssm_conv_w"].rearrange("l w (t p) -> (l w t) p", p=P)).then_inc(s_vld, 16)
            pool.dma_start(head_v[0:SH, 0:1], a["ssm_dt_bias"].rearrange("l h -> h l")).then_inc(s_vld, 16)
            pool.dma_start(head_v[0:SH, 1:2], a["ssm_a_log"].rearrange("l h -> h l")).then_inc(s_vld, 16)
            pool.dma_start(d_row[0:2, :], a["ssm_d"].rearrange("l (t r) -> (l r) t", r=2)).then_inc(s_vld, 16)
            pool.dma_start(csr[0:CW * NS - NS, :], a["state_conv"][0].rearrange("b w c -> (b w) c")).then_inc(s_csld, 16)
            pool.dma_start(conv_s[0, :, 0:2, :].rearrange("b w c -> b (w c)"),
                           a["state_conv"][0, :, 1:3, :].rearrange("b w c -> b (w c)")).then_inc(s_pout, 16)
            link(pool.memset(ones[:, :], 1.0))
            pool.affine_select(out=ident[:, :], in_=ones[:, :], compare_op=ALU.is_equal, fill=0.0, base=0,
                               pattern=[[-1, P]], channel_multiplier=1).then_inc(s_const, 1)
            pool.affine_select(out=upper[:, :], in_=ones[:, :], compare_op=ALU.is_ge, fill=0.0, base=0,
                               pattern=[[1, P]], channel_multiplier=-1).then_inc(s_const, 1)
            pool.affine_select(out=strict[:, :], in_=ones[:, :], compare_op=ALU.is_gt, fill=0.0, base=0,
                               pattern=[[1, P]], channel_multiplier=-1).then_inc(s_const, 1)
            link(pool.affine_select(out=half[:, :], in_=ones[0:2, :], compare_op=ALU.is_ge, fill=0.0, base=0,
                                    pattern=[[1, P]], channel_multiplier=-HD))
            pool.affine_select(out=half[:, :], in_=half[:, :], compare_op=ALU.is_ge, fill=0.0, base=HD - 1,
                               pattern=[[-1, P]], channel_multiplier=HD).then_inc(s_const, 1)
            pool.iota(slot_no[:, :], [[1, SLOTS]], base=0, channel_multiplier=0,
                      allow_small_or_imprecise_dtypes=True).then_inc(s_const, 1)
            pool.iota(first4[:, :], [[-1, EG]], base=EG, channel_multiplier=0,
                      allow_small_or_imprecise_dtypes=True).then_inc(s_const, 1)
            pool.iota(first8[:, :], [[-1, EPG]], base=EPG, channel_multiplier=0,
                      allow_small_or_imprecise_dtypes=True).then_inc(s_const, 1)
            pool.iota(thresh[:, :], [[SLOTS, 8]], base=0, channel_multiplier=0,
                      allow_small_or_imprecise_dtypes=True).then_inc(s_const, 1)

            for i, ct in enumerate(tile_order):
                if i == 0:
                    pool.wait_ge(s_stc, 3)
                if i >= RAWS:
                    pool.wait_ge(s_cv, i - RAWS + 1)
                old = raws[:, i % RAWS, SAMP0:RAW].rearrange("p (b w) -> p b w", w=CW)[:, :, 0:PADW]
                pool.tensor_copy(old, stT[:, ct, :].rearrange("p (b w) -> p b w", w=PADW)).then_inc(s_rst, 1)
                pool.wait_ge(s_raw, 2 * i + 2)
                new = raws[:, i % RAWS, SAMP0:RAW].rearrange("p (b w) -> p b w", w=CW)[:, :, PADW]
                pool.tensor_copy(newc[:, ct, 0:PADW], raws[:, i % RAWS, TP:TP + PADW]).then_inc(s_nc, 1)
                pool.tensor_copy(newc[:, ct, PADW:PADW + NS], new).then_inc(s_nc, 1)
            for q in range(CT // 4):
                pool.wait_ge(s_nrw, q + 1)
                pool.dma_start(conv_p[0, 0, :, 512 * q:512 * q + 512], newr[0:3, q % 2, :]).then_inc(s_nst[q % 2], 16)
                pool.dma_start(conv_s[0, :, 2, 512 * q:512 * q + 512], newr[3:11, q % 2, :]).then_inc(s_nst[q % 2], 16)

            for t in range(XT_TILES):
                pool.wait_ge(s_So, t + 1)
                pool.dma_start(ssm_p[0, 0, 2 * t:2 * t + 2].rearrange("h p n -> (h p) n"),
                               hout[:, t % 2, :]).then_inc(s_Sst[t % 2], 16)
            for i in range(2):
                pool.wait_ge(s_Sst[i], 16 * XT_TILES // 2)

            def state(x, t, q):
                return x[0, 4 * q:4 * q + 4, 2 * t:2 * t + 2].rearrange("b h p n -> (h p) b n")

            for u in range(2 * XT_TILES + 1):
                if u < 2 * XT_TILES:
                    if u == 0:
                        pool.wait_ge(s_y, XT_TILES)
                    if u >= 2:
                        pool.wait_ge(s_hst[u % 2], 16 * (u // 2))
                        pool.wait_ge(s_ys, u - 1)
                    pool.dma_start(st_in[:, u % 2, :, :],
                                   state(a["state_ssm"], u // 2, u % 2)).then_inc(s_stl[u % 2], 16)
                if u >= 1:
                    v = u - 1
                    pool.wait_ge(s_h, v + 1)
                    pool.dma_start(state(ssm_s, v // 2, v % 2), st_in[:, v % 2, :, :]).then_inc(s_hst[v % 2], 16)
            pool.wait_ge(s_pout, 16)
            for i in range(2):
                pool.wait_ge(s_nst[i], 16 * CT // 4)
                pool.wait_ge(s_hst[i], 16 * XT_TILES)

            router_weights(0)

            pool.wait_ge(s_xa, 12)
            for g in range(NGRP):
                link(pool.memset(mask[:, g, :], 0.0))
                for c0, c1, base in ((0, P, 0), (P, 3 * P, P)):
                    v_ = mask[:, g, c0:c1]
                    link(pool.affine_select(out=v_, in_=v_, compare_op=ALU.is_ge, fill=NEG, base=base,
                                            pattern=[[-1, c1 - c0]], channel_multiplier=1))
                    if g == 0:
                        link(pool.affine_select(out=v_, in_=v_, compare_op=ALU.is_ge, fill=NEG, base=P - base,
                                                pattern=[[1, c1 - c0]], channel_multiplier=-1))
            pool.iota(pT[:, 0, 0, :, :].rearrange("p a b -> p (a b)").bitcast(I32), [[-1, 3 * P]], base=4 * P,
                      channel_multiplier=1).then_inc(s_const, 1)

            def cache_rows(g, b, kv):
                w, dil = PATTERNS[g]
                return caches[g][0, b, :, kv].rearrange("(n s) h d -> s n (h d)", s=dil)[0]

            def keys_of(g):
                for b in range(NS):
                    u = NS * g + b
                    n = KEYS[g]
                    if u >= 2:
                        pool.wait_ge(k_r, u - 1)
                    pool.dma_start(K_in[0:n, u % 2, :], cache_rows(g, b, 0)).then_inc(k_l[u % 2], 16)

            for g in range(NGRP):
                if g >= 1:
                    keys_of(g - 1)
                pool.wait_ge(kv_e, 14 * g + 12)
                lo = 1 if g == 0 else 0
                pool.dma_start(kv_p[g][0, 0].rearrange("(c p) w h d -> p c (w h d)", p=P),
                               KV[:, lo:2, :, :].rearrange("p c w d -> p c (w d)")).then_inc(kvst, 16)
                pool.dma_start(kv_s[g][0].rearrange("b s w h d -> b (s w h d)"),
                               kv_s_rows[0:NS, :]).then_inc(kvst, 16)
            keys_of(NGRP - 1)
            pool.wait_ge(h_o, DT * NGRP)
            pool.wait_ge(kvst, 32 * NGRP)
            for b in range(NS):
                if b >= 2:
                    pool.wait_ge(v_p, b - 1)
                for g in range(NGRP):
                    pool.dma_start(V_in[0:KEYS[g], b % 2, g, :], cache_rows(g, b, 1)).then_inc(v_l[b % 2], 16)
            router_weights(1)
            pool.dma_start(gfin[:, :], a["norm_final"].rearrange("(o d) -> o d", o=1).to_broadcast([P, D])
                           ).then_inc(s_vld, 16)

        @block.tensor
        def _(pe):
            def transpose(out, in_):
                return pe.transpose(out, in_, ident[0:in_.shape[0], 0:in_.shape[0]])

            def norm(k, xn):
                pe.wait_ge(n_xn, 3 * (k + 1))
                for d in range(DT):
                    if d >= 2:
                        pe.wait_ge(n_ht, DT * k + d - 1)
                    for t, r in enumerate(ROWS):
                        mm = transpose(bank[d % 2][:, t * P:t * P + r], xn[0:r, t, d * P:(d + 1) * P])
                    mm.then_inc(n_tp, 1)

            def moe(l):
                s = moes[l]
                pe.wait_ge(m_wr, 16 * (1 + EG) * (l + 1))
                pe.wait_ge(n_ht, DT * (2 * l + 2))
                for t, r in enumerate(ROWS):
                    for k in range(DT):
                        mm = pe.matmul(bank[6][0:r, t * (EG + NE):(t + 1) * (EG + NE)], hT[:, k, t * P:t * P + r],
                                       wr[:, k, :], start=(k == 0), stop=(k == DT - 1))
                mm.then_inc(m_lg, 1)
                pe.wait_ge(m_mk, 2 * (l + 1))
                for t, r in enumerate(ROWS + (P,)):
                    out = bank[7][0:r, t * NE:(t + 1) * NE]
                    for u in range(min(t + 1, 3)):
                        ru = ROWS[u]
                        how = strict if u == t else ones
                        mm = pe.matmul(out, how[0:ru, 0:r], msk[0:ru, u, :], start=(u == 0), stop=(u == min(t, 2)))
                mm.then_inc(m_rk, 1)
                pe.wait_ge(m_R, l + 1)
                rounds = pe.value_load(rounds_i[0:1, 0:1], min_val=1, max_val=ROUNDS)

                def chunk_landed(j, it):
                    slot = (MOE_SLOT[l] + j) % RING
                    before = sum((n + STREAM_SLOT[l]) % RING == slot for n in range((SSM_CHUNKS, ATT_CHUNKS)[l]))
                    pe.wait_ge(loads[l][slot], it * 16 + 16 * (before + 1))

                def weights(j, k_tiles):
                    return ring[:, (MOE_SLOT[l] + j) % RING, :].rearrange("p (k n) -> p k n", k=k_tiles)

                def gather(q):
                    for d in range(4):
                        c = (4 * q + d) * P
                        for t, r in enumerate(ROWS):
                            mm = pe.matmul(bank[4 + q][:, d * P:(d + 1) * P], xn_e[0:r, t, c:c + P],
                                           Pm[0:r, t, :, :].rearrange("p e s -> p (e s)"),
                                           start=(t == 0), stop=(t == 2))
                    mm.then_inc(s.ga, 1)

                def gate_or_up(j, it):
                    chunk_landed(2 * j, it)
                    chunk_landed(2 * j + 1, it)
                    for k in range(DT):
                        for e in range(2):
                            mm = pe.matmul(bank[j][e * SLOTS:(e + 1) * SLOTS, :], Xg[:, k, e * SLOTS:(e + 1) * SLOTS],
                                           weights(2 * j + e, DT)[:, k, :], start=(k == 0), stop=(k == DT - 1))
                    mm.then_inc(s.gu, 1)

                def scatter(d):
                    pe.matmul(bank[6 + d % 2][:, 0:T], ysl[:, d, :], CmT[:, :], start=True, stop=True).then_inc(s.sc, 1)

                def down(q):
                    for k in range(4):
                        for e in range(2):
                            mm = pe.matmul(bank[2 + q][e * SLOTS:(e + 1) * SLOTS, :],
                                           actT[:, k, e * SLOTS:(e + 1) * SLOTS],
                                           weights(4 + e, 4)[:, k, q * 512:(q + 1) * 512],
                                           start=(k == 0), stop=(k == 3))
                            if k == 3 and q == 1:
                                mm.then_inc(s.dn, 1)
                    if q == 0:
                        mm.then_inc(s.dh, 1)

                pe.wait_ge(s.peq, 1)
                gather(0)
                gather(1)
                with pe.Fori(0, rounds * PAIRS) as it:
                    pe.wait_ge(s.xg, it * 2 + 2)
                    pe.wait_ge(s.at, it + 1)
                    gate_or_up(0, it)
                    pe.wait_ge(s.cpt, it + 1)
                    gate_or_up(1, it)
                    pe.wait_ge(s.y, it * 2 + 2)
                    for d in range(DT):
                        pe.wait_ge(s.acc, it * 8 + max(1, d))
                        scatter(d)
                    pe.wait_ge(s.act, it + 2)
                    for f in range(4):
                        mm = transpose(bank[0][:, f * P:(f + 1) * P], act_r[:, f * P:(f + 1) * P])
                    mm.then_inc(s.tp, 1)
                    pe.wait_ge(s.cm, it + 1)
                    for t, r in enumerate(ROWS):
                        mm = transpose(bank[1][:, t * P:t * P + r], Cm[0:r, t, :, :].rearrange("p e s -> p (e s)"))
                    mm.then_inc(s.cp, 1)
                    pe.wait_ge(s.peq, it + 2)
                    gather(0)
                    gather(1)
                    pe.wait_ge(s.at, it + 2)
                    chunk_landed(4, it)
                    chunk_landed(5, it)
                    down(0)
                    down(1)
                pe.wait_ge(s.cpt, rounds * PAIRS + 1)
                pe.wait_ge(s.y, rounds * (2 * PAIRS) + 2)
                for d in range(DT):
                    pe.wait_ge(s.acc, rounds * (8 * PAIRS) + max(1, d))
                    scatter(d)
                pe.wait_ge(s.acc, rounds * (8 * PAIRS) + 9)
                for t, r in enumerate(ROWS):
                    for q in range(2):
                        j = 2 * t + q
                        if j >= 2:
                            pe.wait_ge(s_xa, 12 * l + 6 + j - 1)
                        for d in range(4):
                            mm = transpose(bank[j % 2][0:r, d * P:(d + 1) * P], accT[:, 4 * q + d, t * P:t * P + r])
                        mm.then_inc(m_t, 1)

            pe.wait_ge(s_const, 8)
            pe.wait_ge(s_vld, 128)
            transpose(bank[7][:, 0:72], vrow[0:72, :])
            transpose(bank[7][:, 72:168], cwrow[0:96, :])
            pe.matmul(bank[7][:, 168:184], half[:, :], d_row[0:2, :], start=True, stop=True).then_inc(s_pvec, 1)
            norm(0, xn_m)
            pe.wait_ge(s_csld, 16)
            w = (CW - 1) * NS
            for q in range(2):
                for c in range(12):
                    ct = 12 * q + c
                    mm = transpose(bank[5 + q][:, c * w:(c + 1) * w], csr[0:w, ct * P:(ct + 1) * P])
                mm.then_inc(s_stp, 1)
            pe.wait_ge(s_dtld, 16)
            pe.wait_ge(n_ht, DT)
            for k in range(DT):
                mm = pe.matmul(bank[4][0:SH, 0:T], dtw[:, k, :], hT[:, k, :], start=(k == 0), stop=(k == DT - 1))
            mm.then_inc(s_dtp, 1)
            for i in range(CT):
                if i % 4 == 0:
                    wait_chunk(pe, i // 4)
                if i >= 2:
                    pe.wait_ge(s_raw, 2 * i - 2)
                wv = ring[:, (i // 4) % RING, :].rearrange("p (k n) -> p k n", k=DT)
                for k in range(DT):
                    mm = pe.matmul(bank[i % 2][:, 0:T], wv[:, k, (i % 4) * P:(i % 4 + 1) * P], hT[:, k, :],
                                   start=(k == 0), stop=(k == DT - 1))
                mm.then_inc(s_prj, 1)
            pe.wait_ge(s_nc, 2 * CT)
            for q in range(CT // 4):
                if q >= 2:
                    pe.wait_ge(s_nrw, q - 1)
                for c in range(4):
                    mm = transpose(bank[5 + q % 2][0:11, c * P:(c + 1) * P], newc[:, 4 * q + c, :])
                mm.then_inc(s_ntp, 1)

            pe.wait_ge(s_dt, 2)
            for j, v in enumerate((dtT, dAT)):
                for t, r in enumerate(ROWS):
                    mm = transpose(bank[4][0:r, (3 * j + t) * SH:(3 * j + t + 1) * SH], v[0:SH, t * P:t * P + r])
            mm.then_inc(s_tk, 1)
            pe.wait_ge(s_tkv, 4)
            pe.wait_ge(s_nrw, CT // 4)
            for c in range(2):
                pe.matmul(bank[5][:, 2 * c * SH:(2 * c + 1) * SH], upper[:, :], dA_tok[:, c, :], start=True, stop=True)
                mm = pe.matmul(bank[5][:, (2 * c + 1) * SH:(2 * c + 2) * SH], ones[:, :], dA_tok[:, c, :],
                               start=True, stop=True)
            mm.then_inc(s_tk, 1)
            pe.wait_ge(s_cx, 2 * CT)
            for c in range(2):
                for g in range(SG):
                    mm = transpose(bank[2 + c][:, g * N:(g + 1) * N], conv_out[:, 16 + g, c * P:(c + 1) * P])
            mm.then_inc(s_tk, 1)

            for g in range(SG):
                if g >= 1:
                    pe.wait_ge(s_cbm, 3 * g)
                    pe.wait_ge(s_So, TPG * g)
                for c in range(2):
                    for j in range(TPG):
                        mm = transpose(bank[6 + c][:, j * P:(j + 1) * P], conv_out[:, TPG * g + j, c * P:(c + 1) * P])
                    mm.then_inc(s_xtp, 1)
                pe.wait_ge(s_xdt, 2 * g + 2)
                Bg, Cg = conv_out[:, 16 + g, :], conv_out[:, 20 + g, :]
                for j, (cj, ci) in enumerate(((0, 0), (1, 1), (0, 1))):
                    mm = pe.matmul(bank[6][:, j * P:(j + 1) * P], Bg[:, cj * P:(cj + 1) * P], Cg[:, ci * P:(ci + 1) * P],
                                   start=True, stop=True)
                mm.then_inc(s_cb, 1)
                for j in range(TPG):
                    t = TPG * g + j
                    if t == 0:
                        pe.wait_ge(s_tkv, 8)
                    if t >= 2:
                        pe.wait_ge(s_seg, 4 * (t - 1))
                    for c in range(2):
                        for h in range(2):
                            mm = pe.matmul(bank[2 + t % 2][:, (2 * c + h) * P:(2 * c + h + 1) * P],
                                           dA_tok[:, c, 2 * t + h:2 * t + h + 1].to_broadcast([P, P]), upper[:, :],
                                           start=True, stop=True)
                    mm.then_inc(s_csb, 1)
                    yb = bank[4 + t % 2]
                    if t < 2:
                        pe.wait_ge(s_tkv, 8)
                    else:
                        pe.wait_ge(s_y, t - 1)
                    for h in range(2):
                        pe.matmul(yb[h * HD:(h + 1) * HD, 3 * P:4 * P],
                                  dA_tok[:, 1, 2 * t + h:2 * t + h + 1].to_broadcast([P, HD]),
                                  upper[:, :], start=True, stop=True)
                    pe.wait_ge(s_cbm, 3 * g + 3)
                    pe.wait_ge(s_M, t + 1)
                    for c in range(2):
                        for h in range(2):
                            pe.matmul(yb[h * HD:(h + 1) * HD, c * P:(c + 1) * P],
                                      xdt[:, c, j * P + h * HD:j * P + (h + 1) * HD],
                                      seg[:, t % 2, (2 * c + h) * P:(2 * c + h + 1) * P], start=True, stop=True)
                    pe.matmul(yb[:, 2 * P:3 * P], xw[:, 0, j * P:(j + 1) * P], cbm[:, 2, :],
                              start=True, stop=True).then_inc(s_yp, 1)
                    if t >= 1:
                        pe.wait_ge(s_So, t)
                    for c in range(2):
                        mm = pe.matmul(bank[7][:, c * N:(c + 1) * N], xw[:, c, j * P:(j + 1) * P],
                                       b_tok[:, c, g * N:(g + 1) * N], start=True, stop=True)
                    mm.then_inc(s_Sp, 1)

            pe.wait_ge(s_y, XT_TILES)
            pe.wait_ge(s_So, XT_TILES)
            for j in range(2):
                for g in range(SG):
                    mm = transpose(bank[2 + j][0:NS, g * N:(g + 1) * N], conv_out[:, 16 + SG * j + g, TP:T])
            mm.then_inc(s_dtk, 1)
            for t in range(XT_TILES):
                for h in range(2):
                    mm = pe.matmul(bank[4][h * HD:(h + 1) * HD, t * NS:(t + 1) * NS],
                                   ident[0:SH, 2 * t + h:2 * t + h + 1].to_broadcast([SH, HD]),
                                   dAT[0:SH, TP:T], start=True, stop=True)
            mm.then_inc(s_dtk, 1)
            for t in range(XT_TILES):
                g = t // TPG
                if t % TPG == 0:
                    if g >= 1:
                        pe.wait_ge(s_dcv, 3 + g)
                    else:
                        pe.wait_ge(s_dcv, 3)
                    for j in range(TPG):
                        mm = transpose(bank[5][0:NS, j * P:(j + 1) * P], conv_out[:, t + j, TP:T])
                    mm.then_inc(s_dtk, 1)
                    pe.wait_ge(s_cbp, 2 * g + 1)
                    if g >= 1:
                        pe.wait_ge(s_h, 2 * t)
                    for q in range(2):
                        mm = pe.matmul(bank[6 + q][:, :], ones[0:NS, :], diagm[0:NS, 4 * q:4 * q + 4, :],
                                       start=True, stop=True)
                    mm.then_inc(s_cbv, 1)
                n = 6 + t // 4
                if t % 4 == 0:
                    wait_chunk(pe, n)
                if t >= 2:
                    pe.wait_ge(s_zc, t - 1)
                wv = ring[:, n % RING, :].rearrange("p (k n) -> p k n", k=DT)
                for k in range(DT):
                    mm = pe.matmul(bank[t % 2][:, 0:T], wv[:, k, (t % 4) * P:(t % 4 + 1) * P], hT[:, k, :],
                                   start=(k == 0), stop=(k == DT - 1))
                mm.then_inc(s_zp if t < 15 else moes[0].gu, 1)
                for q in range(2):
                    u = 2 * t + q
                    if t % TPG == 0 and q == 0:
                        pe.wait_ge(s_cbp, 2 * g + 2)
                        pe.wait_ge(s_dcv, 4 + g)
                    if u >= 2:
                        pe.wait_ge(s_h, u - 1)
                    pe.matmul(bank[6 + q][:, :], dtx[0:NS, (t % TPG) * P:(t % TPG + 1) * P],
                              diagm[0:NS, 4 * q:4 * q + 4, :], start=True, stop=True).then_inc(s_op, 1)
            pe.wait_ge(s_gq, 1)
            for t, r in enumerate(ROWS):
                for k in range(XT_TILES):
                    mm = pe.matmul(bank[2][0:r, t:t + 1], zT[:, k, t * P:t * P + r], ones[:, 0:1],
                                   start=(k == 0), stop=(k == XT_TILES - 1))
            mm.then_inc(s_gs, 1)
            pe.wait_ge(s_gn, XT_TILES)
            for d in range(DT):
                n = 10 + d // 2
                if d % 2 == 0:
                    wait_chunk(pe, n)
                if d >= 2:
                    pe.wait_ge(s_oc, d - 1)
                wv = ring[:, n % RING, :].rearrange("p (k n) -> p k n", k=16)
                for k in range(XT_TILES):
                    mm = pe.matmul(bank[d % 2][:, 0:T], wv[:, k, (d % 2) * P:(d % 2 + 1) * P], conv_out[:, k, :],
                                   start=(k == 0), stop=(k == XT_TILES - 1))
                mm.then_inc({3: moes[0].gu, 5: moes[0].dn, 7: moes[0].dn}.get(d, s_op2), 1)
            pe.wait_ge(s_oc, DT)
            for t, r in enumerate(ROWS):
                for q in range(2):
                    j = 2 * t + q
                    if j >= 2:
                        pe.wait_ge(s_xa, j - 1)
                    for d in range(4):
                        mm = transpose(bank[3 + j % 2][0:r, d * P:(d + 1) * P], hT[:, 4 * q + d, t * P:t * P + r])
                    mm.then_inc(s_ot, 1)
            norm(1, xn_e)
            moe(0)

            norm(2, xn_a)
            pe.matmul(bank[7][:, 0:P], half[:, :], half[:, :], start=True, stop=True).then_inc(c_p, 1)
            pe.wait_ge(n_ht, 3 * DT)

            def qkv_tile(i):
                n = i // 4
                slot = (STREAM_SLOT[1] + n) % RING
                if i % 4 == 0:
                    pe.wait_ge(loads[1][slot], 16 * (n // RING + 1))
                if i >= 2:
                    pe.wait_ge(q_e, i - 1)
                wv = ring[:, slot, :].rearrange("p (k n) -> p k n", k=DT)
                for k in range(DT):
                    mm = pe.matmul(bank[i % 2][:, 0:T], wv[:, k, (i % 4) * P:(i % 4 + 1) * P], hT[:, k, :],
                                   start=(k == 0), stop=(k == DT - 1))
                mm.then_inc(moes[1].gu if i in (63, 71) else q_p, 1)

            def kv_job(g, j):
                n = 14 * g + j
                if n >= 2:
                    pe.wait_ge(kv_e, n - 1)
                if j < 12:
                    kind, q, c = j // 6, j % 6 // 3, j % 3
                    pe.wait_ge(q_e, 24 * g + 8 * kind + 4 * q + 4)
                else:
                    kind, q, c = 2, j - 12, 2
                    pe.wait_ge(h_c, 2 * DT * (g + 1))
                for d in range(4):
                    src = vT[:, d, :] if kind == 0 else (kT if kind == 1 else qT)[:, 4 * q + d, :]
                    mm = transpose(bank[4 + n % 2][0:ROWS[c], d * P:(d + 1) * P], src[:, c * P:c * P + ROWS[c]])
                mm.then_inc(kv_t, 1)

            def query(g, u):
                b, q = u // 2, u % 2
                n = 16 * g + u
                if u == 0:
                    pe.wait_ge(kv_e, 14 * g + 14)
                    pe.wait_ge(h_m, 2 * DT * (g + 1))
                if n >= 2:
                    pe.wait_ge(k_m, n - 1)
                pe.matmul(bank[2 + q][:, :], ident[0:NS, b:b + 1].to_broadcast([NS, P]),
                          q_s[0:NS, 512 * q:512 * q + 512], start=True, stop=True).then_inc(k_q, 1)

            def scores(g, t):
                n = DT * g + t
                pe.wait_ge(q_e, 24 * g + 17 + t)
                for h in range(2):
                    if n >= 1:
                        pe.wait_ge(h_m, 2 * n - 1 + h)
                    if t == 0 and g >= 1:
                        pe.wait_ge(k_m, 16 * g)
                    r = slice(h * HD, (h + 1) * HD)
                    pe.matmul(bank[2 + h][:, 0:P], qT[r, t, 0:P], kT[r, t, 0:P], start=True, stop=True)
                    pe.matmul(bank[2 + h][:, P:3 * P], qT[r, t, P:TP], kT[r, t, 0:TP],
                              start=True, stop=True).then_inc(h_s, 1)

            def turn(g, t):
                n = DT * g + t
                pe.wait_ge(h_e, 4 * (n + 1))
                if t == 0:
                    pe.wait_ge(kv_e, 14 * g + 12)
                for h in range(2):
                    if n >= 1:
                        pe.wait_ge(h_c, 2 * n - 1 + h)
                    for j in range(3):
                        mm = transpose(bank[4 + h][:, j * P:(j + 1) * P], sm[:, t % 2, h, j * P:(j + 1) * P])
                    mm.then_inc(h_t, 1)

            def values(g, t):
                n = DT * g + t
                pe.wait_ge(h_c, 2 * n + 2)
                if n >= 1:
                    pe.wait_ge(h_o, n)
                for h in range(2):
                    c = (2 * t + h) * HD
                    out = [bank[6][:, (2 * i + h) * HD:(2 * i + h + 1) * HD] for i in range(2)]
                    pe.matmul(out[0], pT[:, t % 2, h, 0, :], KV[:, 0, 1, c:c + HD], start=True, stop=True)
                    pe.matmul(out[1], pT[:, t % 2, h, 1, :], KV[:, 0, 1, c:c + HD], start=True, stop=False)
                    mm = pe.matmul(out[1], pT[:, t % 2, h, 2, :], KV[:, 1, 1, c:c + HD], start=False, stop=True)
                mm.then_inc(h_v, 1)

            for g in range(NGRP):
                for i in range(16):
                    qkv_tile(24 * g + i)
                    if g >= 1:
                        query(g - 1, i)
                    if i % 4 == 0 and i >= 4:
                        for j in range(3):
                            kv_job(g, 3 * (i // 4 - 1) + j)
                for t in range(DT + 3):
                    if t < DT:
                        qkv_tile(24 * g + 16 + t)
                    if t == 0:
                        for j in range(3):
                            kv_job(g, 9 + j)
                    if 1 <= t <= DT:
                        scores(g, t - 1)
                    if 2 <= t <= DT + 1:
                        turn(g, t - 2)
                    if t >= 3:
                        values(g, t - 3)
                kv_job(g, 12)
                kv_job(g, 13)
            for u in range(16):
                query(NGRP - 1, u)
            pe.wait_ge(o_n, 2)
            for c in range(2):
                for q in range(2):
                    j = 2 * c + q
                    if j >= 2:
                        pe.wait_ge(o_c, j - 1)
                    for d in range(4):
                        mm = transpose(bank[4 + q][:, d * P:(d + 1) * P], O[:, c, (4 * q + d) * P:(4 * q + d + 1) * P])
                    mm.then_inc(o_t, 1)
            pe.wait_ge(k_r, NS * NGRP)
            pe.wait_ge(c_v, 1 + NGRP)
            at = 0
            for g in range(NGRP):
                transpose(bank[7][:, at:at + KEYS[g]], S_s[0:KEYS[g], g, :])
                at += KEYS[g]
            for g in range(NGRP):
                for h in range(2):
                    r = slice(h * HD, (h + 1) * HD)
                    mm = pe.matmul(bank[7][r, at + g:at + g + 1], prod[r, g, :], ones[r, 0:1], start=True, stop=True)
            mm.then_inc(c_p, 1)
            pe.wait_ge(c_v, 6 + NGRP)
            at = 0
            for g in range(NGRP):
                transpose(bank[6][0:KEYS[g], g * P:(g + 1) * P], p_s[:, at:at + KEYS[g]])
                mm = pe.matmul(bank[2][:, g * DT * NS:(g + 1) * DT * NS], PHp[:, g, :], fold[:, :],
                               start=True, stop=True)
                at += KEYS[g]
            mm.then_inc(c_p, 1)
            pe.wait_ge(c_a, 3)
            pe.wait_ge(o_c, 4)
            for b in range(NS):
                pe.wait_ge(v_l[b % 2], 48 * (b // 2 + 1))
                for t in range(DT):
                    c = 2 * (b * DT + t)
                    for g in range(NGRP):
                        n = KEYS[g]
                        mm = pe.matmul(bank[4][:, c:c + 2], V_in[0:n, b % 2, g, t * P:(t + 1) * P],
                                       pTs[0:n, g, t * NS + b:P:DT * NS], start=(g == 0), stop=(g == NGRP - 1))
                mm.then_inc(v_p, 1)
            pe.wait_ge(c_v, 8 + NGRP)
            for d in range(DT):
                n = ATT_CHUNKS - 2 + d // 4
                slot = (STREAM_SLOT[1] + n) % RING
                if d % 4 == 0:
                    pe.wait_ge(loads[1][slot], 16 * (n // RING + 1))
                if d >= 2:
                    pe.wait_ge(s_oc, DT + d - 1)
                wv = ring[:, slot, :].rearrange("p (k n) -> p k n", k=DT)
                for k in range(DT):
                    mm = pe.matmul(bank[d % 2][:, 0:T], wv[:, k, (d % 4) * P:(d % 4 + 1) * P], yT[:, k, :],
                                   start=(k == 0), stop=(k == DT - 1))
                mm.then_inc(moes[1].dn if d % 4 == 3 else s_op2, 1)
            pe.wait_ge(s_oc, 2 * DT)
            for t, r in enumerate(ROWS):
                for q in range(2):
                    j = 2 * t + q
                    if j >= 2:
                        pe.wait_ge(s_xa, 12 + j - 1)
                    for d in range(4):
                        mm = transpose(bank[3 + j % 2][0:r, d * P:(d + 1) * P], hT[:, 4 * q + d, t * P:t * P + r])
                    mm.then_inc(s_ot, 1)
            norm(3, xn_e)
            moe(1)

        @block.scalar
        def _(act):
            def norm(k, xn):
                if k == 0:
                    act.wait_ge(s_xld, 32)
                else:
                    act.wait_ge(s_xa, 6 * k)
                for t, r in enumerate(ROWS):
                    act.activation(xn[0:r, t, :], X[0:r, t, :], ACT.Square, accum_out=ss[0:r, t:t + 1]).then_inc(n_ss, 1)
                act.wait_ge(n_var, k + 1)
                act.activation(rstd[:, 0:3], ss[:, 0:3], ACT.Sqrt).then_inc(n_std, 1)

            def moe(l):
                s = moes[l]
                act.sem_inc(s.at, 1)
                act.wait_ge(m_ge, 2 * l + 1)
                act.activation(g_a[:, :, :], g_a[:, :, :], ACT.Exp).then_inc(m_ex, 1)
                act.wait_ge(m_ge, 2 * l + 2)
                act.activation(g_s[:, 4, :], g_s[:, 4, :], ACT.Exp).then_inc(m_ex, 1)
                act.wait_ge(m_R, l + 1)
                rounds = act.value_load(rounds_i[0:1, 0:1], min_val=1, max_val=ROUNDS)
                with act.Fori(0, rounds * PAIRS) as it:
                    act.wait_ge(s.gu, it * 2 + 3)
                    act.wait_ge(s.act, it + 1)
                    act.activation(sg[:, :], bank[0][:, :], ACT.Silu).then_inc(s.sg, 1)
                    act.wait_ge(s.tp, it + 1)
                    act.activation(actT[:, :, :], bank[0][:, :].rearrange("p (f s) -> p f s", f=4),
                                   ACT.Copy).then_inc(s.at, 1)
                    act.wait_ge(s.cp, it + 1)
                    act.activation(CmT[:, :], bank[1][:, 0:T], ACT.Copy).then_inc(s.cpt, 1)
                    act.wait_ge(s.dh, it + 1)
                    act.activation(ysl[:, 0:4, :], bank[2][:, :].rearrange("p (d s) -> p d s", d=4),
                                   ACT.Copy).then_inc(s.y, 1)
                    act.wait_ge(s.dn, it * 2 + 4)
                    act.activation(ysl[:, 4:8, :], bank[3][:, :].rearrange("p (d s) -> p d s", d=4),
                                   ACT.Copy).then_inc(s.y, 1)

            act.wait_ge(s_vvec, 3)
            norm(0, xn_m)
            act.wait_ge(s_vld, 128)
            act.wait_ge(s_dtp, 1)
            act.activation(spt[0:SH, 0, :], bank[4][0:SH, 0:T], ACT.Identity, bias=head_v[0:SH, 0:1]).then_inc(s_dtz, 1)
            act.activation(head_v[0:SH, 2:3], head_v[0:SH, 1:2], ACT.Exp).then_inc(s_dtz, 1)
            act.wait_ge(s_dte, 1)
            act.activation(spt[0:SH, 2, :], spt[0:SH, 1, :], ACT.Exp, scale=-1.0).then_inc(s_dtz, 1)
            for i in range(CT + 2):
                if i < CT:
                    act.wait_ge(s_prj, i + 1)
                    if i == 0:
                        act.wait_ge(s_stc, 3)
                    if i >= RAWS:
                        act.wait_ge(s_cv, i - RAWS + 1)
                        act.wait_ge(s_nc, 2 * (i - RAWS + 1))
                    b = bank[i % 2]
                    act.activation(raws[:, i % RAWS, PADW:PADW + TP], b[:, 0:TP], ACT.Copy).then_inc(s_raw, 1)
                    new = raws[:, i % RAWS, SAMP0:RAW].rearrange("p (b w) -> p b w", w=CW)[:, :, PADW]
                    act.activation(new, b[:, TP:T], ACT.Copy).then_inc(s_raw, 1)
                if i >= 2:
                    j = i - 2
                    ct = tile_order[j]
                    act.wait_ge(s_cv, j + 1)
                    act.activation(conv_out[:, ct, 0:TP], cacc[:, j % 2, 0:TP], ACT.Silu,
                                   bias=cbcol[:, ct:ct + 1]).then_inc(s_cx, 1)
                    act.activation(conv_out[:, ct, TP:T], cacc[:, j % 2, SAMP0:CONV:CW], ACT.Silu,
                                   bias=cbcol[:, ct:ct + 1]).then_inc(s_cx, 1)
            for q in range(CT // 4):
                act.wait_ge(s_ntp, q + 1)
                if q >= 2:
                    act.wait_ge(s_nst[q % 2], 32 * (q // 2))
                act.activation(newr[0:11, q % 2, :], bank[5 + q % 2][0:11, :], ACT.Copy).then_inc(s_nrw, 1)
            act.wait_ge(s_tkv, 5)
            act.activation(w_tok[:, :, :], w_tok[:, :, :], ACT.Exp).then_inc(s_achain, 1)
            for t in range(XT_TILES):
                act.wait_ge(s_seg, 4 * (t + 1))
                act.activation(seg[:, t % 2, :], seg[:, t % 2, :], ACT.Exp).then_inc(s_dec, 1)
                act.wait_ge(s_yp, t + 1)
                if t >= 2:
                    act.wait_ge(s_So, t - 1)
                    act.wait_ge(s_y, t - 1)
                act.activation(Et[:, t % 2, :], bank[4 + t % 2][:, 3 * P:4 * P], ACT.Exp).then_inc(s_E, 1)
                act.wait_ge(s_Sp, t + 1)
                if t >= 2:
                    act.wait_ge(s_Sst[t % 2], 16 * (t // 2))
                act.activation(hout[:, t % 2, :], bank[7][:, N:2 * N], ACT.Copy).then_inc(s_S1, 1)
            act.wait_ge(s_dtk, 2)
            act.activation(dAe[:, :, :], bank[4][:, 0:XT_TILES * NS].rearrange("p (t b) -> p t b", b=NS),
                           ACT.Exp).then_inc(s_dcv, 1)
            for t in range(XT_TILES):
                if t < 15:
                    act.wait_ge(s_zp, t + 1)
                else:
                    act.wait_ge(moes[0].gu, 1)
                act.activation(zT[:, t, :], bank[t % 2][:, 0:T], ACT.Copy).then_inc(s_zc, 1)
            act.wait_ge(s_zc, XT_TILES)
            act.activation(zT[:, :, :], zT[:, :, :], ACT.Silu).then_inc(s_zs, 1)
            act.wait_ge(s_g, XT_TILES)
            act.activation(zT[:, :, :], conv_out[:, 0:XT_TILES, :], ACT.Square).then_inc(s_gq, 1)
            for t in range(XT_TILES):
                act.wait_ge(s_gq, 1)
                act.activation(conv_out[:, t, :], conv_out[:, t, :], ACT.Copy, scale=gssm[:, t:t + 1]).then_inc(s_gn, 1)
            act.wait_ge(s_gs, 2)
            act.activation(rstd[:, 0:3], ss[:, 0:3], ACT.Sqrt).then_inc(s_gq, 1)
            for d in range(DT):
                when = {0: (s_op2, 1), 1: (s_op2, 2), 2: (s_op2, 3), 3: (moes[0].gu, 2), 4: (s_op2, 4),
                        5: (moes[0].dn, 1), 6: (s_op2, 5), 7: (moes[0].dn, 2)}[d]
                act.wait_ge(*when)
                act.activation(hT[:, d, :], bank[d % 2][:, 0:T], ACT.Copy).then_inc(s_oc, 1)
            norm(1, xn_e)
            moe(0)

            norm(2, xn_a)

            def qkv_done(i):
                if i in (63, 71):
                    act.wait_ge(moes[1].gu, 1 if i == 63 else 2)
                else:
                    act.wait_ge(q_p, i + 1 - (i > 63))

            def copy_tile(g, i):
                n = 24 * g + i
                qkv_done(n)
                if i < 8:
                    if i >= 4:
                        act.wait_ge(kv_t, 14 * g + 3)
                    elif g >= 1:
                        act.wait_ge(kv_t, 14 * g - 8)
                    act.activation(vTs[:, g, i * NS:(i + 1) * NS], bank[n % 2][:, TP:T], ACT.Copy).then_inc(q_vs, 1)
                    dst = vT[:, i % 4, :]
                elif i < 16:
                    if g >= 1:
                        act.wait_ge(h_s, 2 * DT * g)
                        act.wait_ge(c_v, g)
                    dst = kT[:, i - 8, :]
                else:
                    dst = qT[:, i - 16, :]
                act.activation(dst, bank[n % 2][:, 0:T], ACT.Copy).then_inc(q_e, 1)

            def copy_rows(g, j):
                n = 14 * g + j
                act.wait_ge(kv_t, n + 1)
                if j < 12:
                    kind, q, c = j // 6, j % 6 // 3, j % 3
                    if g >= 1 and j == 0:
                        act.wait_ge(kvst, 32 * g)
                        act.wait_ge(h_v, DT * g)
                    row = kv_s_rows[:, (1 - kind) * D:(2 - kind) * D] if c == 2 else KV[:, c, 1 - kind, :]
                else:
                    q, c = j - 12, 2
                    if g >= 1:
                        act.wait_ge(k_q, 16 * g)
                    row = q_s[:, :]
                act.activation(row[0:ROWS[c], 512 * q:512 * q + 512], bank[4 + n % 2][0:ROWS[c], :],
                               ACT.Copy).then_inc(kv_e, 1)

            def exps(g, t):
                n = DT * g + t
                act.wait_ge(h_x, n + 1)
                hs = slice(2 * t, 2 * t + 2)
                if g >= 1:
                    act.activation(al[:, :, hs], al[:, :, hs], ACT.Exp).then_inc(s_achain, 1)
                for h in range(2):
                    for i, (c0, c1) in enumerate(((0, P), (P, 3 * P))):
                        k = 2 * t + h
                        act.activation(sm[:, t % 2, h, c0:c1], sm[:, t % 2, h, c0:c1], ACT.Exp,
                                       bias=Mn[:, i, k:k + 1], accum_out=rs[:, i, k:k + 1]).then_inc(h_e, 1)

            def copy_probs(g, t):
                n = DT * g + t
                for h in range(2):
                    act.wait_ge(h_t, 2 * n + h + 1)
                    if n >= 2:
                        act.wait_ge(h_v, n - 1)
                    act.activation(pT[:, t % 2, h, :, :].rearrange("p a b -> p (a b)"), bank[4 + h][:, 0:3 * P],
                                   ACT.Copy).then_inc(h_c, 1)

            act.wait_ge(a_mv, 3)
            for g in range(NGRP):
                for i in range(16):
                    if i % 4 == 0 and i >= 4:
                        for j in range(3):
                            copy_rows(g, 3 * (i // 4 - 1) + j)
                    copy_tile(g, i)
                for t in range(DT + 3):
                    if t < DT:
                        copy_tile(g, 16 + t)
                    if t == 0:
                        for j in range(3):
                            copy_rows(g, 9 + j)
                    if 2 <= t <= DT + 1:
                        copy_probs(g, t - 2)
                    if 1 <= t <= DT:
                        exps(g, t - 1)
                copy_rows(g, 12)
                copy_rows(g, 13)
            for j in range(4):
                c, q = j // 2, j % 2
                act.wait_ge(o_t, j + 1)
                act.activation(yT[:, 4 * q:4 * q + 4, c * P:(c + 1) * P],
                               bank[4 + q][:, :].rearrange("p (d i) -> p d i", d=4), ACT.Copy).then_inc(o_c, 1)
            n_keys = sum(KEYS) + NGRP
            act.wait_ge(c_v, 2 + NGRP)
            act.activation(p_s[:, 0:n_keys], bank[7][:, 0:n_keys], ACT.Exp, bias=s_st[:, 1:2], scale=SCALE,
                           accum_out=s_st[:, 2:3]).then_inc(c_a, 1)
            act.wait_ge(c_p, 3)
            act.activation(pTs[:, 0:2, :], bank[6][:, 0:2 * P].rearrange("p (g c) -> p g c", g=2),
                           ACT.Copy).then_inc(c_a, 1)
            act.activation(pTs[0:KEYS[2], 2, :], bank[6][0:KEYS[2], 2 * P:3 * P], ACT.Copy).then_inc(c_a, 1)
            for d in range(DT):
                if d % 4 == 3:
                    act.wait_ge(moes[1].dn, d // 4 + 1)
                else:
                    act.wait_ge(s_op2, 5 + 3 * (d // 4) + d % 4 + 1)
                act.activation(hT[:, d, :], bank[d % 2][:, 0:T], ACT.Copy).then_inc(s_oc, 1)
            norm(3, xn_e)
            moe(1)
            norm(4, xn_e)

        @block.vector
        def _(v):
            steps = [0]

            def link(ins):
                steps[0] += 1
                ins.then_inc(s_chain, 1)
                v.wait_ge(s_chain, steps[0])

            v.memset(ss[:, :], 1.0).then_inc(s_vvec, 1)
            v.memset(rstd[:, :], 1.0).then_inc(s_vvec, 1)
            v.memset(arena[:, 0:4], 0.0).then_inc(s_vvec, 1)
            v.wait_ge(s_pvec, 1)
            v.tensor_copy(vcol[:, :], bank[7][:, 0:72]).then_inc(s_vvec, 1)
            v.tensor_copy(cwcol[:, :], bank[7][:, 72:168]).then_inc(s_vvec, 1)
            v.tensor_copy(d_col[:, :], bank[7][:, 168:184]).then_inc(s_vvec, 1)

            def norm(k, xn, g):
                v.wait_ge(n_ss, 3 * (k + 1))
                v.tensor_scalar(ss[:, 0:3], ss[:, 0:3], 1.0 / D, EPS, ALU.mult, ALU.add).then_inc(n_var, 1)
                v.wait_ge(n_std, k + 1)
                link(v.reciprocal(rstd[:, 0:3], rstd[:, 0:3]))
                for t, r in enumerate(ROWS):
                    v.tensor_scalar(xn[0:r, t, :], X[0:r, t, :], rstd[0:r, t:t + 1], None, ALU.mult).then_inc(n_xn, 1)
                for d in range(DT):
                    v.wait_ge(n_tp, DT * k + d + 1)
                    v.tensor_scalar(hT[:, d, :], bank[d % 2][:, 0:T], g[:, d:d + 1], None, ALU.mult).then_inc(n_ht, 1)

            def bc(x, *shape):
                return x.to_broadcast([P, *shape])

            def first_max(x, order, n, mx, oh, tmp):
                link(v.tensor_reduce(mx, x, AX, ALU.max))
                link(v.tensor_tensor(oh, x, bc(mx.unsqueeze(2), 3, n), ALU.is_equal))
                link(v.tensor_tensor(oh, oh, bc(order.unsqueeze(1), 3, n), ALU.mult))
                link(v.tensor_reduce(tmp, oh, AX, ALU.max))
                link(v.tensor_tensor(oh, oh, bc(tmp.unsqueeze(2), 3, n), ALU.is_equal))

            def moe(l):
                s = moes[l]
                v.sem_inc(s.act, 1)
                v.memset(CmT[:, :], 0.0).then_inc(s.cpt, 1)
                v.memset(ysl[:, :, :], 0.0).then_inc(s.y, 2)
                v.memset(accT[:, :, :], 0.0).then_inc(s.acc, 1)
                link(v.memset(lg[:, :, :], 0.0))
                link(v.memset(rk[:, :, :], -1.0))
                link(v.memset(cc[:, :, :], 0.0))
                link(v.memset(msk[:, :, :], 0.0))
                link(v.memset(cmb[:, :, :], 0.0))
                link(v.memset(rnk[:, :, :], 0.0))
                v.wait_ge(m_lg, l + 1)
                b6 = bank[6][:, 0:3 * (EG + NE)].rearrange("p (t e) -> p t e", t=3)
                link(v.tensor_copy(lg[:, 0:2, :], b6[:, 0:2, :]))
                link(v.tensor_copy(lg[0:NS, 2, :], b6[0:NS, 2, :]))
                gl = lg[:, :, 0:EG]
                el = lg[:, :, EG:].rearrange("p t (g e) -> p t g e", g=EG)
                gmax, gtmp, gate, m1, dd, w1, w2, m2 = (g_s[:, i, :] for i in range(8))
                first_max(gl, first4[:, :], EG, gmax, g_oh[:, :, :], gtmp)
                v.tensor_tensor(g_a[:, :, :], gl, bc(gmax.unsqueeze(2), 3, EG), ALU.subtract).then_inc(m_ge, 1)
                link(v.tensor_tensor(e_w[:, :, :, :], el, bc(g_oh[:, :, :].unsqueeze(3), 3, EG, EPG), ALU.mult))
                link(v.tensor_reduce(es[:, :, :], e_w[:, :, :, :].rearrange("p t g e -> p t e g"), AX, ALU.add))
                first_max(es[:, :, :], first8[:, :], EPG, m1, oh1[:, :, :], gtmp)
                link(v.scalar_tensor_tensor(out=e_a[:, :, :], in0=oh1[:, :, :], scalar=-BIG, in1=es[:, :, :],
                                            op0=ALU.mult, op1=ALU.add))
                first_max(e_a[:, :, :], first8[:, :], EPG, m2, oh2[:, :, :], gtmp)
                v.tensor_tensor(dd, m2, m1, ALU.subtract).then_inc(m_ge, 1)
                v.wait_ge(m_ex, 2 * l + 1)
                link(v.tensor_reduce(gate, g_a[:, :, :], AX, ALU.add))
                v.wait_ge(m_ex, 2 * l + 2)
                link(v.tensor_scalar(w1, dd, 1.0, None, ALU.add))
                link(v.tensor_tensor(w1, w1, gate, ALU.mult))
                link(v.reciprocal(w1, w1))
                link(v.tensor_tensor(w2, w1, dd, ALU.mult))
                link(v.tensor_tensor(e_sel[:, :, :], oh1[:, :, :], oh2[:, :, :], ALU.add))
                link(v.tensor_tensor(oh1[:, :, :], oh1[:, :, :], bc(w1.unsqueeze(2), 3, EPG), ALU.mult))
                link(v.tensor_tensor(oh2[:, :, :], oh2[:, :, :], bc(w2.unsqueeze(2), 3, EPG), ALU.mult))
                link(v.tensor_tensor(e_in[:, :, :], oh1[:, :, :], oh2[:, :, :], ALU.add))
                for out, x in ((cmb, e_in), (msk, e_sel)):
                    for r, t0, t1 in ((P, 0, 2), (NS, 2, 3)):
                        n = t1 - t0
                        ins = v.tensor_tensor(out[0:r, t0:t1, :].rearrange("p t (g e) -> p t g e", g=EG),
                                              g_oh[0:r, t0:t1, :].unsqueeze(3).to_broadcast([r, n, EG, EPG]),
                                              x[0:r, t0:t1, :].unsqueeze(2).to_broadcast([r, n, EG, EPG]), ALU.mult)
                        if out is msk:
                            ins.then_inc(m_mk, 1)
                        else:
                            link(ins)
                v.wait_ge(m_rk, l + 1)
                v.wait_ge(m_mk, 2 * l + 2)
                b7 = bank[7][:, 0:4 * NE].rearrange("p (t e) -> p t e", t=4)
                link(v.tensor_reduce(cnt_s[0:1, 0:1], b7[0:1, 3, :], AX, ALU.max))
                link(v.tensor_scalar(cnt_s[0:1, 1:1 + ROUNDS], thresh[0:1, 0:ROUNDS], cnt_s[0:1, 0:1], None, ALU.is_lt))
                link(v.tensor_reduce(cnt_s[0:1, 7:8], cnt_s[0:1, 1:1 + ROUNDS], AX, ALU.add))
                v.tensor_copy(rounds_i[0:1, 0:1], cnt_s[0:1, 7:8]).then_inc(m_R, 1)
                link(v.scalar_tensor_tensor(out=rnk[:, 0:2, :], in0=b7[:, 0:2, :], scalar=1.0, in1=msk[:, 0:2, :],
                                            op0=ALU.add, op1=ALU.mult))
                link(v.scalar_tensor_tensor(out=rnk[0:NS, 2, :], in0=b7[0:NS, 2, :], scalar=1.0, in1=msk[0:NS, 2, :],
                                            op0=ALU.add, op1=ALU.mult))
                for r in range(ROUNDS):
                    link(v.tensor_scalar(rk[:, :, r * NE:(r + 1) * NE], rnk[:, :, :], -1.0 - SLOTS * r, None, ALU.add))
                    link(v.tensor_copy(cc[:, :, r * NE:(r + 1) * NE], cmb[:, :, :]))

                def slots(col):
                    for t in range(3):
                        ins = v.tensor_tensor(Pm[:, t, :, :], slot_no[:, :].unsqueeze(1).to_broadcast([P, 2, SLOTS]),
                                              bc(rk[:, t, col].unsqueeze(2), 2, SLOTS), ALU.is_equal)
                    ins.then_inc(s.peq, 1)

                def shares(col):
                    for t in range(3):
                        ins = v.tensor_tensor(Cm[:, t, :, :], Pm[:, t, :, :],
                                              bc(cc[:, t, col].unsqueeze(2), 2, SLOTS), ALU.mult)
                    ins.then_inc(s.cm, 1)

                def tokens(n):
                    for q in range(2):
                        v.wait_ge(s.ga, n * 2 + q + 1)
                        v.tensor_tensor(Xg[:, 4 * q:4 * q + 4, :], bank[4 + q][:, :].rearrange("p (d s) -> p d s", d=4),
                                        bc(gffn(l)[:, 4 * q:4 * q + 4].unsqueeze(2), 4, P), ALU.mult).then_inc(s.xg, 1)

                def add(n):
                    for d in range(DT):
                        v.wait_ge(s.sc, n * 8 + d + 1)
                        v.tensor_tensor(accT[:, d, :], accT[:, d, :], bank[6 + d % 2][:, 0:T], ALU.add).then_inc(s.acc, 1)

                slots(slice(0, 2))
                v.wait_ge(m_R, l + 1)
                rounds = v.value_load(rounds_i[0:1, 0:1], min_val=1, max_val=ROUNDS)
                tokens(0)
                with v.Fori(0, rounds * PAIRS) as it:
                    v.wait_ge(s.peq, it + 1)
                    shares(bass.ds(it * 2, 2))
                    v.wait_ge(s.cm, it + 1)
                    slots(bass.ds(it * 2 + 2, 2))
                    v.wait_ge(s.sg, it + 1)
                    v.wait_ge(s.gu, it * 2 + 4)
                    v.tensor_tensor(act_r[:, :], sg[:, :], bank[1][:, :], ALU.mult).then_inc(s.act, 1)
                    add(it)
                    tokens(it + 1)
                add(rounds * PAIRS)
                v.wait_ge(s.acc, rounds * (8 * PAIRS) + 9)
                for t, r in enumerate(ROWS):
                    for q in range(2):
                        j = 2 * t + q
                        v.wait_ge(m_t, 6 * l + j + 1)
                        xs = X[0:r, t, 512 * q:512 * q + 512]
                        v.tensor_tensor(xs, xs, bank[j % 2][0:r, :], ALU.add).then_inc(s_xa, 1)

            v.wait_ge(s_vvec, 6)
            norm(0, xn_m, gmix(0))
            for q in range(2):
                v.wait_ge(s_stp, q + 1)
                v.tensor_copy(stT[:, 12 * q:12 * q + 12, :],
                              bank[5 + q][:, 0:288].rearrange("p (c w) -> p c w", c=12)).then_inc(s_stc, 1)
            v.memset(raws[:, :, 0:PADW], 0.0).then_inc(s_stc, 1)
            z, az, u, s, s2, p_ = (spt[0:SH, i, :] for i in range(6))
            v.wait_ge(s_dtz, 2)
            v.scalar_tensor_tensor(out=az, in0=z, scalar=-1.0, in1=z, op0=ALU.mult, op1=ALU.max).then_inc(s_dte, 1)
            v.wait_ge(s_dtz, 3)
            link(v.tensor_scalar(s, u, 2.0, None, ALU.add))
            link(v.reciprocal(s, s))
            link(v.tensor_tensor(s, s, u, ALU.mult))
            link(v.tensor_tensor(s2, s, s, ALU.mult))
            link(v.tensor_scalar(p_, s2, 1.0 / 15, None, ALU.mult))
            for k in range(13, 1, -2):
                link(v.scalar_tensor_tensor(out=p_, in0=p_, scalar=1.0 / k, in1=s2, op0=ALU.add, op1=ALU.mult))
            link(v.scalar_tensor_tensor(out=p_, in0=p_, scalar=1.0, in1=s, op0=ALU.add, op1=ALU.mult))
            link(v.tensor_scalar(z, z, 0.0, None, ALU.max))
            link(v.scalar_tensor_tensor(out=dtT[0:SH, :], in0=p_, scalar=2.0, in1=z, op0=ALU.mult, op1=ALU.add))
            v.tensor_scalar(head_v[0:SH, 3:4], head_v[0:SH, 2:3], -1.0, None, ALU.mult).then_inc(s_dt, 1)
            v.wait_ge(s_dt, 1)
            v.tensor_scalar(dAT[0:SH, :], dtT[0:SH, :], head_v[0:SH, 3:4], None, ALU.mult).then_inc(s_dt, 1)
            for i, ct in enumerate(tile_order):
                v.wait_ge(s_raw, 2 * i + 2)
                v.wait_ge(s_rst, i + 1)
                if i >= 2:
                    v.wait_ge(s_cx, 2 * i - 2)
                r, acc = raws[:, i % RAWS, :], cacc[:, i % 2, :]
                link(v.tensor_scalar(acc, r[:, 0:CONV], cwcol[:, ct:ct + 1], None, ALU.mult))
                for w in range(1, CW):
                    c = cwcol[:, w * CT + ct:w * CT + ct + 1]
                    ins = v.scalar_tensor_tensor(out=acc, in0=r[:, w:w + CONV], scalar=c, in1=acc,
                                                 op0=ALU.mult, op1=ALU.add)
                    if w < CW - 1:
                        link(ins)
                ins.then_inc(s_cv, 1)
            v.wait_ge(s_tk, 1)
            bt = bank[4][:, 0:6 * SH].rearrange("p (j t h) -> p j t h", j=2, t=3)
            v.tensor_copy(dt_tok[:, 0:2, :], bt[:, 0, 0:2, :]).then_inc(s_tkv, 1)
            v.tensor_copy(dt_tok[0:NS, 2, :], bt[0:NS, 0, 2, :]).then_inc(s_tkv, 1)
            v.tensor_copy(dA_tok[:, 0:2, :], bt[:, 1, 0:2, :]).then_inc(s_tkv, 1)
            v.tensor_copy(dA_tok[0:NS, 2, :], bt[0:NS, 1, 2, :]).then_inc(s_tkv, 1)
            v.wait_ge(s_tk, 2)
            bt = bank[5][:, 0:4 * SH].rearrange("p (c j h) -> p c j h", c=2, j=2)
            link(v.tensor_copy(cs_tok[:, :, :], bt[:, :, 0, :]))
            v.tensor_tensor(w_tok[:, :, :], bt[:, :, 1, :], cs_tok[:, :, :], ALU.subtract).then_inc(s_tkv, 1)
            v.wait_ge(s_tk, 3)
            for c in range(2):
                v.tensor_copy(b_tok[:, c, :], bank[2 + c][:, :]).then_inc(s_tkv, 1)
            v.memset(ysum[:, 0:4], 0.0).then_inc(s_tkv, 1)
            v.wait_ge(s_achain, 1)
            v.wait_ge(s_tkv, 8)
            for i in range(2):
                v.wait_ge(s_nst[i], 16 * CT // 4)
            for g in range(SG):
                if g >= 1:
                    v.wait_ge(s_Sp, TPG * g)
                hs = slice(2 * TPG * g, 2 * TPG * (g + 1))
                for c in range(2):
                    v.wait_ge(s_xtp, 2 * g + c + 1)
                    xv = xdt[:, c, :].rearrange("p (h d) -> p h d", d=HD)
                    link(v.tensor_tensor(xv, bank[6 + c][:, :].rearrange("p (h d) -> p h d", d=HD),
                                         dt_tok[:, c, hs].unsqueeze(2).to_broadcast([P, 2 * TPG, HD]), ALU.mult))
                    v.tensor_tensor(xw[:, c, :].rearrange("p (h d) -> p h d", d=HD), xv,
                                    w_tok[:, c, hs].unsqueeze(2).to_broadcast([P, 2 * TPG, HD]),
                                    ALU.mult).then_inc(s_xdt, 1)
                v.wait_ge(s_cb, g + 1)
                for j in range(2):
                    v.tensor_tensor(cbm[:, j, :], bank[6][:, j * P:(j + 1) * P], upper[:, :], ALU.mult).then_inc(s_cbm, 1)
                v.tensor_copy(cbm[:, 2, :], bank[6][:, 2 * P:3 * P]).then_inc(s_cbm, 1)
                for j in range(TPG):
                    t = TPG * g + j
                    v.wait_ge(s_csb, t + 1)
                    if t >= 2:
                        v.wait_ge(s_yp, t - 1)
                    for c in range(2):
                        for h in range(2):
                            q = 2 * c + h
                            v.tensor_scalar(seg[:, t % 2, q * P:(q + 1) * P], bank[2 + t % 2][:, q * P:(q + 1) * P],
                                            cs_tok[:, c, 2 * t + h:2 * t + h + 1], 0.0,
                                            ALU.subtract, ALU.min).then_inc(s_seg, 1)
                    v.wait_ge(s_dec, t + 1)
                    v.wait_ge(s_cbm, 3 * g + 3)
                    sv = seg[:, t % 2, :].rearrange("p (c h i) -> p c h i", c=2, h=2)
                    v.tensor_tensor(sv, sv, cbm[:, 0:2, :].unsqueeze(2).to_broadcast([P, 2, 2, P]),
                                    ALU.mult).then_inc(s_M, 1)
                    v.wait_ge(s_E, t + 1)
                    yb = bank[4 + t % 2]
                    link(v.tensor_tensor(y1[:, 0, :], yb[:, 2 * P:3 * P], Et[:, t % 2, :], ALU.mult))
                    link(v.scalar_tensor_tensor(out=conv_out[:, t, 0:TP], in0=conv_out[:, t, 0:TP],
                                                scalar=d_col[:, t:t + 1], in1=yb[:, 0:TP], op0=ALU.mult, op1=ALU.add))
                    v.tensor_tensor(conv_out[:, t, P:TP], conv_out[:, t, P:TP], y1[:, 0, :], ALU.add).then_inc(s_y, 1)
                    v.wait_ge(s_S1, t + 1)
                    v.scalar_tensor_tensor(out=hout[:, t % 2, :], in0=bank[7][:, 0:N], scalar=Et[:, t % 2, P - 1:P],
                                           in1=hout[:, t % 2, :], op0=ALU.mult, op1=ALU.add).then_inc(s_So, 1)
            v.wait_ge(s_dtk, 1)
            for j in range(2):
                v.tensor_copy(sb_rows[0:NS, j * 512:(j + 1) * 512], bank[2 + j][0:NS, :]).then_inc(s_dcv, 1)
            v.wait_ge(s_dcv, 3)
            eye8 = ident[0:NS, 0:NS].unsqueeze(2).to_broadcast([NS, NS, N])

            def rows_to_diagonal(j, g):
                r = sb_rows[0:NS, j * 512 + g * N:j * 512 + (g + 1) * N].unsqueeze(1).to_broadcast([NS, NS, N])
                v.tensor_tensor(diagm[0:NS, :, :], r, eye8, ALU.mult).then_inc(s_cbp, 1)

            for t in range(XT_TILES):
                g = t // TPG
                if t % TPG == 0:
                    if g >= 1:
                        v.wait_ge(s_op, 2 * t)
                    rows_to_diagonal(1, g)
                    v.wait_ge(s_dtk, 3 + g)
                    v.tensor_tensor(dtx[0:NS, :].rearrange("p (h d) -> p h d", d=HD),
                                    bank[5][0:NS, :].rearrange("p (h d) -> p h d", d=HD),
                                    dt_tok[0:NS, 2, 2 * t:2 * t + 2 * TPG].unsqueeze(2).to_broadcast([NS, 2 * TPG, HD]),
                                    ALU.mult).then_inc(s_dcv, 1)
                    v.wait_ge(s_cbv, g + 1)
                    for q in range(2):
                        link(v.tensor_copy(Cb[:, 4 * q:4 * q + 4, :],
                                           bank[6 + q][:, :].rearrange("p (b n) -> p b n", n=N)))
                    rows_to_diagonal(0, g)
                for q in range(2):
                    u = 2 * t + q
                    st = st_in[:, q, :, :]
                    v.wait_ge(s_stl[q], 16 * (t + 1))
                    link(v.tensor_tensor(st, st, dAe[:, t, 4 * q:4 * q + 4].unsqueeze(2).to_broadcast([P, 4, N]),
                                         ALU.mult))
                    v.wait_ge(s_op, u + 1)
                    v.tensor_tensor(st, st, bank[6 + q][:, :].rearrange("p (b n) -> p b n", n=N),
                                    ALU.add).then_inc(s_h, 1)
                    v.wait_ge(s_h, u + 1)
                    link(v.tensor_tensor(st_y[:, :, :], st, Cb[:, 4 * q:4 * q + 4, :], ALU.mult))
                    v.tensor_reduce(ysum[:, 4 * q:4 * q + 4], st_y[:, :, :], AX, ALU.add).then_inc(s_ys, 1)
                v.wait_ge(s_ys, 2 * t + 2)
                link(v.scalar_tensor_tensor(out=conv_out[:, t, TP:T], in0=conv_out[:, t, TP:T], scalar=d_col[:, t:t + 1],
                                            in1=ysum[:, 0:NS], op0=ALU.mult, op1=ALU.add))
            v.wait_ge(s_zs, 1)
            for t in range(XT_TILES):
                v.tensor_tensor(conv_out[:, t, :], conv_out[:, t, :], zT[:, t, :], ALU.mult).then_inc(s_g, 1)
            v.wait_ge(s_gs, 1)
            link(v.tensor_copy(ss[:, 0:2], bank[2][:, 0:2]))
            link(v.tensor_copy(ss[0:NS, 2:3], bank[2][0:NS, 2:3]))
            v.tensor_scalar(ss[:, 0:3], ss[:, 0:3], 1.0 / DI, EPS, ALU.mult, ALU.add).then_inc(s_gs, 1)
            v.wait_ge(s_gq, 2)
            link(v.reciprocal(rstd[:, 0:3], rstd[:, 0:3]))
            for t, r in enumerate(ROWS):
                for q in range(2):
                    v.wait_ge(s_ot, 2 * t + q + 1)
                    xs = X[0:r, t, 512 * q:512 * q + 512]
                    v.scalar_tensor_tensor(out=xs, in0=bank[3 + q][0:r, :], scalar=rstd[0:r, t:t + 1], in1=xs,
                                           op0=ALU.mult, op1=ALU.add).then_inc(s_xa, 1)
            norm(1, xn_e, gffn(0))
            moe(0)

            norm(2, xn_a, gmix(1))
            v.wait_ge(s_const, 9)
            v.tensor_copy(mask[:, 0, 0:1], mask[:, 0, 0:1]).then_inc(a_mv, 1)
            dist = pT[:, 0, 0, :, :].rearrange("p a b -> p (a b)")
            rest = pT[:, 0, 1, :, :].rearrange("p a b -> p (a b)")
            for g in range(1, NGRP):
                link(v.tensor_scalar(rest.bitcast(I32), dist.bitcast(I32), PATTERNS[g][1] - 1, None, ALU.bitwise_and))
                link(v.tensor_copy(sm[:, 0, 0, :], rest.bitcast(I32)))
                link(v.tensor_scalar(sm[:, 0, 0, :], sm[:, 0, 0, :], 0.0, NEG, ALU.not_equal, ALU.mult))
                v.tensor_tensor(mask[:, g, :], mask[:, g, :], sm[:, 0, 0, :], ALU.min).then_inc(a_mv, 1)
            v.wait_ge(a_mv, 3)
            link(v.tensor_tensor(fold[:, :], ident[:, 0:HD], ident[:, HD:P], ALU.add))

            def own_scores(g):
                v.wait_ge(q_e, 24 * (g + 1))
                v.tensor_tensor(prod[:, g, :].rearrange("p (t b) -> p t b", b=NS), qT[:, :, TP:T], kT[:, :, TP:T],
                                ALU.mult).then_inc(c_v, 1)

            def masked(g, t):
                n = DT * g + t
                hs = slice(2 * t, 2 * t + 2)
                s_ = sm[:, t % 2, :, :]
                if n >= 2:
                    v.wait_ge(h_t, 2 * n - 2)
                for h in range(2):
                    v.wait_ge(h_s, 2 * n + h + 1)
                    v.scalar_tensor_tensor(out=s_[:, h, :], in0=bank[2 + h][:, 0:3 * P], scalar=SCALE,
                                           in1=mask[:, g, :], op0=ALU.mult, op1=ALU.add).then_inc(h_m, 1)
                v.wait_ge(h_m, 2 * n + 2)
                dst = rs if g else M_
                link(v.tensor_reduce(dst[:, 0, hs], s_[:, :, 0:P], AX, ALU.max))
                link(v.tensor_reduce(dst[:, 1, hs], s_[:, :, P:3 * P], AX, ALU.max))
                if g:
                    link(v.tensor_tensor(rs[:, :, hs], rs[:, :, hs], M_[:, :, hs], ALU.max))
                    link(v.tensor_tensor(al[:, :, hs], M_[:, :, hs], rs[:, :, hs], ALU.subtract))
                    link(v.tensor_copy(M_[:, :, hs], rs[:, :, hs]))
                v.tensor_scalar(Mn[:, :, hs], M_[:, :, hs], -1.0, None, ALU.mult).then_inc(h_x, 1)

            def taken_up(g, t):
                n = DT * g + t
                hs = slice(2 * t, 2 * t + 2)
                v.wait_ge(h_e, 4 * n + 4)
                v.wait_ge(h_v, n + 1)
                o = O[:, :, 2 * t * HD:(2 * t + 2) * HD].rearrange("p i (h d) -> p i h d", d=HD)
                new = bank[6][:, 0:4 * HD].rearrange("p (i h d) -> p i h d", i=2, h=2)
                if g == 0:
                    link(v.tensor_copy(L_[:, :, hs], rs[:, :, hs]))
                    v.tensor_copy(o, new).then_inc(h_o, 1)
                    return
                link(v.tensor_tensor(L_[:, :, hs], L_[:, :, hs], al[:, :, hs], ALU.mult))
                link(v.tensor_tensor(L_[:, :, hs], L_[:, :, hs], rs[:, :, hs], ALU.add))
                link(v.tensor_tensor(o, o, al[:, :, hs].unsqueeze(3).to_broadcast([P, 2, 2, HD]), ALU.mult))
                v.tensor_tensor(o, o, new, ALU.add).then_inc(h_o, 1)

            def cache_scores(g, u):
                b, q = u // 2, u % 2
                n, k = 16 * g + u, NS * g + b
                r = KEYS[g]
                if q == 0:
                    v.wait_ge(k_l[k % 2], 16 * (k // 2 + 1))
                v.wait_ge(k_q, n + 1)
                kk = K_in[0:r, k % 2, 512 * q:512 * q + 512]
                v.tensor_tensor(kk, kk, bank[2 + q][0:r, :], ALU.mult).then_inc(k_m, 1)
                if q:
                    v.wait_ge(k_m, n + 1)
                    out = S_s[0:r, g, :].rearrange("p (h t b) -> p t h b", h=2, t=DT)[:, :, :, b]
                    v.tensor_reduce(out, K_in[0:r, k % 2, :].rearrange("p (t h d) -> p t h d", h=2, d=HD),
                                    AX, ALU.add).then_inc(k_r, 1)

            for g in range(NGRP):
                if g >= 1:
                    for u in range(16):
                        cache_scores(g - 1, u)
                for t in range(DT + 2):
                    if t < DT:
                        masked(g, t)
                    if t >= 2:
                        taken_up(g, t - 2)
                own_scores(g)
            for u in range(16):
                cache_scores(NGRP - 1, u)
            link(v.reciprocal(L_[:, :, :], L_[:, :, :]))
            for c in range(2):
                o = O[:, c, :].rearrange("p (h d) -> p h d", d=HD)
                v.tensor_tensor(o, o, bc(L_[:, c, :].unsqueeze(2), AH, HD), ALU.mult).then_inc(o_n, 1)
            v.wait_ge(c_p, 1)
            v.wait_ge(k_r, NS * NGRP)
            v.tensor_copy(same[:, :], bank[7][:, 0:P]).then_inc(c_v, 1)
            n_keys = sum(KEYS) + NGRP
            v.wait_ge(c_p, 2)
            link(v.tensor_reduce(s_st[:, 0:1], bank[7][:, 0:n_keys], AX, ALU.max))
            v.tensor_scalar(s_st[:, 1:2], s_st[:, 0:1], -SCALE, None, ALU.mult).then_inc(c_v, 1)
            v.wait_ge(c_a, 1)
            link(v.reciprocal(s_st[:, 3:4], s_st[:, 2:3]))
            v.tensor_scalar(p_s[:, 0:n_keys], p_s[:, 0:n_keys], s_st[:, 3:4], None, ALU.mult).then_inc(c_v, 1)
            v.wait_ge(c_v, NGRP + 3)
            for g in range(NGRP):
                v.tensor_scalar(PHp[:, g, :], same[:, :], p_s[:, sum(KEYS) + g:sum(KEYS) + g + 1], None,
                                ALU.mult).then_inc(c_v, 1)
            v.wait_ge(c_p, 3)
            v.wait_ge(q_vs, DT * NGRP)
            link(v.tensor_tensor(y_s1[:, :, :], bank[2][:, 0:NGRP * DT * NS].rearrange("p (g c) -> p g c", g=NGRP),
                                 vTs[:, :, :], ALU.mult))
            link(v.tensor_tensor(y_s2, y_s1[:, 0, :], y_s1[:, 1, :], ALU.add))
            link(v.tensor_tensor(y_s2, y_s2, y_s1[:, 2, :], ALU.add))
            v.wait_ge(v_p, NS)
            for h in range(2):
                r = slice(h * HD, (h + 1) * HD)
                got = bank[4][r, 0:2 * DT * NS].rearrange("p (b t h) -> p t b h", b=NS, h=2)[:, :, :, h]
                v.tensor_tensor(yT[r, :, TP:T], got, y_s2[r, :].rearrange("p (t b) -> p t b", b=NS),
                                ALU.add).then_inc(c_v, 1)
            for t, r in enumerate(ROWS):
                for q in range(2):
                    v.wait_ge(s_ot, 6 + 2 * t + q + 1)
                    xs = X[0:r, t, 512 * q:512 * q + 512]
                    v.tensor_tensor(xs, xs, bank[3 + q][0:r, :], ALU.add).then_inc(s_xa, 1)
            norm(3, xn_e, gffn(1))
            moe(1)
            v.wait_ge(n_ss, 15)
            v.tensor_scalar(ss[:, 0:3], ss[:, 0:3], 1.0 / D, EPS, ALU.mult, ALU.add).then_inc(n_var, 1)
            v.wait_ge(n_std, 5)
            link(v.reciprocal(rstd[:, 0:3], rstd[:, 0:3]))
            v.wait_ge(s_vld, 144)
            for t, r in enumerate(ROWS):
                v.scalar_tensor_tensor(out=X[0:r, t, :], in0=X[0:r, t, :], scalar=rstd[0:r, t:t + 1],
                                       in1=gfin[0:r, :], op0=ALU.mult, op1=ALU.mult).then_inc(s_fin, 1)


INS = ["x_prompt", "x_sample", "state_conv", "state_ssm", "cache_kv_w128", "cache_kv_w512", "cache_kv_w2048",
       "norm_mix", "norm_ffn", "norm_final", "ssm_in_proj", "ssm_conv_w", "ssm_conv_b", "ssm_dt_bias", "ssm_a_log",
       "ssm_d", "ssm_norm", "ssm_out_proj", "attn_qkv", "attn_out", "moe_route_group", "moe_route_expert",
       "moe_w_gate_up", "moe_w_down"]
OUTS = [(1, TP, D), (NS, 1, D), (1, 1, PADW, CD), (1, NS, PADW, CD), (1, 1, SH, HD, N), (1, NS, SH, HD, N),
        (1, 1, 128, 2, AH, HD), (1, NS, 1, 2, AH, HD), (1, 1, TP, 2, AH, HD), (1, NS, 1, 2, AH, HD),
        (1, 1, TP, 2, AH, HD), (1, NS, 1, 2, AH, HD)]


def kernel(**inputs):
    import numpy as np
    import concourse.bacc as bacc
    from concourse.bass_utils import run_bass_kernel_spmd

    nc = bacc.Bacc("TRN2", target_bir_lowering=False, num_devices=1)
    arrays, handles = {}, {}
    for name in INS:
        v = np.ascontiguousarray(inputs[name])
        arrays[f"in_{name}"] = v
        handles[name] = nc.dram_tensor(f"in_{name}", v.shape, mybir.dt.from_np(v.dtype), kind="ExternalInput").ap()
    outs = [nc.dram_tensor(f"out_{i}", s, F32, kind="ExternalOutput").ap() for i, s in enumerate(OUTS)]
    bass_hybrid_step(nc, handles, outs)
    r = run_bass_kernel_spmd(nc, [arrays], core_ids=[0])
    return tuple(r.results[0][f"out_{i}"] for i in range(len(OUTS)))
```

```python
from contextlib import ExitStack

import concourse.bass as bass
from concourse import mybir

ALU = mybir.AluOpType
ACT = mybir.ActivationFunctionType
F32 = mybir.dt.float32
I32 = mybir.dt.int32
AX = mybir.AxisListType.X

P = 128
D = 1024
DT = D // P
TP = 256
NS = 8
T = TP + NS
ROWS = (P, P, NS)
EPS = 1e-6

DI = 2 * D
HD = 64
SH = DI // HD
SG = 4
N = 128
CD = DI + 2 * SG * N
CW = 4
CT = CD // P
XT_TILES = DI // P
TPG = XT_TILES // SG
IN_DIM = DI + CD + SH
PADW = CW - 1
SAMP0 = PADW + TP
RAW = SAMP0 + CW * NS
CONV = RAW - PADW
RAWS = 8
STATES = 3

AH = 16
PATTERNS = ((128, 1), (512, 4), (2048, 16))
PAST = 1024
NGRP = len(PATTERNS)
KEYS = [min(w, PAST) // dil for w, dil in PATTERNS]
SCALE = HD ** -0.5
NEG = -1.0e30

EG = 4
EPG = 8
NE = EG * EPG
DE = 512
SLOTS = 64
ROUNDS = -(-T // SLOTS)
BIG = 1.0e30
RC = ROUNDS * NE + 2
PAIRS = NE // 2

CH = 4096
RING = 6
SSM_CHUNKS = (IN_DIM - SH) // 512 + DI * D // (P * CH)
ATT_CHUNKS = NGRP * 3 * D // 512 + D * D // (P * CH)
STREAM_SLOT = (0, (SSM_CHUNKS + 3 * NE) % RING)
MOE_SLOT = (SSM_CHUNKS % RING, (STREAM_SLOT[1] + ATT_CHUNKS) % RING)


def bass_hybrid_step(nc, a, outs):
    (y_p, y_s, conv_p, conv_s, ssm_p, ssm_s, kv0_p, kv0_s, kv1_p, kv1_s, kv2_p, kv2_s) = outs
    kv_p = (kv0_p, kv1_p, kv2_p)
    kv_s = (kv0_s, kv1_s, kv2_s)
    caches = (a["cache_kv_w128"], a["cache_kv_w512"], a["cache_kv_w2048"])

    with ExitStack() as ctx:
        ctx.enter_context(nc.allow_non_contiguous_dma("short per-head vectors"))

        def sb(name, shape, dt=F32):
            return ctx.enter_context(nc.sbuf_tensor(name, shape, dt))

        def sem(name):
            return ctx.enter_context(nc.semaphore(name))

        ring = sb("ring", [P, RING, CH])
        X = sb("X", [P, 3, D])
        hT = sb("hT", [P, DT, T])
        ident = sb("ident", [P, P])
        upper = sb("upper", [P, P])
        strict = sb("strict", [P, P])
        ones = sb("ones", [P, P])
        half = sb("half", [2, P])
        vcol = sb("vcol", [P, 72])
        cwcol = sb("cwcol", [P, CW * CT])
        slot_no = sb("slot_no", [P, SLOTS])
        first4 = sb("first4", [P, EG])
        first8 = sb("first8", [P, EPG])
        thresh = sb("thresh", [1, 8])
        ss = sb("ss", [P, 4])
        rstd = sb("rstd", [P, 4])
        rounds_i = sb("rounds_i", [1, 2], I32)
        ARENA = 22330
        arena = sb("arena", [P, ARENA])
        bank = [ctx.enter_context(nc.psum_tensor(f"bank{i}", [P, 512], F32)) for i in range(8)]

        class Area:

            def __init__(self, at=0):
                self.at = at

            def __call__(self, *shape):
                n = 1
                for s in shape:
                    n *= s
                v = arena[:, self.at:self.at + n]
                self.at += n
                assert self.at <= ARENA, self.at
                if len(shape) == 2:
                    return v.rearrange("p (a b) -> p a b", b=shape[1])
                if len(shape) == 3:
                    return v.rearrange("p (a b c) -> p a b c", b=shape[1], c=shape[2])
                if len(shape) == 4:
                    return v.rearrange("p (a b c d) -> p a b c d", b=shape[1], c=shape[2], d=shape[3])
                return v

        def gmix(i):
            return vcol[:, DT * i:DT * i + DT]

        def gffn(i):
            return vcol[:, 16 + DT * i:16 + DT * i + DT]

        gssm = vcol[:, 32:48]
        cbcol = vcol[:, 48:72]

        m = Area()
        conv_out = m(CT, T)
        zT = m(XT_TILES, T)
        dtT = m(T)
        dAT = m(T)
        dt_tok = m(3, SH)
        dA_tok = m(3, SH)
        cs_tok = m(2, SH)
        w_tok = m(2, SH)
        b_tok = m(2, SG * N)
        d_col = m(16)
        head_v = m(8)
        d_row = m(16)
        dAe = m(XT_TILES, NS)
        ysum = m(T)
        after_vec = m.at
        raws = m(RAWS, RAW)
        cacc = m(2, CONV)
        stT = m(CT, CW * NS - NS)
        newc = m(CT, 3 + NS)
        newr = m(2, 512)
        spt = m(6, T)
        conv_end = m.at
        m = Area(after_vec)
        xdt = m(2, TPG * P)
        xw = m(2, TPG * P)
        seg = m(2, 512)
        cbm = m(3, P)
        Et = m(2, P)
        y1 = m(2, P)
        hout = m(2, P)
        st_in = m(STATES, NS, N)
        st_y = m(NS, N)
        dtx = m(2, TPG * P)
        m = Area(after_vec)
        sb_rows = m(2 * SG * N)
        diagC = m(NS, N)
        diagB = m(NS, N)
        Cb = m(NS, N)
        m = Area(conv_end)
        dtw = m(DT, SH)
        vrow = m(P)
        cwrow = m(P)
        m = Area(0)
        xn_m = m(3, D)
        csr = m(CD)

        m = Area()
        xn_e = m(3, D)
        accT = m(DT, T)
        Xg = m(DT, P)
        Pm = m(3, 2, SLOTS)
        Cm = m(3, 2, SLOTS)
        CmT = m(T)
        sg = m(DE)
        act_r = m(DE)
        actT = m(4, P)
        ysl = m(DT, P)
        rk = m(3, RC)
        cc = m(3, RC)
        wr = m(DT, EG + NE)
        lg = m(3, EG + NE)
        g_a, g_b, g_oh = m(3, EG), m(3, EG), m(3, EG)
        g_s = m(8, 3)
        e_w = m(3, EG, EPG)
        es, e_a, oh1, oh2, e_sel, e_in = (m(3, EPG) for _ in range(6))
        msk, cmb, rnk = m(3, NE), m(3, NE), m(3, NE)
        cnt_s = m(8)
        gfin = m(D)

        m = Area()
        qT = m(DT, T)
        kT = m(DT, T)
        yT = qT
        V_in = Area(m.at)(2, NGRP, D)
        KV = m(2, 2, D)
        vT = m(4, T)
        sm = m(2, 2, 3 * P)
        pT = m(2, 2, 3, P)
        assert m.at >= 2 * DT * T + 2 * NGRP * D
        O = m(2, D)
        mask = m(NGRP, 3 * P)
        K_in = m(2, D)
        q_s = m(D)
        kv_s_rows = m(2 * D)
        S_s = m(NGRP, P)
        prod = m(NGRP, DT * NS)
        vTs = m(NGRP, DT * NS)
        O_st = m(5, 2, AH)
        M_, Mn, L_, al, rs = (O_st[:, i, :, :] for i in range(5))
        xn_a = Area(3 * D + DT * T)(3, D)
        fold = sb("fold", [P, DT * NS])
        s_st = sb("s_st", [P, 8])
        quarter = sb("quarter", [P, 4])
        own_head = mask.rearrange("p g k -> p (g k)")[:, 0:512]
        y_own = mask.rearrange("p g k -> p (g k)")[:, 512:1024]
        p_s = K_in.rearrange("p a n -> p (a n)")[:, 0:384]
        pTs = K_in.rearrange("p a n -> p (a n)")[:, 384:768].rearrange("p (g c) -> p g c", g=NGRP)
        PHp = K_in.rearrange("p a n -> p (a n)")[:, 768:1152].rearrange("p (g c) -> p g c", g=NGRP)
        y_s1 = K_in.rearrange("p a n -> p (a n)")[:, 1152:1344].rearrange("p (g c) -> p g c", g=NGRP)
        y_s2 = K_in.rearrange("p a n -> p (a n)")[:, 1344:1408]
        same = K_in.rearrange("p a n -> p (a n)")[:, 1408:1536]

        loads = [[sem(f"weights{l}_landed{i}") for i in range(RING)] for l in range(2)]
        s_ld = loads[0]
        s_xld = sem("x_landed")
        s_vld = sem("vectors_landed")
        s_dtld = sem("dt_weights_landed")
        s_const = sem("constants_made")
        s_chain = sem("vector_step")
        s_achain = sem("scalar_step")
        s_pchain = sem("pool_step")
        s_pvec = sem("pe_vectors")
        s_vvec = sem("vectors_ready")
        s_out = sem("outputs_stored")
        s_pout = sem("old_conv_rows_moved")
        n_ss = sem("norm_squares")
        n_var = sem("norm_var")
        n_std = sem("norm_std")
        n_xn = sem("norm_rows")
        n_tp = sem("norm_transposed")
        n_ht = sem("norm_ready")
        s_stp = sem("conv_state_transposed")
        s_stc = sem("conv_state_columns")
        s_dtp = sem("dt_projected")
        s_dtz = sem("dt_biased")
        s_dte = sem("dt_exp")
        s_dt = sem("dt_ready")
        s_prj = sem("tile_projected")
        s_raw = sem("raw_ready")
        s_rst = sem("raw_state_ready")
        s_cv = sem("convolved")
        s_cx = sem("conv_activated")
        s_nc = sem("new_conv_columns")
        s_ntp = sem("new_conv_transposed")
        s_nrw = sem("new_conv_rows")
        s_nst = [sem(f"new_conv_stored{i}") for i in range(2)]
        s_tk = sem("scan_tokens_pe")
        s_tkv = sem("scan_tokens_ready")
        s_xtp = sem("x_transposed")
        s_xdt = sem("xdt_ready")
        s_cb = sem("cb_products")
        s_cbm = sem("cb_masked")
        s_csb = sem("cs_broadcast")
        s_seg = sem("segments")
        s_dec = sem("decays")
        s_M = sem("scores_ready")
        s_yp = sem("scan_products")
        s_E = sem("offset_decay")
        s_y = sem("scan_rows")
        s_Sp = sem("state_products")
        s_S1 = sem("state_copied")
        s_So = sem("state_ready")
        s_Sst = [sem(f"state_stored{i}") for i in range(2)]
        s_dtk = sem("decode_rows_pe")
        s_dcv = sem("decode_rows_ready")
        s_cbp = sem("decode_diagonals")
        s_cbv = sem("decode_c_everywhere")
        s_cbc = sem("decode_c_ready")
        s_op = sem("decode_outer")
        s_stl = [sem(f"decode_state_landed{i}") for i in range(STATES)]
        s_h = sem("decode_state_new")
        s_hst = [sem(f"decode_state_stored{i}") for i in range(STATES)]
        s_ys = sem("decode_rows_summed")
        s_zp = sem("z_projected")
        s_zc = sem("z_activated")
        s_g = sem("gated")
        s_gq = sem("gated_squares")
        s_gs = sem("gated_sum_pe")
        s_gn = sem("gated_scaled")
        s_op2 = sem("out_projected")
        s_oc = sem("out_copied")
        s_ot = sem("out_transposed")
        s_xa = sem("residual_added")
        m_wr = sem("router_weights_landed")
        m_lg = sem("logits_projected")
        m_ge = sem("router_exponents")
        m_ex = sem("router_exps")
        m_mk = sem("token_masks")
        m_rk = sem("token_ranks")
        m_R = sem("rounds_known")

        class Moe:

            def __init__(self, l):
                self.peq = sem(f"slots_built{l}")
                self.cm = sem(f"shares_built{l}")
                self.ga = sem(f"tokens_gathered{l}")
                self.xg = sem(f"tokens_ready{l}")
                self.gu = sem(f"gate_or_up_done{l}")
                self.sg = sem(f"silu_done{l}")
                self.act = sem(f"act_ready{l}")
                self.tp = sem(f"act_transposed{l}")
                self.at = sem(f"act_columns_ready{l}")
                self.cp = sem(f"shares_transposed{l}")
                self.cpt = sem(f"shares_copied{l}")
                self.dh = sem(f"down_half_done{l}")
                self.dn = sem(f"down_done{l}")
                self.y = sem(f"result_rows_ready{l}")
                self.sc = sem(f"results_scattered{l}")
                self.acc = sem(f"results_added{l}")

        moes = [Moe(0), Moe(1)]

        a_mv = sem("masks_ready")
        q_p = sem("qkv_projected")
        q_e = sem("qkv_copied")
        q_vs = sem("sample_v_copied")
        kv_t = sem("kv_rows_transposed")
        kv_e = sem("kv_rows_copied")
        kvst = sem("kv_stored")
        h_s = sem("head_scores")
        h_m = sem("head_masked")
        h_x = sem("head_maxima")
        h_e = sem("head_exps")
        h_t = sem("head_transposed")
        h_c = sem("head_probs_copied")
        h_v = sem("head_values")
        h_o = sem("head_output")
        k_l = [sem(f"cache_keys_landed{i}") for i in range(2)]
        k_q = sem("cache_query_broadcast")
        k_m = sem("cache_products")
        k_r = sem("cache_scores")
        c_p = sem("sample_softmax_pe")
        c_v = sem("sample_softmax_vector")
        c_a = sem("sample_softmax_scalar")
        v_l = [sem(f"cache_values_landed{i}") for i in range(2)]
        v_p = sem("cache_values_summed")
        y_o = sem("own_channels_masked")
        o_n = sem("rows_divided")
        o_t = sem("rows_transposed")
        o_c = sem("rows_copied")

        block = ctx.enter_context(nc.Block())

        w_in = a["ssm_in_proj"][0].rearrange("(k p) n -> p k n", p=P)
        w_out = a["ssm_out_proj"][0].rearrange("(k p) n -> p k n", p=P)

        in_cols = [2 * DI, 2 * DI + 512] + [DI + 512 * i for i in range(4)] + [512 * i for i in range(4)]
        tile_order = [16 + i for i in range(8)] + list(range(16))

        def cache_rows(g, b, kv):
            w, dil = PATTERNS[g]
            return caches[g][0, b, :, kv].rearrange("(n s) h d -> s n (h d)", s=dil)[0]

        def wait_chunk(eng, n):
            eng.wait_ge(s_ld[n % RING], 16 * (n // RING + 1))

        @block.sync
        def _(sp):
            def chunk_used(n):
                if n < 6:
                    sp.wait_ge(s_prj, 4 * (n + 1))
                else:
                    sp.wait_ge(s_zp, 4 * (n - 5))

            def values_in():
                sp.wait_ge(h_o, DT * NGRP)
                sp.wait_ge(kvst, 32 * NGRP)
                for b in range(NS):
                    if b >= 2:
                        sp.wait_ge(v_p, b - 1)
                    for g in range(NGRP):
                        sp.dma_start(V_in[0:KEYS[g], b % 2, g, :], cache_rows(g, b, 1)).then_inc(v_l[b % 2], 16)

            def moe_stream(l):
                s = moes[l]
                gu = a["moe_w_gate_up"][l].rearrange("g e (k p) n -> (g e) p k n", p=P)
                dn = a["moe_w_down"][l].rearrange("g e (k p) n -> (g e) p k n", p=P)

                def chunk(j, pair, e):
                    slot = (MOE_SLOT[l] + j) % RING
                    half = slice((j // 2) * DE, (j // 2 + 1) * DE)
                    if j < 4:
                        sp.wait_ge(s.gu, pair * 2 + (j // 2 + 1))
                        src = gu[bass.ds(e + j % 2, 1), :, :, half]
                    else:
                        sp.wait_ge(s.dn, pair * 2 + (j - 3))
                        src = dn[bass.ds(e + (j - 4), 1)]
                    dst = ring[:, slot, :].rearrange("p (k n) -> p k n", n=src.shape[3])
                    sp.dma_start(dst, src.rearrange("o p k n -> (o p) k n")).then_inc(loads[l][slot], 16)

                for j in range(6):
                    if l == 1 and j == 4:
                        values_in()
                    chunk(j, 0, 0)
                sp.wait_ge(m_R, l + 1)
                rounds = sp.value_load(rounds_i[0:1, 0:1], min_val=1, max_val=ROUNDS)
                with sp.Fori(0, rounds) as r:
                    with sp.Fori(1, PAIRS) as q:
                        for j in range(6):
                            chunk(j, r * PAIRS + q, q * 2)
                    with sp.If(r + 1 < rounds):
                        for j in range(6):
                            chunk(j, r * PAIRS + PAIRS, 0)
                    sp.nop()
                return rounds

            sp.dma_start(X[:, 0:2, :], a["x_prompt"][0].rearrange("(t p) d -> p t d", p=P)).then_inc(s_xld, 16)
            sp.dma_start(X[0:NS, 2, :], a["x_sample"].rearrange("b s d -> (b s) d")).then_inc(s_xld, 16)
            sp.dma_start(dtw[:, :, :], w_in[:, :, IN_DIM - SH:IN_DIM]).then_inc(s_dtld, 16)

            def states_in(t):
                if t == 0:
                    sp.wait_ge(s_y, 1)
                if t >= STATES:
                    sp.wait_ge(s_hst[t % STATES], 16 * (t // STATES))
                    sp.wait_ge(s_ys, t - STATES + 1)
                sp.dma_start(st_in[:, t % STATES, :, :], a["state_ssm"][0, :, 2 * t:2 * t + 2].rearrange(
                    "b h p n -> (h p) b n")).then_inc(s_stl[t % STATES], 16)

            for n in range(SSM_CHUNKS):
                if n >= 12:
                    for t in (range(0, 5) if n == 12 else range(5, 9)):
                        states_in(t)
                if n == 0:
                    sp.wait_ge(s_xld, 32)
                if n >= RING:
                    chunk_used(n - RING)
                if n < 10:
                    c = in_cols[n]
                    src = w_in[:, :, c:c + 512]
                    dst = ring[:, n % RING, :].rearrange("p (k n) -> p k n", k=DT)
                else:
                    c = (n - 10) * 256
                    src = w_out[:, :, c:c + 256]
                    dst = ring[:, n % RING, :].rearrange("p (k n) -> p k n", k=16)
                sp.dma_start(dst, src).then_inc(s_ld[n % RING], 16)
            for t in range(9, XT_TILES):
                states_in(t)
            rounds = moe_stream(0)
            qkv = a["attn_qkv"][0].rearrange("(k p) n -> p k n", p=P)
            wo = a["attn_out"][0].rearrange("(k p) n -> p k n", p=P)
            for n in range(ATT_CHUNKS):
                slot = (STREAM_SLOT[1] + n) % RING
                if n < RING:
                    free = moes[0].gu if n < 4 else moes[0].dn
                    sp.wait_ge(free, rounds * NE + 1 + (n // 2 if n < 4 else n - 4))
                else:
                    sp.wait_ge(q_p, 4 * (n - RING + 1))
                if n < ATT_CHUNKS - 2:
                    g, j = n // 6, n % 6
                    c = (3 * g + 2 - j // 2) * D + (j % 2) * 512
                    src = qkv[:, :, c:c + 512]
                else:
                    c = (n - ATT_CHUNKS + 2) * 512
                    src = wo[:, :, c:c + 512]
                sp.dma_start(ring[:, slot, :].rearrange("p (k n) -> p k n", k=DT), src).then_inc(loads[1][slot], 16)
            moe_stream(1)
            sp.dma_start(gfin[:, :], a["norm_final"].rearrange("(o d) -> o d", o=1).to_broadcast([P, D])
                         ).then_inc(s_vld, 16)
            sp.wait_ge(n_xn, 15)
            sp.dma_start(y_p[0].rearrange("(t p) d -> p t d", p=P), X[:, 0:2, :]).then_inc(s_out, 16)
            sp.dma_start(y_s.rearrange("b s d -> (b s) d"), X[0:NS, 2, :]).then_inc(s_out, 16)
            sp.wait_ge(s_out, 32)

        @block.gpsimd
        def _(pool):
            steps = [0]

            def link(ins):
                steps[0] += 1
                ins.then_inc(s_pchain, 1)
                pool.wait_ge(s_pchain, steps[0])

            def router_weights(l):
                pool.wait_ge(s_xa, 12 * l + 6)
                pool.dma_start(wr[:, :, 0:EG],
                               a["moe_route_group"][l].rearrange("(k p) g -> p k g", p=P)).then_inc(m_wr, 16)
                for g in range(EG):
                    pool.dma_start(wr[:, :, EG + EPG * g:EG + EPG * (g + 1)],
                                   a["moe_route_expert"][l, g].rearrange("(k p) e -> p k e", p=P)).then_inc(m_wr, 16)

            pool.dma_start(conv_s[0, :, 0:2, :].rearrange("b w c -> b (w c)"),
                           a["state_conv"][0, :, 1:3, :].rearrange("b w c -> b (w c)")).then_inc(s_pout, 16)
            link(pool.memset(ones[:, :], 1.0))
            pool.affine_select(out=ident[:, :], in_=ones[:, :], compare_op=ALU.is_equal, fill=0.0, base=0,
                               pattern=[[-1, P]], channel_multiplier=1).then_inc(s_const, 1)
            pool.affine_select(out=upper[:, :], in_=ones[:, :], compare_op=ALU.is_ge, fill=0.0, base=0,
                               pattern=[[1, P]], channel_multiplier=-1).then_inc(s_const, 1)
            pool.affine_select(out=strict[:, :], in_=ones[:, :], compare_op=ALU.is_gt, fill=0.0, base=0,
                               pattern=[[1, P]], channel_multiplier=-1).then_inc(s_const, 1)
            link(pool.affine_select(out=half[:, :], in_=ones[0:2, :], compare_op=ALU.is_ge, fill=0.0, base=0,
                                    pattern=[[1, P]], channel_multiplier=-HD))
            pool.affine_select(out=half[:, :], in_=half[:, :], compare_op=ALU.is_ge, fill=0.0, base=HD - 1,
                               pattern=[[-1, P]], channel_multiplier=HD).then_inc(s_const, 1)
            pool.iota(slot_no[:, :], [[1, SLOTS]], base=0, channel_multiplier=0,
                      allow_small_or_imprecise_dtypes=True).then_inc(s_const, 1)
            pool.iota(first4[:, :], [[-1, EG]], base=EG, channel_multiplier=0,
                      allow_small_or_imprecise_dtypes=True).then_inc(s_const, 1)
            pool.iota(first8[:, :], [[-1, EPG]], base=EPG, channel_multiplier=0,
                      allow_small_or_imprecise_dtypes=True).then_inc(s_const, 1)
            pool.iota(thresh[:, :], [[SLOTS, 8]], base=0, channel_multiplier=0,
                      allow_small_or_imprecise_dtypes=True).then_inc(s_const, 1)

            for i, ct in enumerate(tile_order):
                if i == 0:
                    pool.wait_ge(s_stc, 3)
                if i >= RAWS:
                    pool.wait_ge(s_cv, i - RAWS + 1)
                old = raws[:, i % RAWS, SAMP0:RAW].rearrange("p (b w) -> p b w", w=CW)[:, :, 0:PADW]
                pool.tensor_copy(old, stT[:, ct, :].rearrange("p (b w) -> p b w", w=PADW)).then_inc(s_rst, 1)
                pool.wait_ge(s_raw, 2 * i + 2)
                new = raws[:, i % RAWS, SAMP0:RAW].rearrange("p (b w) -> p b w", w=CW)[:, :, PADW]
                pool.tensor_copy(newc[:, ct, 0:PADW], raws[:, i % RAWS, TP:TP + PADW]).then_inc(s_nc, 1)
                pool.tensor_copy(newc[:, ct, PADW:PADW + NS], new).then_inc(s_nc, 1)
            for q in range(CT // 4):
                pool.wait_ge(s_nrw, q + 1)
                pool.dma_start(conv_p[0, 0, :, 512 * q:512 * q + 512], newr[0:3, q % 2, :]).then_inc(s_nst[q % 2], 16)
                pool.dma_start(conv_s[0, :, 2, 512 * q:512 * q + 512], newr[3:11, q % 2, :]).then_inc(s_nst[q % 2], 16)

            for t in range(XT_TILES):
                pool.wait_ge(s_So, t + 1)
                pool.dma_start(ssm_p[0, 0, 2 * t:2 * t + 2].rearrange("h p n -> (h p) n"),
                               hout[:, t % 2, :]).then_inc(s_Sst[t % 2], 16)
            for i in range(2):
                pool.wait_ge(s_Sst[i], 16 * XT_TILES // 2)

            eye8 = ident[0:NS, 0:NS].unsqueeze(2).to_broadcast([NS, NS, N])

            def rows_to_diagonal(out, j, g):
                r = sb_rows[0:NS, j * 512 + g * N:j * 512 + (g + 1) * N].unsqueeze(1).to_broadcast([NS, NS, N])
                pool.tensor_tensor(out[0:NS, :, :], r, eye8, ALU.mult).then_inc(s_cbp, 1)

            pool.wait_ge(s_dcv, 3)
            rows_to_diagonal(diagC, 1, 0)
            rows_to_diagonal(diagB, 0, 0)
            for t in range(XT_TILES):
                g = t // TPG + 1
                if t % TPG == 0 and g < SG:
                    pool.wait_ge(s_cbv, g)
                    rows_to_diagonal(diagC, 1, g)
                if t % TPG == TPG - 1 and g < SG:
                    pool.wait_ge(s_op, 2 * TPG * g)
                    rows_to_diagonal(diagB, 0, g)
                pool.wait_ge(s_h, 2 * t + 2)
                pool.dma_start(ssm_s[0, :, 2 * t:2 * t + 2].rearrange("b h p n -> (h p) b n"),
                               st_in[:, t % STATES, :, :]).then_inc(s_hst[t % STATES], 16)
            pool.wait_ge(s_pout, 16)
            for i in range(2):
                pool.wait_ge(s_nst[i], 16 * CT // 4)
            for i in range(STATES):
                pool.wait_ge(s_hst[i], 16 * len(range(i, XT_TILES, STATES)))

            router_weights(0)

            pool.wait_ge(s_xa, 12)
            for g in range(NGRP):
                link(pool.memset(mask[:, g, :], 0.0))
                for c0, c1, base in ((0, P, 0), (P, 3 * P, P)):
                    v_ = mask[:, g, c0:c1]
                    link(pool.affine_select(out=v_, in_=v_, compare_op=ALU.is_ge, fill=NEG, base=base,
                                            pattern=[[-1, c1 - c0]], channel_multiplier=1))
                    if g == 0:
                        link(pool.affine_select(out=v_, in_=v_, compare_op=ALU.is_ge, fill=NEG, base=P - base,
                                                pattern=[[1, c1 - c0]], channel_multiplier=-1))
            pool.iota(pT[:, 0, 0, :, :].rearrange("p a b -> p (a b)").bitcast(I32), [[-1, 3 * P]], base=4 * P,
                      channel_multiplier=1).then_inc(s_const, 1)

            def keys_of(g):
                for b in range(NS):
                    u = NS * g + b
                    n = KEYS[g]
                    if u >= 2:
                        pool.wait_ge(k_r, u - 1)
                    pool.dma_start(K_in[0:n, u % 2, :], cache_rows(g, b, 0)).then_inc(k_l[u % 2], 16)

            for g in range(NGRP):
                if g >= 1:
                    keys_of(g - 1)
                pool.wait_ge(kv_e, 14 * g + 12)
                lo = 1 if g == 0 else 0
                pool.dma_start(kv_p[g][0, 0].rearrange("(c p) w h d -> p c (w h d)", p=P),
                               KV[:, lo:2, :, :].rearrange("p c w d -> p c (w d)")).then_inc(kvst, 16)
                pool.dma_start(kv_s[g][0].rearrange("b s w h d -> b (s w h d)"),
                               kv_s_rows[0:NS, :]).then_inc(kvst, 16)
            keys_of(NGRP - 1)
            pool.wait_ge(h_m, 2 * DT * NGRP)
            link(pool.memset(own_head, 0.0))
            own = own_head.rearrange("p (t h d) -> p t h d", t=4, h=2)
            for c in range(2):
                for q in range(2):
                    link(pool.affine_select(out=own, in_=own, compare_op=ALU.not_equal, fill=1.0,
                                            base=-(64 * c + 32 * q + 4 * q), pattern=[[-1, 4], [-8, 2], [0, HD]],
                                            channel_multiplier=1))
            link(pool.affine_select(out=quarter[:, :], in_=ones[:, 0:4], compare_op=ALU.is_ge, fill=0.0, base=0,
                                    pattern=[[-32, 4]], channel_multiplier=1))
            pool.affine_select(out=quarter[:, :], in_=quarter[:, :], compare_op=ALU.is_ge, fill=0.0, base=31,
                               pattern=[[32, 4]], channel_multiplier=-1).then_inc(s_const, 1)
            router_weights(1)

        @block.tensor
        def _(pe):
            def transpose(out, in_):
                return pe.transpose(out, in_, ident[0:in_.shape[0], 0:in_.shape[0]])

            def norm(k, xn):
                pe.wait_ge(n_xn, 3 * (k + 1))
                for d in range(DT):
                    if d >= 4:
                        pe.wait_ge(n_ht, DT * k + d - 3)
                    for t, r in enumerate(ROWS):
                        mm = transpose(bank[d % 4][:, t * P:t * P + r], xn[0:r, t, d * P:(d + 1) * P])
                    mm.then_inc(n_tp, 1)

            def moe(l):
                s = moes[l]
                pe.wait_ge(m_wr, 16 * (1 + EG) * (l + 1))
                pe.wait_ge(n_ht, DT * (2 * l + 2))
                for t, r in enumerate(ROWS):
                    for k in range(DT):
                        mm = pe.matmul(bank[6][0:r, t * (EG + NE):(t + 1) * (EG + NE)], hT[:, k, t * P:t * P + r],
                                       wr[:, k, :], start=(k == 0), stop=(k == DT - 1))
                mm.then_inc(m_lg, 1)
                pe.wait_ge(m_mk, 2 * (l + 1))
                for t, r in enumerate(ROWS + (P,)):
                    out = bank[7][0:r, t * NE:(t + 1) * NE]
                    for u in range(min(t + 1, 3)):
                        ru = ROWS[u]
                        how = strict if u == t else ones
                        mm = pe.matmul(out, how[0:ru, 0:r], msk[0:ru, u, :], start=(u == 0), stop=(u == min(t, 2)))
                mm.then_inc(m_rk, 1)
                pe.wait_ge(m_R, l + 1)
                rounds = pe.value_load(rounds_i[0:1, 0:1], min_val=1, max_val=ROUNDS)

                def chunk_landed(j, it):
                    slot = (MOE_SLOT[l] + j) % RING
                    before = sum((n + STREAM_SLOT[l]) % RING == slot for n in range((SSM_CHUNKS, ATT_CHUNKS)[l]))
                    pe.wait_ge(loads[l][slot], it * 16 + 16 * (before + 1))

                def weights(j, k_tiles):
                    return ring[:, (MOE_SLOT[l] + j) % RING, :].rearrange("p (k n) -> p k n", k=k_tiles)

                def gather(q):
                    for d in range(4):
                        c = (4 * q + d) * P
                        for t, r in enumerate(ROWS):
                            mm = pe.matmul(bank[4 + q][:, d * P:(d + 1) * P], xn_e[0:r, t, c:c + P],
                                           Pm[0:r, t, :, :].rearrange("p e s -> p (e s)"),
                                           start=(t == 0), stop=(t == 2))
                    mm.then_inc(s.ga, 1)

                def gate_or_up(j, it):
                    chunk_landed(2 * j, it)
                    chunk_landed(2 * j + 1, it)
                    for k in range(DT):
                        for e in range(2):
                            mm = pe.matmul(bank[j][e * SLOTS:(e + 1) * SLOTS, :], Xg[:, k, e * SLOTS:(e + 1) * SLOTS],
                                           weights(2 * j + e, DT)[:, k, :], start=(k == 0), stop=(k == DT - 1))
                    mm.then_inc(s.gu, 1)

                def scatter(d):
                    pe.matmul(bank[6 + d % 2][:, 0:T], ysl[:, d, :], CmT[:, :], start=True, stop=True).then_inc(s.sc, 1)

                def down(q):
                    for k in range(4):
                        for e in range(2):
                            mm = pe.matmul(bank[2 + q][e * SLOTS:(e + 1) * SLOTS, :],
                                           actT[:, k, e * SLOTS:(e + 1) * SLOTS],
                                           weights(4 + e, 4)[:, k, q * 512:(q + 1) * 512],
                                           start=(k == 0), stop=(k == 3))
                            if k == 3 and q == 1:
                                mm.then_inc(s.dn, 1)
                    if q == 0:
                        mm.then_inc(s.dh, 1)

                pe.wait_ge(s.peq, 1)
                gather(0)
                gather(1)
                with pe.Fori(0, rounds * PAIRS) as it:
                    pe.wait_ge(s.xg, it * 2 + 2)
                    pe.wait_ge(s.at, it + 1)
                    gate_or_up(0, it)
                    pe.wait_ge(s.cpt, it + 1)
                    gate_or_up(1, it)
                    pe.wait_ge(s.y, it * 2 + 2)
                    for d in range(DT):
                        pe.wait_ge(s.acc, it * 8 + max(1, d))
                        scatter(d)
                    pe.wait_ge(s.act, it + 2)
                    for f in range(4):
                        mm = transpose(bank[0][:, f * P:(f + 1) * P], act_r[:, f * P:(f + 1) * P])
                    mm.then_inc(s.tp, 1)
                    pe.wait_ge(s.cm, it + 1)
                    for t, r in enumerate(ROWS):
                        mm = transpose(bank[1][:, t * P:t * P + r], Cm[0:r, t, :, :].rearrange("p e s -> p (e s)"))
                    mm.then_inc(s.cp, 1)
                    pe.wait_ge(s.peq, it + 2)
                    gather(0)
                    gather(1)
                    pe.wait_ge(s.at, it + 2)
                    chunk_landed(4, it)
                    chunk_landed(5, it)
                    down(0)
                    down(1)
                pe.wait_ge(s.cpt, rounds * PAIRS + 1)
                pe.wait_ge(s.y, rounds * (2 * PAIRS) + 2)
                for d in range(DT):
                    pe.wait_ge(s.acc, rounds * (8 * PAIRS) + max(1, d))
                    scatter(d)
                pe.wait_ge(s.acc, rounds * (8 * PAIRS) + 9)
                for t, r in enumerate(ROWS):
                    for q in range(2):
                        j = 2 * t + q
                        if j >= 4:
                            pe.wait_ge(s_xa, 12 * l + 6 + j - 3)
                        for d in range(4):
                            mm = transpose(bank[j % 4][0:r, d * P:(d + 1) * P], accT[:, 4 * q + d, t * P:t * P + r])
                        mm.then_inc(s_ot, 1)

            pe.wait_ge(s_const, 8)
            pe.wait_ge(s_vld, 144)
            transpose(bank[7][:, 0:72], vrow[0:72, :])
            transpose(bank[7][:, 72:168], cwrow[0:96, :])
            pe.matmul(bank[7][:, 168:184], half[:, :], d_row[0:2, :], start=True, stop=True).then_inc(s_pvec, 1)
            norm(0, xn_m)
            pe.wait_ge(s_vld, 144)
            w = (CW - 1) * NS
            for q in range(2):
                for c in range(12):
                    ct = 12 * q + c
                    mm = transpose(bank[5 + q][:, c * w:(c + 1) * w], csr[0:w, ct * P:(ct + 1) * P])
                mm.then_inc(s_stp, 1)
            pe.wait_ge(s_dtld, 16)
            pe.wait_ge(n_ht, DT)
            for k in range(DT):
                mm = pe.matmul(bank[4][0:SH, 0:T], dtw[:, k, :], hT[:, k, :], start=(k == 0), stop=(k == DT - 1))
            mm.then_inc(s_dtp, 1)
            for i in range(CT):
                if i % 4 == 0:
                    wait_chunk(pe, i // 4)
                if i >= 2:
                    pe.wait_ge(s_raw, 2 * i - 2)
                wv = ring[:, (i // 4) % RING, :].rearrange("p (k n) -> p k n", k=DT)
                for k in range(DT):
                    mm = pe.matmul(bank[i % 2][:, 0:T], wv[:, k, (i % 4) * P:(i % 4 + 1) * P], hT[:, k, :],
                                   start=(k == 0), stop=(k == DT - 1))
                mm.then_inc(s_prj, 1)
            pe.wait_ge(s_nc, 2 * CT)
            for q in range(CT // 4):
                if q >= 2:
                    pe.wait_ge(s_nrw, q - 1)
                for c in range(4):
                    mm = transpose(bank[5 + q % 2][0:11, c * P:(c + 1) * P], newc[:, 4 * q + c, :])
                mm.then_inc(s_ntp, 1)

            pe.wait_ge(s_dt, 2)
            for j, v in enumerate((dtT, dAT)):
                for t, r in enumerate(ROWS):
                    mm = transpose(bank[4][0:r, (3 * j + t) * SH:(3 * j + t + 1) * SH], v[0:SH, t * P:t * P + r])
            mm.then_inc(s_tk, 1)
            pe.wait_ge(s_tkv, 4)
            pe.wait_ge(s_nrw, CT // 4)
            for c in range(2):
                pe.matmul(bank[5][:, 2 * c * SH:(2 * c + 1) * SH], upper[:, :], dA_tok[:, c, :], start=True, stop=True)
                mm = pe.matmul(bank[5][:, (2 * c + 1) * SH:(2 * c + 2) * SH], ones[:, :], dA_tok[:, c, :],
                               start=True, stop=True)
            mm.then_inc(s_tk, 1)
            pe.wait_ge(s_cx, 2 * CT)
            for c in range(2):
                for g in range(SG):
                    mm = transpose(bank[2 + c][:, g * N:(g + 1) * N], conv_out[:, 16 + g, c * P:(c + 1) * P])
            mm.then_inc(s_tk, 1)

            def cs_rows(t):
                if t < 2:
                    pe.wait_ge(s_tkv, 8)
                else:
                    pe.wait_ge(s_seg, 4 * (t - 1))
                for c in range(2):
                    for h in range(2):
                        mm = pe.matmul(bank[2 + t % 2][:, (2 * c + h) * P:(2 * c + h + 1) * P],
                                       dA_tok[:, c, 2 * t + h:2 * t + h + 1].to_broadcast([P, P]), upper[:, :],
                                       start=True, stop=True)
                mm.then_inc(s_csb, 1)

            cs_rows(0)
            for g in range(SG):
                if g >= 1:
                    pe.wait_ge(s_cbm, 3 * g)
                    pe.wait_ge(s_So, TPG * g)
                for c in range(2):
                    for j in range(TPG):
                        mm = transpose(bank[6 + c][:, j * P:(j + 1) * P], conv_out[:, TPG * g + j, c * P:(c + 1) * P])
                    mm.then_inc(s_xtp, 1)
                pe.wait_ge(s_xdt, 2 * g + 2)
                Bg, Cg = conv_out[:, 16 + g, :], conv_out[:, 20 + g, :]
                for j, (cj, ci) in enumerate(((0, 0), (1, 1), (0, 1))):
                    mm = pe.matmul(bank[6][:, j * P:(j + 1) * P], Bg[:, cj * P:(cj + 1) * P], Cg[:, ci * P:(ci + 1) * P],
                                   start=True, stop=True)
                mm.then_inc(s_cb, 1)
                for j in range(TPG):
                    t = TPG * g + j
                    if t + 1 < XT_TILES:
                        cs_rows(t + 1)
                    yb = bank[4 + t % 2]
                    if t < 2:
                        pe.wait_ge(s_tkv, 8)
                    else:
                        pe.wait_ge(s_y, t - 1)
                    for h in range(2):
                        pe.matmul(yb[h * HD:(h + 1) * HD, 3 * P:4 * P],
                                  dA_tok[:, 1, 2 * t + h:2 * t + h + 1].to_broadcast([P, HD]),
                                  upper[:, :], start=True, stop=True)
                    pe.wait_ge(s_cbm, 3 * g + 3)
                    pe.wait_ge(s_M, t + 1)
                    for c in range(2):
                        for h in range(2):
                            pe.matmul(yb[h * HD:(h + 1) * HD, c * P:(c + 1) * P],
                                      xdt[:, c, j * P + h * HD:j * P + (h + 1) * HD],
                                      seg[:, t % 2, (2 * c + h) * P:(2 * c + h + 1) * P], start=True, stop=True)
                    pe.matmul(yb[:, 2 * P:3 * P], xw[:, 0, j * P:(j + 1) * P], cbm[:, 2, :],
                              start=True, stop=True).then_inc(s_yp, 1)
                    if t >= 1:
                        pe.wait_ge(s_So, t)
                    for c in range(2):
                        mm = pe.matmul(bank[7][:, c * N:(c + 1) * N], xw[:, c, j * P:(j + 1) * P],
                                       b_tok[:, c, g * N:(g + 1) * N], start=True, stop=True)
                    mm.then_inc(s_Sp, 1)

            pe.wait_ge(s_y, XT_TILES)
            pe.wait_ge(s_So, XT_TILES)
            for j in range(2):
                for g in range(SG):
                    mm = transpose(bank[2 + j][0:NS, g * N:(g + 1) * N], conv_out[:, 16 + SG * j + g, TP:T])
            mm.then_inc(s_dtk, 1)
            for t in range(XT_TILES):
                for h in range(2):
                    mm = pe.matmul(bank[4][h * HD:(h + 1) * HD, t * NS:(t + 1) * NS],
                                   ident[0:SH, 2 * t + h:2 * t + h + 1].to_broadcast([SH, HD]),
                                   dAT[0:SH, TP:T], start=True, stop=True)
            mm.then_inc(s_dtk, 1)
            def group_rows(g):
                pe.wait_ge(s_dcv, 3 + g)
                for j in range(TPG):
                    mm = transpose(bank[5][0:NS, j * P:(j + 1) * P], conv_out[:, TPG * g + j, TP:T])
                mm.then_inc(s_dtk, 1)
                pe.wait_ge(s_cbp, 2 * g + 1)
                if g >= 1:
                    pe.wait_ge(s_cbc, g)
                for q in range(2):
                    mm = pe.matmul(bank[2 + q][:, :], ones[0:NS, :], diagC[0:NS, 4 * q:4 * q + 4, :],
                                   start=True, stop=True)
                mm.then_inc(s_cbv, 1)

            group_rows(0)
            for t in range(XT_TILES):
                g = t // TPG
                n = 6 + t // 4
                if t % 4 == 0:
                    wait_chunk(pe, n)
                if t >= 2:
                    pe.wait_ge(s_zc, t - 1)
                wv = ring[:, n % RING, :].rearrange("p (k n) -> p k n", k=DT)
                for k in range(DT):
                    mm = pe.matmul(bank[t % 2][:, 0:T], wv[:, k, (t % 4) * P:(t % 4 + 1) * P], hT[:, k, :],
                                   start=(k == 0), stop=(k == DT - 1))
                mm.then_inc(s_zp if t < 15 else moes[0].gu, 1)
                for q in range(2):
                    u = 2 * t + q
                    if t % TPG == 0 and q == 0:
                        pe.wait_ge(s_cbp, 2 * g + 2)
                        pe.wait_ge(s_dcv, 4 + g)
                    if u >= 2:
                        pe.wait_ge(s_h, u - 1)
                    pe.matmul(bank[6 + q][:, :], dtx[0:NS, g % 2, (t % TPG) * P:(t % TPG + 1) * P],
                              diagB[0:NS, 4 * q:4 * q + 4, :], start=True, stop=True).then_inc(s_op, 1)
                if t % TPG == 1 and g + 1 < SG:
                    group_rows(g + 1)
            for d in range(DT):
                n = 10 + d // 2
                if d % 2 == 0:
                    wait_chunk(pe, n)
                if d >= 2:
                    pe.wait_ge(s_oc, d - 1)
                wv = ring[:, n % RING, :].rearrange("p (k n) -> p k n", k=16)
                for k in range(XT_TILES):
                    if d == 0:
                        pe.wait_ge(s_gn, k + 1)
                    mm = pe.matmul(bank[d % 2][:, 0:T], wv[:, k, (d % 2) * P:(d % 2 + 1) * P], conv_out[:, k, :],
                                   start=(k == 0), stop=(k == XT_TILES - 1))
                mm.then_inc({3: moes[0].gu, 5: moes[0].dn, 7: moes[0].dn}.get(d, s_op2), 1)
                if d == 0:
                    pe.wait_ge(s_gq, XT_TILES)
                    for t, r in enumerate(ROWS):
                        for k in range(XT_TILES):
                            mm = pe.matmul(bank[2][0:r, t:t + 1], zT[:, k, t * P:t * P + r], ones[:, 0:1],
                                           start=(k == 0), stop=(k == XT_TILES - 1))
                    mm.then_inc(s_gs, 1)
            pe.wait_ge(s_oc, DT)
            for t, r in enumerate(ROWS):
                for q in range(2):
                    j = 2 * t + q
                    if j >= 4:
                        pe.wait_ge(s_xa, j - 3)
                    for d in range(4):
                        mm = transpose(bank[3 + j % 4][0:r, d * P:(d + 1) * P], hT[:, 4 * q + d, t * P:t * P + r])
                    mm.then_inc(s_ot, 1)
            norm(1, xn_e)
            moe(0)

            norm(2, xn_a)
            pe.matmul(bank[7][:, 0:P], half[:, :], half[:, :], start=True, stop=True).then_inc(c_p, 1)
            pe.wait_ge(n_ht, 3 * DT)

            def qkv_tile(i):
                n = i // 4
                slot = (STREAM_SLOT[1] + n) % RING
                if i % 4 == 0:
                    pe.wait_ge(loads[1][slot], 16 * (n // RING + 1))
                if i >= 2:
                    pe.wait_ge(q_e, i - 1)
                wv = ring[:, slot, :].rearrange("p (k n) -> p k n", k=DT)
                for k in range(DT):
                    mm = pe.matmul(bank[i % 2][:, 0:T], wv[:, k, (i % 4) * P:(i % 4 + 1) * P], hT[:, k, :],
                                   start=(k == 0), stop=(k == DT - 1))
                mm.then_inc(moes[1].gu if i in (63, 71) else q_p, 1)

            def kv_job(g, j):
                n = 14 * g + j
                if n >= 2:
                    pe.wait_ge(kv_e, n - 1)
                if j < 12:
                    kind, q, c = j // 6, j % 6 // 3, j % 3
                    pe.wait_ge(q_e, 24 * g + 8 * kind + 4 * q + 4)
                else:
                    kind, q, c = 2, j - 12, 2
                    pe.wait_ge(h_c, 2 * DT * (g + 1))
                for d in range(4):
                    src = vT[:, d, :] if kind == 0 else (kT if kind == 1 else qT)[:, 4 * q + d, :]
                    mm = transpose(bank[4 + n % 2][0:ROWS[c], d * P:(d + 1) * P], src[:, c * P:c * P + ROWS[c]])
                mm.then_inc(kv_t, 1)

            def query(g, u):
                b, q = u // 2, u % 2
                n = 16 * g + u
                if u == 0:
                    pe.wait_ge(kv_e, 14 * g + 14)
                    pe.wait_ge(h_m, 2 * DT * (g + 1))
                if n >= 2:
                    pe.wait_ge(k_m, n - 1)
                pe.matmul(bank[2 + q][:, :], ident[0:NS, b:b + 1].to_broadcast([NS, P]),
                          q_s[0:NS, 512 * q:512 * q + 512], start=True, stop=True).then_inc(k_q, 1)

            def scores(g, t):
                n = DT * g + t
                pe.wait_ge(q_e, 24 * g + 17 + t)
                for h in range(2):
                    if n >= 1:
                        pe.wait_ge(h_m, 2 * n - 1 + h)
                    if t == 0 and g >= 1:
                        pe.wait_ge(k_m, 16 * g)
                    r = slice(h * HD, (h + 1) * HD)
                    pe.matmul(bank[2 + h][:, 0:P], qT[r, t, 0:P], kT[r, t, 0:P], start=True, stop=True)
                    pe.matmul(bank[2 + h][:, P:3 * P], qT[r, t, P:TP], kT[r, t, 0:TP],
                              start=True, stop=True).then_inc(h_s, 1)

            def turn(g, t):
                n = DT * g + t
                pe.wait_ge(h_e, 4 * (n + 1))
                if t == 0:
                    pe.wait_ge(kv_e, 14 * g + 12)
                for h in range(2):
                    if n >= 1:
                        pe.wait_ge(h_c, 2 * n - 1 + h)
                    for j in range(3):
                        mm = transpose(bank[4 + h][:, j * P:(j + 1) * P], sm[:, t % 2, h, j * P:(j + 1) * P])
                    mm.then_inc(h_t, 1)

            def values(g, t):
                n = DT * g + t
                pe.wait_ge(h_c, 2 * n + 2)
                if n >= 1:
                    pe.wait_ge(h_o, n)
                for h in range(2):
                    c = (2 * t + h) * HD
                    out = [bank[6][:, (2 * i + h) * HD:(2 * i + h + 1) * HD] for i in range(2)]
                    pe.matmul(out[0], pT[:, t % 2, h, 0, :], KV[:, 0, 1, c:c + HD], start=True, stop=True)
                    pe.matmul(out[1], pT[:, t % 2, h, 1, :], KV[:, 0, 1, c:c + HD], start=True, stop=False)
                    mm = pe.matmul(out[1], pT[:, t % 2, h, 2, :], KV[:, 1, 1, c:c + HD], start=False, stop=True)
                mm.then_inc(h_v, 1)

            for g in range(NGRP):
                for i in range(16):
                    qkv_tile(24 * g + i)
                    if g >= 1:
                        query(g - 1, i)
                    if i % 4 == 0 and i >= 4:
                        for j in range(3):
                            kv_job(g, 3 * (i // 4 - 1) + j)
                for t in range(DT + 3):
                    if t < DT:
                        qkv_tile(24 * g + 16 + t)
                    if t == 0:
                        for j in range(3):
                            kv_job(g, 9 + j)
                    if 1 <= t <= DT:
                        scores(g, t - 1)
                    if 2 <= t <= DT + 1:
                        turn(g, t - 2)
                    if t >= 3:
                        values(g, t - 3)
                kv_job(g, 12)
                kv_job(g, 13)
            for u in range(16):
                query(NGRP - 1, u)
            pe.wait_ge(o_n, 2)
            for c in range(2):
                for q in range(2):
                    j = 2 * c + q
                    if j >= 2:
                        pe.wait_ge(o_c, j - 1)
                    for d in range(4):
                        mm = transpose(bank[4 + q][:, d * P:(d + 1) * P], O[:, c, (4 * q + d) * P:(4 * q + d + 1) * P])
                    mm.then_inc(o_t, 1)
            pe.wait_ge(k_r, NS * NGRP)
            pe.wait_ge(c_v, 1 + NGRP)
            at = 0
            for g in range(NGRP):
                transpose(bank[7][:, at:at + KEYS[g]], S_s[0:KEYS[g], g, :])
                at += KEYS[g]
            for g in range(NGRP):
                for h in range(2):
                    r = slice(h * HD, (h + 1) * HD)
                    mm = pe.matmul(bank[7][r, at + g:at + g + 1], prod[r, g, :], ones[r, 0:1], start=True, stop=True)
            mm.then_inc(c_p, 1)
            pe.wait_ge(c_v, 6 + NGRP)
            at = 0
            for g in range(NGRP):
                transpose(bank[6][0:KEYS[g], g * P:(g + 1) * P], p_s[:, at:at + KEYS[g]])
                mm = pe.matmul(bank[2][:, g * DT * NS:(g + 1) * DT * NS], PHp[:, g, :], fold[:, :],
                               start=True, stop=True)
                at += KEYS[g]
            mm.then_inc(c_p, 1)
            pe.wait_ge(c_a, 3)
            pe.wait_ge(o_c, 4)
            pe.wait_ge(c_v, 7 + NGRP)

            def own_channels(i):
                pe.wait_ge(y_o, i + 1)
                for t in range(4):
                    mm = pe.matmul(bank[3][:, 16 * i + 4 * t:16 * i + 4 * t + 4], y_own[:, t * P:(t + 1) * P],
                                   quarter[:, :], start=True, stop=True)
                mm.then_inc(c_p, 1)

            for b in range(NS):
                pe.wait_ge(v_l[b % 2], 48 * (b // 2 + 1))
                if b >= 4 and b % 2 == 0:
                    pe.wait_ge(y_o, b // 2 - 1)
                for g in range(NGRP):
                    n = KEYS[g]
                    for q in range(2):
                        r = 64 * (b % 2) + 32 * q
                        mm = pe.matmul(bank[4 + b // 2 % 2][r:r + 2 * DT, :], pTs[0:n, g, b:P:NS],
                                       V_in[0:n, b % 2, g, 512 * q:512 * q + 512],
                                       start=(g == 0), stop=(g == NGRP - 1))
                mm.then_inc(v_p, 1)
                if b >= 3 and b % 2:
                    own_channels(b // 2 - 1)
            own_channels(3)
            pe.wait_ge(c_v, 9 + NGRP)
            for d in range(DT):
                n = ATT_CHUNKS - 2 + d // 4
                slot = (STREAM_SLOT[1] + n) % RING
                if d % 4 == 0:
                    pe.wait_ge(loads[1][slot], 16 * (n // RING + 1))
                if d >= 2:
                    pe.wait_ge(s_oc, DT + d - 1)
                wv = ring[:, slot, :].rearrange("p (k n) -> p k n", k=DT)
                for k in range(DT):
                    mm = pe.matmul(bank[d % 2][:, 0:T], wv[:, k, (d % 4) * P:(d % 4 + 1) * P], yT[:, k, :],
                                   start=(k == 0), stop=(k == DT - 1))
                mm.then_inc(moes[1].dn if d % 4 == 3 else s_op2, 1)
            pe.wait_ge(s_oc, 2 * DT)
            for t, r in enumerate(ROWS):
                for q in range(2):
                    j = 2 * t + q
                    if j >= 4:
                        pe.wait_ge(s_xa, 12 + j - 3)
                    for d in range(4):
                        mm = transpose(bank[3 + j % 4][0:r, d * P:(d + 1) * P], hT[:, 4 * q + d, t * P:t * P + r])
                    mm.then_inc(s_ot, 1)
            norm(3, xn_e)
            moe(1)

        @block.scalar
        def _(act):
            def norm(k, xn):
                if k == 0:
                    act.wait_ge(s_xld, 32)
                for t, r in enumerate(ROWS):
                    if k:
                        act.wait_ge(s_xa, 6 * (k - 1) + 2 * (t + 1))
                    act.activation(xn[0:r, t, :], X[0:r, t, :], ACT.Square, accum_out=ss[0:r, t:t + 1]).then_inc(n_ss, 1)
                act.wait_ge(n_var, k + 1)
                act.activation(rstd[:, 0:3], ss[:, 0:3], ACT.Sqrt).then_inc(n_std, 1)

            def moe(l):
                s = moes[l]
                act.sem_inc(s.at, 1)
                act.wait_ge(m_ge, 2 * l + 1)
                act.activation(g_a[:, :, :], g_a[:, :, :], ACT.Exp).then_inc(m_ex, 1)
                act.wait_ge(m_ge, 2 * l + 2)
                act.activation(g_s[:, 4, :], g_s[:, 4, :], ACT.Exp).then_inc(m_ex, 1)
                act.wait_ge(m_R, l + 1)
                rounds = act.value_load(rounds_i[0:1, 0:1], min_val=1, max_val=ROUNDS)
                with act.Fori(0, rounds * PAIRS) as it:
                    act.wait_ge(s.gu, it * 2 + 3)
                    act.wait_ge(s.act, it + 1)
                    act.activation(sg[:, :], bank[0][:, :], ACT.Silu).then_inc(s.sg, 1)
                    act.wait_ge(s.tp, it + 1)
                    act.activation(actT[:, :, :], bank[0][:, :].rearrange("p (f s) -> p f s", f=4),
                                   ACT.Copy).then_inc(s.at, 1)
                    act.wait_ge(s.cp, it + 1)
                    act.activation(CmT[:, :], bank[1][:, 0:T], ACT.Copy).then_inc(s.cpt, 1)
                    act.wait_ge(s.dh, it + 1)
                    act.activation(ysl[:, 0:4, :], bank[2][:, :].rearrange("p (d s) -> p d s", d=4),
                                   ACT.Copy).then_inc(s.y, 1)
                    act.wait_ge(s.dn, it * 2 + 4)
                    act.activation(ysl[:, 4:8, :], bank[3][:, :].rearrange("p (d s) -> p d s", d=4),
                                   ACT.Copy).then_inc(s.y, 1)

            act.dma_start(vrow[0:16, :], a["norm_mix"].rearrange("l (t p) -> (l t) p", p=P)).then_inc(s_vld, 16)
            act.dma_start(vrow[16:32, :], a["norm_ffn"].rearrange("l (t p) -> (l t) p", p=P)).then_inc(s_vld, 16)
            act.dma_start(vrow[32:48, :], a["ssm_norm"].rearrange("l (t p) -> (l t) p", p=P)).then_inc(s_vld, 16)
            act.dma_start(vrow[48:72, :], a["ssm_conv_b"].rearrange("l (t p) -> (l t) p", p=P)).then_inc(s_vld, 16)
            act.dma_start(cwrow[0:96, :], a["ssm_conv_w"].rearrange("l w (t p) -> (l w t) p", p=P)).then_inc(s_vld, 16)
            act.dma_start(head_v[0:SH, 0:1], a["ssm_dt_bias"].rearrange("l h -> h l")).then_inc(s_vld, 16)
            act.dma_start(head_v[0:SH, 1:2], a["ssm_a_log"].rearrange("l h -> h l")).then_inc(s_vld, 16)
            act.dma_start(d_row[0:2, :], a["ssm_d"].rearrange("l (t r) -> (l r) t", r=2)).then_inc(s_vld, 16)
            act.dma_start(csr[0:CW * NS - NS, :], a["state_conv"][0].rearrange("b w c -> (b w) c")).then_inc(s_vld, 16)
            act.wait_ge(s_vvec, 3)
            norm(0, xn_m)
            act.wait_ge(s_vld, 144)
            act.wait_ge(s_dtp, 1)
            act.activation(spt[0:SH, 0, :], bank[4][0:SH, 0:T], ACT.Identity, bias=head_v[0:SH, 0:1]).then_inc(s_dtz, 1)
            act.activation(head_v[0:SH, 2:3], head_v[0:SH, 1:2], ACT.Exp).then_inc(s_dtz, 1)
            act.wait_ge(s_dte, 1)
            act.activation(spt[0:SH, 2, :], spt[0:SH, 1, :], ACT.Exp, scale=-1.0).then_inc(s_dtz, 1)
            for i in range(CT + 2):
                if i < CT:
                    act.wait_ge(s_prj, i + 1)
                    if i == 0:
                        act.wait_ge(s_stc, 3)
                    if i >= RAWS:
                        act.wait_ge(s_cv, i - RAWS + 1)
                        act.wait_ge(s_nc, 2 * (i - RAWS + 1))
                    b = bank[i % 2]
                    act.activation(raws[:, i % RAWS, PADW:PADW + TP], b[:, 0:TP], ACT.Copy).then_inc(s_raw, 1)
                    new = raws[:, i % RAWS, SAMP0:RAW].rearrange("p (b w) -> p b w", w=CW)[:, :, PADW]
                    act.activation(new, b[:, TP:T], ACT.Copy).then_inc(s_raw, 1)
                if i >= 2:
                    j = i - 2
                    ct = tile_order[j]
                    act.wait_ge(s_cv, j + 1)
                    act.activation(conv_out[:, ct, 0:TP], cacc[:, j % 2, 0:TP], ACT.Silu,
                                   bias=cbcol[:, ct:ct + 1]).then_inc(s_cx, 1)
                    act.activation(conv_out[:, ct, TP:T], cacc[:, j % 2, SAMP0:CONV:CW], ACT.Silu,
                                   bias=cbcol[:, ct:ct + 1]).then_inc(s_cx, 1)
            for q in range(CT // 4):
                act.wait_ge(s_ntp, q + 1)
                if q >= 2:
                    act.wait_ge(s_nst[q % 2], 32 * (q // 2))
                act.activation(newr[0:11, q % 2, :], bank[5 + q % 2][0:11, :], ACT.Copy).then_inc(s_nrw, 1)
            act.wait_ge(s_tkv, 5)
            act.activation(w_tok[:, :, :], w_tok[:, :, :], ACT.Exp).then_inc(s_achain, 1)
            for t in range(XT_TILES):
                for u in ((0, 1) if t == 0 else (t + 1,)):
                    if u < XT_TILES:
                        act.wait_ge(s_seg, 4 * (u + 1))
                        act.activation(seg[:, u % 2, :], seg[:, u % 2, :], ACT.Exp).then_inc(s_dec, 1)
                act.wait_ge(s_yp, t + 1)
                if t >= 2:
                    act.wait_ge(s_So, t - 1)
                    act.wait_ge(s_y, t - 1)
                act.activation(Et[:, t % 2, :], bank[4 + t % 2][:, 3 * P:4 * P], ACT.Exp).then_inc(s_E, 1)
                act.wait_ge(s_Sp, t + 1)
                if t >= 2:
                    act.wait_ge(s_Sst[t % 2], 16 * (t // 2))
                act.activation(hout[:, t % 2, :], bank[7][:, N:2 * N], ACT.Copy).then_inc(s_S1, 1)
            act.wait_ge(s_dtk, 2)
            act.activation(dAe[:, :, :], bank[4][:, 0:XT_TILES * NS].rearrange("p (t b) -> p t b", b=NS),
                           ACT.Exp).then_inc(s_dcv, 1)
            for t in range(XT_TILES):
                if t < 15:
                    act.wait_ge(s_zp, t + 1)
                else:
                    act.wait_ge(moes[0].gu, 1)
                act.activation(zT[:, t, :], bank[t % 2][:, 0:T], ACT.Silu).then_inc(s_zc, 1)
                if t % TPG == 0:
                    act.wait_ge(s_cbv, t // TPG + 1)
                    if t:
                        act.wait_ge(s_ys, t)
                    act.activation(Cb[:, 0:4, :], bank[2][:, :].rearrange("p (b n) -> p b n", n=N), ACT.Copy)
                    act.activation(Cb[:, 4:8, :], bank[3][:, :].rearrange("p (b n) -> p b n", n=N),
                                   ACT.Copy).then_inc(s_cbc, 1)
            for t in range(XT_TILES):
                act.wait_ge(s_g, t + 1)
                act.activation(zT[:, t, :], conv_out[:, t, :], ACT.Square).then_inc(s_gq, 1)
                act.wait_ge(s_gq, t + 1)
                act.activation(conv_out[:, t, :], conv_out[:, t, :], ACT.Copy, scale=gssm[:, t:t + 1]).then_inc(s_gn, 1)
            act.wait_ge(s_gs, 2)
            act.activation(rstd[:, 0:3], ss[:, 0:3], ACT.Sqrt).then_inc(s_gq, 1)
            for d in range(DT):
                when = {0: (s_op2, 1), 1: (s_op2, 2), 2: (s_op2, 3), 3: (moes[0].gu, 2), 4: (s_op2, 4),
                        5: (moes[0].dn, 1), 6: (s_op2, 5), 7: (moes[0].dn, 2)}[d]
                act.wait_ge(*when)
                act.activation(hT[:, d, :], bank[d % 2][:, 0:T], ACT.Copy).then_inc(s_oc, 1)
            norm(1, xn_e)
            moe(0)

            norm(2, xn_a)

            def qkv_done(i):
                if i in (63, 71):
                    act.wait_ge(moes[1].gu, 1 if i == 63 else 2)
                else:
                    act.wait_ge(q_p, i + 1 - (i > 63))

            def copy_tile(g, i):
                n = 24 * g + i
                qkv_done(n)
                if i < 8:
                    if i >= 4:
                        act.wait_ge(kv_t, 14 * g + 3)
                    elif g >= 1:
                        act.wait_ge(kv_t, 14 * g - 8)
                    act.activation(vTs[:, g, i * NS:(i + 1) * NS], bank[n % 2][:, TP:T], ACT.Copy).then_inc(q_vs, 1)
                    dst = vT[:, i % 4, :]
                elif i < 16:
                    if g >= 1:
                        act.wait_ge(h_s, 2 * DT * g)
                        act.wait_ge(c_v, g)
                    dst = kT[:, i - 8, :]
                else:
                    dst = qT[:, i - 16, :]
                act.activation(dst, bank[n % 2][:, 0:T], ACT.Copy).then_inc(q_e, 1)

            def copy_rows(g, j):
                n = 14 * g + j
                act.wait_ge(kv_t, n + 1)
                if j < 12:
                    kind, q, c = j // 6, j % 6 // 3, j % 3
                    if g >= 1 and j == 0:
                        act.wait_ge(kvst, 32 * g)
                        act.wait_ge(h_v, DT * g)
                    row = kv_s_rows[:, (1 - kind) * D:(2 - kind) * D] if c == 2 else KV[:, c, 1 - kind, :]
                else:
                    q, c = j - 12, 2
                    if g >= 1:
                        act.wait_ge(k_q, 16 * g)
                    row = q_s[:, :]
                act.activation(row[0:ROWS[c], 512 * q:512 * q + 512], bank[4 + n % 2][0:ROWS[c], :],
                               ACT.Copy).then_inc(kv_e, 1)

            def exps(g, t):
                n = DT * g + t
                act.wait_ge(h_x, n + 1)
                hs = slice(2 * t, 2 * t + 2)
                if g >= 1:
                    act.activation(al[:, :, hs], al[:, :, hs], ACT.Exp).then_inc(s_achain, 1)
                for h in range(2):
                    for i, (c0, c1) in enumerate(((0, P), (P, 3 * P))):
                        k = 2 * t + h
                        act.activation(sm[:, t % 2, h, c0:c1], sm[:, t % 2, h, c0:c1], ACT.Exp,
                                       bias=Mn[:, i, k:k + 1], accum_out=rs[:, i, k:k + 1]).then_inc(h_e, 1)

            def copy_probs(g, t):
                n = DT * g + t
                for h in range(2):
                    act.wait_ge(h_t, 2 * n + h + 1)
                    if n >= 2:
                        act.wait_ge(h_v, n - 1)
                    act.activation(pT[:, t % 2, h, :, :].rearrange("p a b -> p (a b)"), bank[4 + h][:, 0:3 * P],
                                   ACT.Copy).then_inc(h_c, 1)

            act.wait_ge(a_mv, 3)
            for g in range(NGRP):
                for i in range(16):
                    if i % 4 == 0 and i >= 4:
                        for j in range(3):
                            copy_rows(g, 3 * (i // 4 - 1) + j)
                    copy_tile(g, i)
                for t in range(DT + 3):
                    if t < DT:
                        copy_tile(g, 16 + t)
                    if t == 0:
                        for j in range(3):
                            copy_rows(g, 9 + j)
                    if 2 <= t <= DT + 1:
                        copy_probs(g, t - 2)
                    if 1 <= t <= DT:
                        exps(g, t - 1)
                copy_rows(g, 12)
                copy_rows(g, 13)
            for j in range(4):
                c, q = j // 2, j % 2
                act.wait_ge(o_t, j + 1)
                act.activation(yT[:, 4 * q:4 * q + 4, c * P:(c + 1) * P],
                               bank[4 + q][:, :].rearrange("p (d i) -> p d i", d=4), ACT.Copy).then_inc(o_c, 1)
            n_keys = sum(KEYS) + NGRP
            act.wait_ge(c_v, 2 + NGRP)
            act.activation(p_s[:, 0:n_keys], bank[7][:, 0:n_keys], ACT.Exp, bias=s_st[:, 1:2], scale=SCALE,
                           accum_out=s_st[:, 2:3]).then_inc(c_a, 1)
            act.wait_ge(c_p, 3)
            act.activation(pTs[:, 0:2, :], bank[6][:, 0:2 * P].rearrange("p (g c) -> p g c", g=2),
                           ACT.Copy).then_inc(c_a, 1)
            act.activation(pTs[0:KEYS[2], 2, :], bank[6][0:KEYS[2], 2 * P:3 * P], ACT.Copy).then_inc(c_a, 1)
            for d in range(DT):
                if d % 4 == 3:
                    act.wait_ge(moes[1].dn, d // 4 + 1)
                else:
                    act.wait_ge(s_op2, 5 + 3 * (d // 4) + d % 4 + 1)
                act.activation(hT[:, d, :], bank[d % 2][:, 0:T], ACT.Copy).then_inc(s_oc, 1)
            norm(3, xn_e)
            moe(1)
            norm(4, xn_e)

        @block.vector
        def _(v):
            steps = [0]

            def link(ins):
                steps[0] += 1
                ins.then_inc(s_chain, 1)
                v.wait_ge(s_chain, steps[0])

            v.memset(ss[:, :], 1.0).then_inc(s_vvec, 1)
            v.memset(rstd[:, :], 1.0).then_inc(s_vvec, 1)
            v.memset(arena[:, 0:4], 0.0).then_inc(s_vvec, 1)
            v.wait_ge(s_pvec, 1)
            v.tensor_copy(vcol[:, :], bank[7][:, 0:72]).then_inc(s_vvec, 1)
            v.tensor_copy(cwcol[:, :], bank[7][:, 72:168]).then_inc(s_vvec, 1)
            v.tensor_copy(d_col[:, :], bank[7][:, 168:184]).then_inc(s_vvec, 1)

            def norm(k, xn, g):
                v.wait_ge(n_ss, 3 * (k + 1))
                v.tensor_scalar(ss[:, 0:3], ss[:, 0:3], 1.0 / D, EPS, ALU.mult, ALU.add).then_inc(n_var, 1)
                v.wait_ge(n_std, k + 1)
                link(v.reciprocal(rstd[:, 0:3], rstd[:, 0:3]))
                for t, r in enumerate(ROWS):
                    v.tensor_scalar(xn[0:r, t, :], X[0:r, t, :], rstd[0:r, t:t + 1], None, ALU.mult).then_inc(n_xn, 1)
                for d in range(DT):
                    v.wait_ge(n_tp, DT * k + d + 1)
                    v.tensor_scalar(hT[:, d, :], bank[d % 4][:, 0:T], g[:, d:d + 1], None, ALU.mult).then_inc(n_ht, 1)

            def bc(x, *shape):
                return x.to_broadcast([P, *shape])

            def first_max(x, order, n, mx, oh, tmp):
                link(v.tensor_reduce(mx, x, AX, ALU.max))
                link(v.tensor_tensor(oh, x, bc(mx.unsqueeze(2), 3, n), ALU.is_equal))
                link(v.tensor_tensor(oh, oh, bc(order.unsqueeze(1), 3, n), ALU.mult))
                link(v.tensor_reduce(tmp, oh, AX, ALU.max))
                link(v.tensor_tensor(oh, oh, bc(tmp.unsqueeze(2), 3, n), ALU.is_equal))

            def moe(l):
                s = moes[l]
                v.sem_inc(s.act, 1)
                v.memset(CmT[:, :], 0.0).then_inc(s.cpt, 1)
                v.memset(ysl[:, :, :], 0.0).then_inc(s.y, 2)
                v.memset(accT[:, :, :], 0.0).then_inc(s.acc, 1)
                link(v.memset(lg[:, :, :], 0.0))
                link(v.memset(rk[:, :, :], -1.0))
                link(v.memset(cc[:, :, :], 0.0))
                link(v.memset(msk[:, :, :], 0.0))
                link(v.memset(cmb[:, :, :], 0.0))
                link(v.memset(rnk[:, :, :], 0.0))
                v.wait_ge(m_lg, l + 1)
                b6 = bank[6][:, 0:3 * (EG + NE)].rearrange("p (t e) -> p t e", t=3)
                link(v.tensor_copy(lg[:, 0:2, :], b6[:, 0:2, :]))
                link(v.tensor_copy(lg[0:NS, 2, :], b6[0:NS, 2, :]))
                gl = lg[:, :, 0:EG]
                el = lg[:, :, EG:].rearrange("p t (g e) -> p t g e", g=EG)
                gmax, gtmp, gate, m1, dd, w1, w2, m2 = (g_s[:, i, :] for i in range(8))
                first_max(gl, first4[:, :], EG, gmax, g_oh[:, :, :], gtmp)
                v.tensor_tensor(g_a[:, :, :], gl, bc(gmax.unsqueeze(2), 3, EG), ALU.subtract).then_inc(m_ge, 1)
                link(v.tensor_tensor(e_w[:, :, :, :], el, bc(g_oh[:, :, :].unsqueeze(3), 3, EG, EPG), ALU.mult))
                link(v.tensor_reduce(es[:, :, :], e_w[:, :, :, :].rearrange("p t g e -> p t e g"), AX, ALU.add))
                first_max(es[:, :, :], first8[:, :], EPG, m1, oh1[:, :, :], gtmp)
                link(v.scalar_tensor_tensor(out=e_a[:, :, :], in0=oh1[:, :, :], scalar=-BIG, in1=es[:, :, :],
                                            op0=ALU.mult, op1=ALU.add))
                first_max(e_a[:, :, :], first8[:, :], EPG, m2, oh2[:, :, :], gtmp)
                v.tensor_tensor(dd, m2, m1, ALU.subtract).then_inc(m_ge, 1)
                v.wait_ge(m_ex, 2 * l + 1)
                link(v.tensor_reduce(gate, g_a[:, :, :], AX, ALU.add))
                v.wait_ge(m_ex, 2 * l + 2)
                link(v.tensor_scalar(w1, dd, 1.0, None, ALU.add))
                link(v.tensor_tensor(w1, w1, gate, ALU.mult))
                link(v.reciprocal(w1, w1))
                link(v.tensor_tensor(w2, w1, dd, ALU.mult))
                link(v.tensor_tensor(e_sel[:, :, :], oh1[:, :, :], oh2[:, :, :], ALU.add))
                link(v.tensor_tensor(oh1[:, :, :], oh1[:, :, :], bc(w1.unsqueeze(2), 3, EPG), ALU.mult))
                link(v.tensor_tensor(oh2[:, :, :], oh2[:, :, :], bc(w2.unsqueeze(2), 3, EPG), ALU.mult))
                link(v.tensor_tensor(e_in[:, :, :], oh1[:, :, :], oh2[:, :, :], ALU.add))
                for out, x in ((cmb, e_in), (msk, e_sel)):
                    for r, t0, t1 in ((P, 0, 2), (NS, 2, 3)):
                        n = t1 - t0
                        ins = v.tensor_tensor(out[0:r, t0:t1, :].rearrange("p t (g e) -> p t g e", g=EG),
                                              g_oh[0:r, t0:t1, :].unsqueeze(3).to_broadcast([r, n, EG, EPG]),
                                              x[0:r, t0:t1, :].unsqueeze(2).to_broadcast([r, n, EG, EPG]), ALU.mult)
                        if out is msk:
                            ins.then_inc(m_mk, 1)
                        else:
                            link(ins)
                v.wait_ge(m_rk, l + 1)
                v.wait_ge(m_mk, 2 * l + 2)
                b7 = bank[7][:, 0:4 * NE].rearrange("p (t e) -> p t e", t=4)
                link(v.tensor_reduce(cnt_s[0:1, 0:1], b7[0:1, 3, :], AX, ALU.max))
                link(v.tensor_scalar(cnt_s[0:1, 1:1 + ROUNDS], thresh[0:1, 0:ROUNDS], cnt_s[0:1, 0:1], None, ALU.is_lt))
                link(v.tensor_reduce(cnt_s[0:1, 7:8], cnt_s[0:1, 1:1 + ROUNDS], AX, ALU.add))
                v.tensor_copy(rounds_i[0:1, 0:1], cnt_s[0:1, 7:8]).then_inc(m_R, 1)
                link(v.scalar_tensor_tensor(out=rnk[:, 0:2, :], in0=b7[:, 0:2, :], scalar=1.0, in1=msk[:, 0:2, :],
                                            op0=ALU.add, op1=ALU.mult))
                link(v.scalar_tensor_tensor(out=rnk[0:NS, 2, :], in0=b7[0:NS, 2, :], scalar=1.0, in1=msk[0:NS, 2, :],
                                            op0=ALU.add, op1=ALU.mult))
                for r in range(ROUNDS):
                    link(v.tensor_scalar(rk[:, :, r * NE:(r + 1) * NE], rnk[:, :, :], -1.0 - SLOTS * r, None, ALU.add))
                    link(v.tensor_copy(cc[:, :, r * NE:(r + 1) * NE], cmb[:, :, :]))

                def slots(col):
                    for t in range(3):
                        ins = v.tensor_tensor(Pm[:, t, :, :], slot_no[:, :].unsqueeze(1).to_broadcast([P, 2, SLOTS]),
                                              bc(rk[:, t, col].unsqueeze(2), 2, SLOTS), ALU.is_equal)
                    ins.then_inc(s.peq, 1)

                def shares(col):
                    for t in range(3):
                        ins = v.tensor_tensor(Cm[:, t, :, :], Pm[:, t, :, :],
                                              bc(cc[:, t, col].unsqueeze(2), 2, SLOTS), ALU.mult)
                    ins.then_inc(s.cm, 1)

                def tokens(n):
                    for q in range(2):
                        v.wait_ge(s.ga, n * 2 + q + 1)
                        v.tensor_tensor(Xg[:, 4 * q:4 * q + 4, :], bank[4 + q][:, :].rearrange("p (d s) -> p d s", d=4),
                                        bc(gffn(l)[:, 4 * q:4 * q + 4].unsqueeze(2), 4, P), ALU.mult).then_inc(s.xg, 1)

                def add(n):
                    for d in range(DT):
                        v.wait_ge(s.sc, n * 8 + d + 1)
                        v.tensor_tensor(accT[:, d, :], accT[:, d, :], bank[6 + d % 2][:, 0:T], ALU.add).then_inc(s.acc, 1)

                slots(slice(0, 2))
                v.wait_ge(m_R, l + 1)
                rounds = v.value_load(rounds_i[0:1, 0:1], min_val=1, max_val=ROUNDS)
                tokens(0)
                with v.Fori(0, rounds * PAIRS) as it:
                    v.wait_ge(s.peq, it + 1)
                    shares(bass.ds(it * 2, 2))
                    v.wait_ge(s.cm, it + 1)
                    slots(bass.ds(it * 2 + 2, 2))
                    v.wait_ge(s.sg, it + 1)
                    v.wait_ge(s.gu, it * 2 + 4)
                    v.tensor_tensor(act_r[:, :], sg[:, :], bank[1][:, :], ALU.mult).then_inc(s.act, 1)
                    add(it)
                    tokens(it + 1)
                add(rounds * PAIRS)
                v.wait_ge(s.acc, rounds * (8 * PAIRS) + 9)
                for t, r in enumerate(ROWS):
                    for q in range(2):
                        j = 2 * t + q
                        v.wait_ge(s_ot, 12 * l + 6 + j + 1)
                        xs = X[0:r, t, 512 * q:512 * q + 512]
                        v.tensor_tensor(xs, xs, bank[j % 4][0:r, :], ALU.add).then_inc(s_xa, 1)

            v.wait_ge(s_vvec, 6)
            norm(0, xn_m, gmix(0))
            for q in range(2):
                v.wait_ge(s_stp, q + 1)
                v.tensor_copy(stT[:, 12 * q:12 * q + 12, :],
                              bank[5 + q][:, 0:288].rearrange("p (c w) -> p c w", c=12)).then_inc(s_stc, 1)
            v.memset(raws[:, :, 0:PADW], 0.0).then_inc(s_stc, 1)
            z, az, u, s, s2, p_ = (spt[0:SH, i, :] for i in range(6))
            v.wait_ge(s_dtz, 2)
            v.scalar_tensor_tensor(out=az, in0=z, scalar=-1.0, in1=z, op0=ALU.mult, op1=ALU.max).then_inc(s_dte, 1)
            v.wait_ge(s_dtz, 3)
            link(v.tensor_scalar(s, u, 2.0, None, ALU.add))
            link(v.reciprocal(s, s))
            link(v.tensor_tensor(s, s, u, ALU.mult))
            link(v.tensor_tensor(s2, s, s, ALU.mult))
            link(v.tensor_scalar(p_, s2, 1.0 / 15, None, ALU.mult))
            for k in range(13, 1, -2):
                link(v.scalar_tensor_tensor(out=p_, in0=p_, scalar=1.0 / k, in1=s2, op0=ALU.add, op1=ALU.mult))
            link(v.scalar_tensor_tensor(out=p_, in0=p_, scalar=1.0, in1=s, op0=ALU.add, op1=ALU.mult))
            link(v.tensor_scalar(z, z, 0.0, None, ALU.max))
            link(v.scalar_tensor_tensor(out=dtT[0:SH, :], in0=p_, scalar=2.0, in1=z, op0=ALU.mult, op1=ALU.add))
            v.tensor_scalar(head_v[0:SH, 3:4], head_v[0:SH, 2:3], -1.0, None, ALU.mult).then_inc(s_dt, 1)
            v.wait_ge(s_dt, 1)
            v.tensor_scalar(dAT[0:SH, :], dtT[0:SH, :], head_v[0:SH, 3:4], None, ALU.mult).then_inc(s_dt, 1)
            for i, ct in enumerate(tile_order):
                v.wait_ge(s_raw, 2 * i + 2)
                v.wait_ge(s_rst, i + 1)
                if i >= 2:
                    v.wait_ge(s_cx, 2 * i - 2)
                r, acc = raws[:, i % RAWS, :], cacc[:, i % 2, :]
                link(v.tensor_scalar(acc, r[:, 0:CONV], cwcol[:, ct:ct + 1], None, ALU.mult))
                for w in range(1, CW):
                    c = cwcol[:, w * CT + ct:w * CT + ct + 1]
                    ins = v.scalar_tensor_tensor(out=acc, in0=r[:, w:w + CONV], scalar=c, in1=acc,
                                                 op0=ALU.mult, op1=ALU.add)
                    if w < CW - 1:
                        link(ins)
                ins.then_inc(s_cv, 1)
            v.wait_ge(s_tk, 1)
            bt = bank[4][:, 0:6 * SH].rearrange("p (j t h) -> p j t h", j=2, t=3)
            v.tensor_copy(dt_tok[:, 0:2, :], bt[:, 0, 0:2, :]).then_inc(s_tkv, 1)
            v.tensor_copy(dt_tok[0:NS, 2, :], bt[0:NS, 0, 2, :]).then_inc(s_tkv, 1)
            v.tensor_copy(dA_tok[:, 0:2, :], bt[:, 1, 0:2, :]).then_inc(s_tkv, 1)
            v.tensor_copy(dA_tok[0:NS, 2, :], bt[0:NS, 1, 2, :]).then_inc(s_tkv, 1)
            v.wait_ge(s_tk, 2)
            bt = bank[5][:, 0:4 * SH].rearrange("p (c j h) -> p c j h", c=2, j=2)
            link(v.tensor_copy(cs_tok[:, :, :], bt[:, :, 0, :]))
            v.tensor_tensor(w_tok[:, :, :], bt[:, :, 1, :], cs_tok[:, :, :], ALU.subtract).then_inc(s_tkv, 1)
            v.wait_ge(s_tk, 3)
            for c in range(2):
                v.tensor_copy(b_tok[:, c, :], bank[2 + c][:, :]).then_inc(s_tkv, 1)
            v.memset(ysum[:, 0:4], 0.0).then_inc(s_tkv, 1)
            v.wait_ge(s_achain, 1)
            v.wait_ge(s_tkv, 8)
            for i in range(2):
                v.wait_ge(s_nst[i], 16 * CT // 4)
            def segments(t):
                v.wait_ge(s_csb, t + 1)
                if t >= 2:
                    v.wait_ge(s_yp, t - 1)
                for c in range(2):
                    for h in range(2):
                        q = 2 * c + h
                        v.tensor_scalar(seg[:, t % 2, q * P:(q + 1) * P], bank[2 + t % 2][:, q * P:(q + 1) * P],
                                        cs_tok[:, c, 2 * t + h:2 * t + h + 1], 0.0,
                                        ALU.subtract, ALU.min).then_inc(s_seg, 1)

            def finish(t):
                v.wait_ge(s_E, t + 1)
                yb = bank[4 + t % 2]
                v.tensor_tensor(y1[:, t % 2, :], yb[:, 2 * P:3 * P], Et[:, t % 2, :], ALU.mult)
                link(v.scalar_tensor_tensor(out=conv_out[:, t, 0:TP], in0=conv_out[:, t, 0:TP],
                                            scalar=d_col[:, t:t + 1], in1=yb[:, 0:TP], op0=ALU.mult, op1=ALU.add))
                v.tensor_tensor(conv_out[:, t, P:TP], conv_out[:, t, P:TP], y1[:, t % 2, :], ALU.add).then_inc(s_y, 1)
                v.wait_ge(s_S1, t + 1)
                v.scalar_tensor_tensor(out=hout[:, t % 2, :], in0=bank[7][:, 0:N], scalar=Et[:, t % 2, P - 1:P],
                                       in1=hout[:, t % 2, :], op0=ALU.mult, op1=ALU.add).then_inc(s_So, 1)

            segments(0)
            for g in range(SG):
                if g >= 1:
                    finish(TPG * g - 1)
                    v.wait_ge(s_Sp, TPG * g)
                hs = slice(2 * TPG * g, 2 * TPG * (g + 1))
                for c in range(2):
                    v.wait_ge(s_xtp, 2 * g + c + 1)
                    xv = xdt[:, c, :].rearrange("p (h d) -> p h d", d=HD)
                    link(v.tensor_tensor(xv, bank[6 + c][:, :].rearrange("p (h d) -> p h d", d=HD),
                                         dt_tok[:, c, hs].unsqueeze(2).to_broadcast([P, 2 * TPG, HD]), ALU.mult))
                    v.tensor_tensor(xw[:, c, :].rearrange("p (h d) -> p h d", d=HD), xv,
                                    w_tok[:, c, hs].unsqueeze(2).to_broadcast([P, 2 * TPG, HD]),
                                    ALU.mult).then_inc(s_xdt, 1)
                v.wait_ge(s_cb, g + 1)
                for j in range(2):
                    v.tensor_tensor(cbm[:, j, :], bank[6][:, j * P:(j + 1) * P], upper[:, :], ALU.mult).then_inc(s_cbm, 1)
                v.tensor_copy(cbm[:, 2, :], bank[6][:, 2 * P:3 * P]).then_inc(s_cbm, 1)
                for j in range(TPG):
                    t = TPG * g + j
                    v.wait_ge(s_dec, t + 1)
                    v.wait_ge(s_cbm, 3 * g + 3)
                    sv = seg[:, t % 2, :].rearrange("p (c h i) -> p c h i", c=2, h=2)
                    v.tensor_tensor(sv, sv, cbm[:, 0:2, :].unsqueeze(2).to_broadcast([P, 2, 2, P]),
                                    ALU.mult).then_inc(s_M, 1)
                    if t + 1 < XT_TILES:
                        segments(t + 1)
                    if j >= 1:
                        finish(t - 1)
            finish(XT_TILES - 1)
            v.wait_ge(s_dtk, 1)
            for j in range(2):
                v.tensor_copy(sb_rows[0:NS, j * 512:(j + 1) * 512], bank[2 + j][0:NS, :]).then_inc(s_dcv, 1)
            def dt_x(g):
                v.wait_ge(s_dtk, 3 + g)
                v.tensor_tensor(dtx[0:NS, g % 2, :].rearrange("p (h d) -> p h d", d=HD),
                                bank[5][0:NS, :].rearrange("p (h d) -> p h d", d=HD),
                                dt_tok[0:NS, 2, 2 * TPG * g:2 * TPG * (g + 1)].unsqueeze(2).to_broadcast([NS, 2 * TPG, HD]),
                                ALU.mult).then_inc(s_dcv, 1)

            dt_x(0)
            for t in range(XT_TILES):
                g = t // TPG
                st = st_in[:, t % STATES, :, :]
                v.wait_ge(s_stl[t % STATES], 16 * (t // STATES + 1))
                for q in range(2):
                    v.wait_ge(s_op, 2 * t + q + 1)
                    for i in range(4):
                        b = 4 * q + i
                        ins = v.scalar_tensor_tensor(out=st[:, b, :], in0=st[:, b, :], scalar=dAe[:, t, b:b + 1],
                                                     in1=bank[6 + q][:, i * N:(i + 1) * N], op0=ALU.mult, op1=ALU.add)
                    ins.then_inc(s_h, 1)
                v.wait_ge(s_h, 2 * t + 2)
                v.wait_ge(s_cbc, g + 1)
                link(v.tensor_tensor(st_y[:, :, :], st, Cb[:, :, :], ALU.mult))
                v.tensor_reduce(ysum[:, 0:NS], st_y[:, :, :], AX, ALU.add).then_inc(s_ys, 1)
                v.wait_ge(s_ys, t + 1)
                link(v.scalar_tensor_tensor(out=conv_out[:, t, TP:T], in0=conv_out[:, t, TP:T], scalar=d_col[:, t:t + 1],
                                            in1=ysum[:, 0:NS], op0=ALU.mult, op1=ALU.add))
                if t % TPG == 2 and g + 1 < SG:
                    dt_x(g + 1)
            v.wait_ge(s_zc, XT_TILES)
            for t in range(XT_TILES):
                v.tensor_tensor(conv_out[:, t, :], conv_out[:, t, :], zT[:, t, :], ALU.mult).then_inc(s_g, 1)
            v.wait_ge(s_gs, 1)
            link(v.tensor_copy(ss[:, 0:2], bank[2][:, 0:2]))
            link(v.tensor_copy(ss[0:NS, 2:3], bank[2][0:NS, 2:3]))
            v.tensor_scalar(ss[:, 0:3], ss[:, 0:3], 1.0 / DI, EPS, ALU.mult, ALU.add).then_inc(s_gs, 1)
            v.wait_ge(s_gq, XT_TILES + 1)
            link(v.reciprocal(rstd[:, 0:3], rstd[:, 0:3]))
            for t, r in enumerate(ROWS):
                for q in range(2):
                    v.wait_ge(s_ot, 2 * t + q + 1)
                    xs = X[0:r, t, 512 * q:512 * q + 512]
                    v.scalar_tensor_tensor(out=xs, in0=bank[3 + (2 * t + q) % 4][0:r, :], scalar=rstd[0:r, t:t + 1], in1=xs,
                                           op0=ALU.mult, op1=ALU.add).then_inc(s_xa, 1)
            norm(1, xn_e, gffn(0))
            moe(0)

            norm(2, xn_a, gmix(1))
            v.wait_ge(s_const, 9)
            v.tensor_copy(mask[:, 0, 0:1], mask[:, 0, 0:1]).then_inc(a_mv, 1)
            dist = pT[:, 0, 0, :, :].rearrange("p a b -> p (a b)")
            rest = pT[:, 0, 1, :, :].rearrange("p a b -> p (a b)")
            for g in range(1, NGRP):
                link(v.tensor_scalar(rest.bitcast(I32), dist.bitcast(I32), PATTERNS[g][1] - 1, None, ALU.bitwise_and))
                link(v.tensor_copy(sm[:, 0, 0, :], rest.bitcast(I32)))
                link(v.tensor_scalar(sm[:, 0, 0, :], sm[:, 0, 0, :], 0.0, NEG, ALU.not_equal, ALU.mult))
                v.tensor_tensor(mask[:, g, :], mask[:, g, :], sm[:, 0, 0, :], ALU.min).then_inc(a_mv, 1)
            v.wait_ge(a_mv, 3)
            link(v.tensor_tensor(fold[:, :], ident[:, 0:HD], ident[:, HD:P], ALU.add))

            def own_scores(g):
                v.wait_ge(q_e, 24 * (g + 1))
                v.tensor_tensor(prod[:, g, :].rearrange("p (t b) -> p t b", b=NS), qT[:, :, TP:T], kT[:, :, TP:T],
                                ALU.mult).then_inc(c_v, 1)

            def masked(g, t):
                n = DT * g + t
                hs = slice(2 * t, 2 * t + 2)
                s_ = sm[:, t % 2, :, :]
                if n >= 2:
                    v.wait_ge(h_t, 2 * n - 2)
                for h in range(2):
                    v.wait_ge(h_s, 2 * n + h + 1)
                    v.scalar_tensor_tensor(out=s_[:, h, :], in0=bank[2 + h][:, 0:3 * P], scalar=SCALE,
                                           in1=mask[:, g, :], op0=ALU.mult, op1=ALU.add).then_inc(h_m, 1)
                v.wait_ge(h_m, 2 * n + 2)
                dst = rs if g else M_
                link(v.tensor_reduce(dst[:, 0, hs], s_[:, :, 0:P], AX, ALU.max))
                link(v.tensor_reduce(dst[:, 1, hs], s_[:, :, P:3 * P], AX, ALU.max))
                if g:
                    link(v.tensor_tensor(rs[:, :, hs], rs[:, :, hs], M_[:, :, hs], ALU.max))
                    link(v.tensor_tensor(al[:, :, hs], M_[:, :, hs], rs[:, :, hs], ALU.subtract))
                    link(v.tensor_copy(M_[:, :, hs], rs[:, :, hs]))
                v.tensor_scalar(Mn[:, :, hs], M_[:, :, hs], -1.0, None, ALU.mult).then_inc(h_x, 1)

            def taken_up(g, t):
                n = DT * g + t
                hs = slice(2 * t, 2 * t + 2)
                v.wait_ge(h_e, 4 * n + 4)
                v.wait_ge(h_v, n + 1)
                o = O[:, :, 2 * t * HD:(2 * t + 2) * HD].rearrange("p i (h d) -> p i h d", d=HD)
                new = bank[6][:, 0:4 * HD].rearrange("p (i h d) -> p i h d", i=2, h=2)
                if g == 0:
                    link(v.tensor_copy(L_[:, :, hs], rs[:, :, hs]))
                    v.tensor_copy(o, new).then_inc(h_o, 1)
                    return
                link(v.tensor_tensor(L_[:, :, hs], L_[:, :, hs], al[:, :, hs], ALU.mult))
                link(v.tensor_tensor(L_[:, :, hs], L_[:, :, hs], rs[:, :, hs], ALU.add))
                link(v.tensor_tensor(o, o, al[:, :, hs].unsqueeze(3).to_broadcast([P, 2, 2, HD]), ALU.mult))
                v.tensor_tensor(o, o, new, ALU.add).then_inc(h_o, 1)

            def cache_scores(g, u):
                b, q = u // 2, u % 2
                n, k = 16 * g + u, NS * g + b
                r = KEYS[g]
                if q == 0:
                    v.wait_ge(k_l[k % 2], 16 * (k // 2 + 1))
                v.wait_ge(k_q, n + 1)
                kk = K_in[0:r, k % 2, 512 * q:512 * q + 512]
                v.tensor_tensor(kk, kk, bank[2 + q][0:r, :], ALU.mult).then_inc(k_m, 1)
                if q:
                    v.wait_ge(k_m, n + 1)
                    out = S_s[0:r, g, :].rearrange("p (h t b) -> p t h b", h=2, t=DT)[:, :, :, b]
                    v.tensor_reduce(out, K_in[0:r, k % 2, :].rearrange("p (t h d) -> p t h d", h=2, d=HD),
                                    AX, ALU.add).then_inc(k_r, 1)

            for g in range(NGRP):
                if g >= 1:
                    for u in range(16):
                        cache_scores(g - 1, u)
                for t in range(DT + 2):
                    if t < DT:
                        masked(g, t)
                    if t >= 2:
                        taken_up(g, t - 2)
                own_scores(g)
            for u in range(16):
                cache_scores(NGRP - 1, u)
            link(v.reciprocal(L_[:, :, :], L_[:, :, :]))
            for c in range(2):
                o = O[:, c, :].rearrange("p (h d) -> p h d", d=HD)
                v.tensor_tensor(o, o, bc(L_[:, c, :].unsqueeze(2), AH, HD), ALU.mult).then_inc(o_n, 1)
            v.wait_ge(c_p, 1)
            v.wait_ge(k_r, NS * NGRP)
            v.tensor_copy(same[:, :], bank[7][:, 0:P]).then_inc(c_v, 1)
            n_keys = sum(KEYS) + NGRP
            v.wait_ge(c_p, 2)
            link(v.tensor_reduce(s_st[:, 0:1], bank[7][:, 0:n_keys], AX, ALU.max))
            v.tensor_scalar(s_st[:, 1:2], s_st[:, 0:1], -SCALE, None, ALU.mult).then_inc(c_v, 1)
            v.wait_ge(c_a, 1)
            link(v.reciprocal(s_st[:, 3:4], s_st[:, 2:3]))
            v.tensor_scalar(p_s[:, 0:n_keys], p_s[:, 0:n_keys], s_st[:, 3:4], None, ALU.mult).then_inc(c_v, 1)
            v.wait_ge(c_v, NGRP + 3)
            for g in range(NGRP):
                v.tensor_scalar(PHp[:, g, :], same[:, :], p_s[:, sum(KEYS) + g:sum(KEYS) + g + 1], None,
                                ALU.mult).then_inc(c_v, 1)
            v.wait_ge(o_c, 4)
            v.memset(bank[4][:, :], 0.0)
            v.memset(bank[5][:, :], 0.0).then_inc(c_v, 1)
            v.wait_ge(c_p, 3)
            v.wait_ge(q_vs, DT * NGRP)
            link(v.tensor_tensor(y_s1[:, :, :], bank[2][:, 0:NGRP * DT * NS].rearrange("p (g c) -> p g c", g=NGRP),
                                 vTs[:, :, :], ALU.mult))
            link(v.tensor_tensor(y_s2, y_s1[:, 0, :], y_s1[:, 1, :], ALU.add))
            link(v.tensor_tensor(y_s2, y_s2, y_s1[:, 2, :], ALU.add))
            v.wait_ge(s_const, 10)
            for i in range(NS // 2):
                v.wait_ge(v_p, 2 * i + 2)
                if i >= 1:
                    v.wait_ge(c_p, 3 + i)
                v.tensor_tensor(y_own, bank[4 + i % 2][:, :], own_head, ALU.mult).then_inc(y_o, 1)
            v.wait_ge(c_p, 3 + NS // 2)
            for q in range(2):
                got = bank[3][:, 0:DT * NS].rearrange("p (i t c q) -> p t i c q", i=4, t=4, c=2)[:, :, :, :, q]
                v.tensor_tensor(yT[:, 4 * q:4 * q + 4, TP:T].rearrange("p t (i c) -> p t i c", c=2), got,
                                y_s2[:, 4 * q * NS:(4 * q + 4) * NS].rearrange("p (t i c) -> p t i c", i=4, c=2),
                                ALU.add).then_inc(c_v, 1)
            for t, r in enumerate(ROWS):
                for q in range(2):
                    v.wait_ge(s_ot, 12 + 2 * t + q + 1)
                    xs = X[0:r, t, 512 * q:512 * q + 512]
                    v.tensor_tensor(xs, xs, bank[3 + (2 * t + q) % 4][0:r, :], ALU.add).then_inc(s_xa, 1)
            norm(3, xn_e, gffn(1))
            moe(1)
            v.wait_ge(n_ss, 15)
            v.tensor_scalar(ss[:, 0:3], ss[:, 0:3], 1.0 / D, EPS, ALU.mult, ALU.add).then_inc(n_var, 1)
            v.wait_ge(n_std, 5)
            link(v.reciprocal(rstd[:, 0:3], rstd[:, 0:3]))
            v.wait_ge(s_vld, 160)
            for t, r in enumerate(ROWS):
                v.scalar_tensor_tensor(out=X[0:r, t, :], in0=X[0:r, t, :], scalar=rstd[0:r, t:t + 1],
                                       in1=gfin[0:r, :], op0=ALU.mult, op1=ALU.mult).then_inc(n_xn, 1)


INS = ["x_prompt", "x_sample", "state_conv", "state_ssm", "cache_kv_w128", "cache_kv_w512", "cache_kv_w2048",
       "norm_mix", "norm_ffn", "norm_final", "ssm_in_proj", "ssm_conv_w", "ssm_conv_b", "ssm_dt_bias", "ssm_a_log",
       "ssm_d", "ssm_norm", "ssm_out_proj", "attn_qkv", "attn_out", "moe_route_group", "moe_route_expert",
       "moe_w_gate_up", "moe_w_down"]
OUTS = [(1, TP, D), (NS, 1, D), (1, 1, PADW, CD), (1, NS, PADW, CD), (1, 1, SH, HD, N), (1, NS, SH, HD, N),
        (1, 1, 128, 2, AH, HD), (1, NS, 1, 2, AH, HD), (1, 1, TP, 2, AH, HD), (1, NS, 1, 2, AH, HD),
        (1, 1, TP, 2, AH, HD), (1, NS, 1, 2, AH, HD)]


def kernel(**inputs):
    import numpy as np
    import concourse.bacc as bacc
    from concourse.bass_utils import run_bass_kernel_spmd

    nc = bacc.Bacc("TRN2", target_bir_lowering=False, num_devices=1)
    arrays, handles = {}, {}
    for name in INS:
        v = np.ascontiguousarray(inputs[name])
        arrays[f"in_{name}"] = v
        handles[name] = nc.dram_tensor(f"in_{name}", v.shape, mybir.dt.from_np(v.dtype), kind="ExternalInput").ap()
    outs = [nc.dram_tensor(f"out_{i}", s, F32, kind="ExternalOutput").ap() for i, s in enumerate(OUTS)]
    bass_hybrid_step(nc, handles, outs)
    r = run_bass_kernel_spmd(nc, [arrays], core_ids=[0])
    return tuple(r.results[0][f"out_{i}"] for i in range(len(OUTS)))
```
